# Optimizing a Trainium2 kernel written in Bass

```python
import jax, jax.numpy as jnp
from jax import lax
import numpy as np

D_MODEL = 1024
BATCH = 1
SEQ = 256
DEPTH = 2

CHUNK = 64
N_META = 16
D_MIX = D_MODEL
HEAD_DIM = 64
N_Q_HEADS = 8
N_KV_HEADS = 2
Q_PER_KV = N_Q_HEADS // N_KV_HEADS
D_ATTN = N_Q_HEADS * HEAD_DIM
D_KV = N_KV_HEADS * HEAD_DIM
WINDOW = 128
WINDOW_CHUNKS = WINDOW // CHUNK
POOL_SIZES = (2, 4, 8, 16)
N_POOL_GROUPS = len(POOL_SIZES)
D_POOL = D_MIX - D_ATTN
POOL_GROUP = D_POOL // N_POOL_GROUPS
D_IN_PROJ = D_ATTN + 2 * D_KV + D_POOL
D_FF = D_MODEL * 7 // 2
N_EXPERTS = 8
TOP_K = 2
N_DENSE = (DEPTH + 1) // 2
N_MOE = DEPTH // 2
EPS = 1e-5
NEG_INF = -1e30

kernel_name = "hymba_swa_sink_pool_moe_trunk"

def rmsnorm(x, g):
    x32 = x.astype(jnp.float32)
    y = x32 * lax.rsqrt(jnp.mean(x32 * x32, axis=-1, keepdims=True) + EPS)
    return (y * g.astype(jnp.float32)).astype(x.dtype)

def sink_softmax(s, sink):
    sink_b = jnp.broadcast_to(sink, s.shape[:-1] + (1,))
    p = jax.nn.softmax(jnp.concatenate([s, sink_b], axis=-1), axis=-1)
    return p[..., :-1]

def chunk_window_attention(q, k, v, sinks):
    b, l, _ = q.shape
    n_chunks = (l - N_META) // CHUNK
    q = q.reshape(b, l, N_KV_HEADS, Q_PER_KV, HEAD_DIM) * (HEAD_DIM ** -0.5)
    k = k.reshape(b, l, N_KV_HEADS, HEAD_DIM)
    v = v.reshape(b, l, N_KV_HEADS, HEAD_DIM)
    sink = sinks.astype(jnp.float32).reshape(N_KV_HEADS, Q_PER_KV)

    qm, km, vm = q[:, :N_META], k[:, :N_META], v[:, :N_META]
    s_meta = jnp.einsum('bqhgd,bkhd->bhgqk', qm, km).astype(jnp.float32)
    p_meta = sink_softmax(s_meta, sink[None, :, :, None, None])
    o_meta = jnp.einsum('bhgqk,bkhd->bqhgd', p_meta.astype(v.dtype), vm)
    o_meta = o_meta.reshape(b, N_META, D_ATTN)

    def to_chunks(t):
        t = jnp.pad(t[:, N_META:], ((0, 0), (WINDOW_CHUNKS * CHUNK, 0), (0, 0), (0, 0)))
        return t.reshape(b, n_chunks + WINDOW_CHUNKS, CHUNK, N_KV_HEADS, HEAD_DIM)

    def banded(t, t_meta):
        tc = to_chunks(t)
        meta_b = jnp.broadcast_to(t_meta[:, None], (b, n_chunks, N_META, N_KV_HEADS, HEAD_DIM))
        bands = [tc[:, i:i + n_chunks] for i in range(WINDOW_CHUNKS + 1)]
        return jnp.concatenate([meta_b] + bands, axis=2)

    kb = banded(k, km)
    vb = banded(v, vm)
    chunk_idx = jnp.arange(n_chunks)[:, None]
    valid = jnp.concatenate(
        [jnp.ones((n_chunks, N_META), dtype=bool)]
        + [jnp.broadcast_to(chunk_idx >= WINDOW_CHUNKS - i, (n_chunks, CHUNK))
           for i in range(WINDOW_CHUNKS + 1)], axis=1)

    qf = q[:, N_META:].reshape(b, n_chunks, CHUNK, N_KV_HEADS, Q_PER_KV, HEAD_DIM)
    s = jnp.einsum('bnqhgd,bnkhd->bnhgqk', qf, kb).astype(jnp.float32)
    s = jnp.where(valid[None, :, None, None, None, :], s, NEG_INF)
    p = sink_softmax(s, sink[None, None, :, :, None, None])
    o = jnp.einsum('bnhgqk,bnkhd->bnqhgd', p.astype(v.dtype), vb)
    o = o.reshape(b, n_chunks * CHUNK, D_ATTN)
    return jnp.concatenate([o_meta, o], axis=1)

def multiscale_pool(u, w_pool, scale):
    b, l, _ = u.shape
    u32 = u.astype(jnp.float32)
    cs = jnp.cumsum(u32, axis=1)
    outs = []
    for gi, w in enumerate(POOL_SIZES):
        sl = slice(gi * POOL_GROUP, (gi + 1) * POOL_GROUP)
        c = cs[..., sl]
        c_lag = jnp.pad(c, ((0, 0), (w, 0), (0, 0)))[:, :l]
        count = jnp.minimum(jnp.arange(1, l + 1), w).astype(jnp.float32)[None, :, None]
        outs.append((c - c_lag) / count - u32[..., sl])
    d = jnp.stack(outs, axis=2).astype(u.dtype)
    y = jnp.einsum('blgc,gcd->blgd', d, w_pool).reshape(b, l, D_POOL)
    return y * scale

def swiglu(x, w_gate, w_up, w_down):
    return (jax.nn.silu(x @ w_gate) * (x @ w_up)) @ w_down

def moe_swiglu(x, w_router, w_gate, w_up, w_down):
    logits = (x @ w_router).astype(jnp.float32)
    top_vals, top_idx = lax.top_k(logits, TOP_K)
    gates = jax.nn.softmax(top_vals, axis=-1)
    gate_full = jnp.sum(jax.nn.one_hot(top_idx, N_EXPERTS, dtype=jnp.float32) * gates[..., None], axis=1)
    gate_full = gate_full.astype(x.dtype)
    y = jnp.zeros_like(x)
    for e in range(N_EXPERTS):
        y = y + gate_full[:, e:e + 1] * swiglu(x, w_gate[e], w_up[e], w_down[e])
    return y

def setup_inputs(seed: int = 0) -> dict:
    key = jax.random.key(seed)
    ks = jax.random.split(key, 20)
    f32 = jnp.float32

    def nrm(k, shape, scale):
        return jax.random.normal(k, shape, f32) * scale

    return {
        "x": nrm(ks[0], (BATCH, SEQ, D_MODEL), 1.0),
        "meta_tokens": nrm(ks[1], (N_META, D_MODEL), 1.0),
        "norm_mix_g": 1.0 + nrm(ks[2], (DEPTH, D_MODEL), 0.02),
        "w_in": nrm(ks[3], (DEPTH, D_MODEL, D_IN_PROJ), D_MODEL ** -0.5),
        "attn_sinks": nrm(ks[4], (DEPTH, N_Q_HEADS), 0.5),
        "pool_w": nrm(ks[5], (DEPTH, N_POOL_GROUPS, POOL_GROUP, POOL_GROUP), POOL_GROUP ** -0.5),
        "pool_scale": 1.0 + nrm(ks[6], (DEPTH, D_POOL), 0.02),
        "w_out": nrm(ks[7], (DEPTH, D_MIX, D_MODEL), D_MIX ** -0.5),
        "norm_ffn_g": 1.0 + nrm(ks[8], (DEPTH, D_MODEL), 0.02),
        "dense_w_gate": nrm(ks[9], (N_DENSE, D_MODEL, D_FF), D_MODEL ** -0.5),
        "dense_w_up": nrm(ks[10], (N_DENSE, D_MODEL, D_FF), D_MODEL ** -0.5),
        "dense_w_down": nrm(ks[11], (N_DENSE, D_FF, D_MODEL), D_FF ** -0.5),
        "moe_w_router": nrm(ks[12], (N_MOE, D_MODEL, N_EXPERTS), D_MODEL ** -0.5),
        "moe_w_gate": nrm(ks[13], (N_MOE, N_EXPERTS, D_MODEL, D_FF), D_MODEL ** -0.5),
        "moe_w_up": nrm(ks[14], (N_MOE, N_EXPERTS, D_MODEL, D_FF), D_MODEL ** -0.5),
        "moe_w_down": nrm(ks[15], (N_MOE, N_EXPERTS, D_FF, D_MODEL), D_FF ** -0.5),
        "final_norm_g": 1.0 + nrm(ks[16], (D_MODEL,), 0.02),
    }

def reference(x, meta_tokens, norm_mix_g, w_in, attn_sinks, pool_w, pool_scale, w_out,
              norm_ffn_g, dense_w_gate, dense_w_up, dense_w_down, moe_w_router,
              moe_w_gate, moe_w_up, moe_w_down, final_norm_g):
    b = x.shape[0]
    meta = jnp.broadcast_to(meta_tokens[None].astype(x.dtype), (b, N_META, D_MODEL))
    h = jnp.concatenate([meta, x], axis=1)
    for layer in range(DEPTH):
        xn = rmsnorm(h, norm_mix_g[layer])
        proj = xn @ w_in[layer]
        q = proj[..., :D_ATTN]
        k = proj[..., D_ATTN:D_ATTN + D_KV]
        v = proj[..., D_ATTN + D_KV:D_ATTN + 2 * D_KV]
        u = proj[..., D_ATTN + 2 * D_KV:]
        a = chunk_window_attention(q, k, v, attn_sinks[layer])
        p = multiscale_pool(u, pool_w[layer], pool_scale[layer])
        h = h + jnp.concatenate([a, p], axis=-1) @ w_out[layer]
        xn = rmsnorm(h, norm_ffn_g[layer])
        if layer % 2 == 0:
            i = layer // 2
            f = swiglu(xn, dense_w_gate[i], dense_w_up[i], dense_w_down[i])
        else:
            i = layer // 2
            f = moe_swiglu(xn.reshape(-1, D_MODEL), moe_w_router[i], moe_w_gate[i],
                           moe_w_up[i], moe_w_down[i]).reshape(h.shape)
        h = h + f
    return rmsnorm(h[:, N_META:], final_norm_g)


_drawn_inputs = setup_inputs


def setup_inputs(seed=0):
    import zlib

    import numpy as np

    out = dict(_drawn_inputs(seed))
    spreads = {}
    factors = {'attn_sinks': 4.841, 'final_norm_g': 2.86}
    for name, (base, spread) in spreads.items():
        noise = np.random.default_rng([zlib.crc32(name.encode()), seed]).standard_normal(out[name].shape)
        drawn = base * np.exp(spread * noise) if base else spread * noise
        out[name] = __import__('jax').numpy.asarray(drawn.astype(out[name].dtype))
    for name, factor in factors.items():
        out[name] = (out[name] * factor).astype(out[name].dtype)
    return out
```

```python
from contextlib import ExitStack

import concourse.bass as bass
from concourse import mybir

F32 = mybir.dt.float32
F32R = mybir.dt.float32r
I32 = mybir.dt.int32
ALU = mybir.AluOpType
ACT = mybir.ActivationFunctionType
AXX = mybir.AxisListType.X

P = 128
D = 1024
KT = D // P
META, SEQ, CHUNK = 16, 256, 64
L = META + SEQ
NT = SEQ // P
HEADS, HD = 8, 64
POOL_GROUPS = 4
FF = 3584
STEPS = FF // 512
EXPERTS = 8
EPS = 1e-5
NEG = -1e30

GW = 2048
RAW = 6
SPLIT = 3
MIX_G = 9
FFN_G = 6 * STEPS
FFN0 = MIX_G
MIX1 = MIX_G + FFN_G
MOE = MIX1 + MIX_G
LOADS = 6
CONSTS = 20
WINDOW_STEPS = 12
GAP, CHOSEN, ROUTED = 9, 14, 27
AHEAD = 2


def build(nc, x_t, gains, sinks, pool_w, pool_scale, final_g, w_router, w_mix, w_ffn, w_moe, out):
    with ExitStack() as ctx:
        def sb(name, shape, dt=F32):
            return ctx.enter_context(nc.sbuf_tensor(name, shape, dt))

        def sem(name):
            return ctx.enter_context(nc.semaphore(name))

        bank = ctx.enter_context(nc.psum_tensor("bank", [P, 8, 512], F32))

        raw = sb("raw", [P, RAW, GW])
        w_hi = sb("w_hi", [P, SPLIT, GW], F32R)
        w_lo = sb("w_lo", [P, SPLIT, GW], F32R)
        h_t = sb("h_t", [P, KT, L])
        gain = sb("gain", [P, 4, KT])
        sink = sb("sink", [P, 2 * HEADS])
        pw = sb("pw", [P, 2 * POOL_GROUPS, P])
        pscale = sb("pscale", [P, 2 * POOL_GROUPS])
        router = sb("router", [P, KT, EXPERTS])
        g_final = sb("g_final", [P, D])
        eps = sb("eps", [P, 1])
        ones = sb("ones", [P, P])
        ident = sb("ident", [P, P])
        before = sb("before", [P, P])
        slot_no = sb("slot_no", [P, P])
        expert_no = sb("expert_no", [P, NT, EXPERTS])
        mask = sb("mask", [P, NT, L])
        head_count = sb("head_count", [P, POOL_GROUPS, META])
        inv_count = sb("inv_count", [P, POOL_GROUPS, META])
        sums = sb("sums", [P, 2])
        rms = sb("rms", [P, 2])
        rstd2 = sb("rstd2", [P, 2])
        rstd = sb("rstd", [P, L])
        rms_t = sb("rms_t", [P, L])

        with ExitStack() as r1:
            xn, xn_hi, xn_lo = (r1.enter_context(nc.sbuf_tensor(n, [P, KT, L], t))
                                for n, t in (("xn", F32), ("xn_hi", F32R), ("xn_lo", F32R)))
        with ExitStack() as r1:
            h_tok, n_hi, n_lo = (r1.enter_context(nc.sbuf_tensor(n, [P, NT, D], t))
                                 for n, t in (("h_tok", F32), ("n_hi", F32R), ("n_lo", F32R)))
        sb("region1", [P, 3 * KT * L])

        with ExitStack() as r2:
            def r(name, shape, dt=F32):
                return r2.enter_context(nc.sbuf_tensor(name, shape, dt))
            mix_hi = r("mix_hi", [P, KT, L], F32R)
            mix_lo = r("mix_lo", [P, KT, L], F32R)
            u_pad = r("u_pad", [P, POOL_GROUPS, META + L])
            win_a = r("win_a", [P, POOL_GROUPS, META + L])
            win_b = r("win_b", [P, POOL_GROUPS, META + L])
            pooled = r("pooled", [P, POOL_GROUPS, L])
            q_t = r("q_t", [P, HEADS // 2, L])
            k_t = r("k_t", [P, L])
            v_tok = r("v_tok", [P, NT + 1, P])
            prob = r("prob", [P, 3, L])
            prob_t = r("prob_t", [P, 2, NT + 1, P])
            row_max = r("row_max", [P, 24])
            neg_max = r("neg_max", [P, 24])
            exp_sum = r("exp_sum", [P, 24])
            exp_sink = r("exp_sink", [P, 24])
            den = r("den", [P, 24])
            inv_den = r("inv_den", [P, 24])
        with ExitStack() as r2:
            ff_hi = r2.enter_context(nc.sbuf_tensor("ff_hi", [P, 4, 2, L], F32R))
            ff_lo = r2.enter_context(nc.sbuf_tensor("ff_lo", [P, 4, 2, L], F32R))
            ff_silu = r2.enter_context(nc.sbuf_tensor("ff_silu", [P, 2, L], F32))
            ff_h = r2.enter_context(nc.sbuf_tensor("ff_h", [P, 2, L], F32))
        with ExitStack() as r2:
            def r(name, shape, dt=F32):
                return r2.enter_context(nc.sbuf_tensor(name, shape, dt))
            n_tok = r("n_tok", [P, NT, D])
            xr = r("xr", [P, KT, SEQ])
            xg = r("xg", [P, KT, P])
            xg_hi = r("xg_hi", [P, KT, P], F32R)
            xg_lo = r("xg_lo", [P, KT, P], F32R)
            pick = r("pick", [P, NT, P], F32R)
            pick_t = r("pick_t", [P, NT * P], F32R)
            gate_col = r("gate_col", [P, NT])
            slot_gate = r("slot_gate", [P, 1])
            e_silu = r("e_silu", [P, 512])
            e_h = r("e_h", [P, 512])
            ht_hi = r("ht_hi", [P, 4, P], F32R)
            ht_lo = r("ht_lo", [P, 4, P], F32R)
            y = r("y", [P, 2, 512])
            y_hi = r("y_hi", [P, 2, 512], F32R)
            y_lo = r("y_lo", [P, 2, 512], F32R)
            lg, eq, cand, oh1, oh2, l2, ga, gb, chosen, posa = (
                r(n, [P, NT, EXPERTS]) for n in
                ("lg", "eq", "cand", "oh1", "oh2", "l2", "ga", "gb", "chosen", "posa"))
            m1, m2, least, gap, e2, den2, g1, g2 = (
                r(n, [P, NT]) for n in ("m1", "m2", "least", "gap", "e2", "den2", "g1", "g2"))
            gates = r("gates", [P, 2 * EXPERTS + 1, NT])
            place = r("place", [P, 2 * EXPERTS + 1, NT])
            most = r("most", [P, 1])
            rounds_f = r("rounds_f", [P, 1])
            rounds = r("rounds", [P, 1], I32)

        x_loaded = sem("x_loaded")
        consts_loaded = sem("consts_loaded")
        loaded = [sem(f"loaded{s}") for s in range(RAW)]
        consts_built = sem("consts_built")
        hi_ready = sem("hi_ready")
        lo_ready = sem("lo_ready")
        weights_done = sem("weights_done")
        squares_ready = sem("squares_ready")
        square_sum_ready = sem("square_sum_ready")
        rms_ready = sem("rms_ready")
        rstd_ready = sem("rstd_ready")
        xn_ready = sem("xn_ready")
        xn_hi_ready = sem("xn_hi_ready")
        xn_lo_ready = sem("xn_lo_ready")
        proj_evicted = sem("proj_evicted")
        window_step = sem("window_step")
        inv_count_ready = sem("inv_count_ready")
        zeros_ready = sem("zeros_ready")
        pooled_ready = sem("pooled_ready")
        scores_ready = sem("scores_ready")
        masked_ready = sem("masked_ready")
        neg_max_ready = sem("neg_max_ready")
        exp_ready = sem("exp_ready")
        exp_sink_ready = sem("exp_sink_ready")
        den_ready = sem("den_ready")
        inv_den_ready = sem("inv_den_ready")
        prob_ready = sem("prob_ready")
        prob_t_psum = sem("prob_t_psum")
        prob_t_main = sem("prob_t_main")
        prob_t_meta = sem("prob_t_meta")
        head_out_ready = sem("head_out_ready")
        pool_out_ready = sem("pool_out_ready")
        mix_hi_ready = sem("mix_hi_ready")
        mix_lo_ready = sem("mix_lo_ready")
        out_added = sem("out_added")
        silu_ready = sem("silu_ready")
        ff_h_ready = sem("ff_h_ready")
        ff_hi_ready = sem("ff_hi_ready")
        ff_lo_ready = sem("ff_lo_ready")
        down_part = sem("down_part")
        down_added = sem("down_added")
        out_tok_psum = sem("out_tok_psum")
        h_tok_ready = sem("h_tok_ready")
        tok_sum_ready = sem("tok_sum_ready")
        tok_rms_ready = sem("tok_rms_ready")
        tok_rstd_ready = sem("tok_rstd_ready")
        n_tok_ready = sem("n_tok_ready")
        n_hi_ready = sem("n_hi_ready")
        n_lo_ready = sem("n_lo_ready")
        xr_psum = sem("xr_psum")
        xr_ready = sem("xr_ready")
        logits_psum = sem("logits_psum")
        route_step = sem("route_step")
        gap_exp_ready = sem("gap_exp_ready")
        places_psum = sem("places_psum")
        pick_ready = sem("pick_ready")
        gate_col_ready = sem("gate_col_ready")
        slots_psum = sem("slots_psum")
        slots_ready = sem("slots_ready")
        gathered_psum = sem("gathered_psum")
        xg_ready = sem("xg_ready")
        xg_hi_ready = sem("xg_hi_ready")
        xg_lo_ready = sem("xg_lo_ready")
        e_silu_ready = sem("e_silu_ready")
        e_h_ready = sem("e_h_ready")
        ht_psum = sem("ht_psum")
        ht_hi_ready = sem("ht_hi_ready")
        ht_lo_ready = sem("ht_lo_ready")
        y_ready = sem("y_ready")
        y_hi_ready = sem("y_hi_ready")
        y_lo_ready = sem("y_lo_ready")
        scattered_psum = sem("scattered_psum")
        scatter_added = sem("scatter_added")
        out_ready = sem("out_ready")
        stored = sem("stored")

        NORM_GAIN = (0, 2, 1)

        def tile_cols(t):
            return slice(META + t * P, META + (t + 1) * P) if t < NT else slice(0, META)

        def key_blocks(t):
            blocks = [(NT, 0, META)]
            if t < NT:
                blocks += [(kt, META + kt * P, META + (kt + 1) * P) for kt in range(t + 1)]
            return blocks

        def units(l):
            return [(t, j, b) for t in range(NT + 1 - l) for j in range(HEADS // 2) for b in range(2)]

        UNIT0 = (0, len(units(0)))
        PAIR0 = (0, len(units(0)) // 2)
        MIXED0 = (0, len(units(0)) // 2 + POOL_GROUPS)

        def ffn_gate(n, s):
            return FFN0 + 2 * s + (0 if n == 0 else 4 + 6 * (n - 1))

        def e_gate(n):
            return 0 if n == 0 else 4 + 6 * (n - 1)

        def e_down(n):
            return 8 + 6 * n if n < STEPS - 1 else FFN_G - 2

        block = ctx.enter_context(nc.Block())

        @block.sync
        def _(sp):
            def load(g, src, i=None):
                if g >= RAW or i is not None:
                    sp.wait_ge(lo_ready, g - RAW + 1 + (0 if i is None else FFN_G * i))
                sp.dma_start(raw[:, g % RAW, :], src).then_inc(loaded[g % RAW], 16)

            sp.dma_start(h_t[:], x_t).then_inc(x_loaded, 16)
            sp.dma_start(gain[:], gains).then_inc(consts_loaded, 16)
            load(0, w_mix[0, 0])
            load(1, w_mix[0, 1])
            sp.dma_start(sink[:], sinks.partition_broadcast(P)).then_inc(consts_loaded, 16)
            load(2, w_mix[0, 2])
            sp.dma_start(pw[:], pool_w).then_inc(consts_loaded, 16)
            sp.dma_start(pscale[:], pool_scale).then_inc(consts_loaded, 16)
            sp.dma_start(router[:], w_router).then_inc(consts_loaded, 16)
            sp.dma_start(g_final[:], final_g.partition_broadcast(P)).then_inc(consts_loaded, 16)
            for g in range(3, MIX_G):
                load(g, w_mix[0, g])
            for g in range(FFN_G):
                load(FFN0 + g, w_ffn[g])
            for g in range(MIX_G):
                load(MIX1 + g, w_mix[1, g])
            for g in range(RAW):
                load(MOE + g, w_moe[0, g])
            sp.wait_ge(route_step, ROUTED)
            end = sp.value_load(rounds[0:1, 0:1], min_val=EXPERTS, max_val=2 * EXPERTS)
            with sp.Fori(0, end) as i:
                this = sp.snap(i % EXPERTS)
                for g in range(RAW, FFN_G):
                    load(MOE + g, w_moe[this, g], i)
                following = sp.snap((i + 1) % EXPERTS)
                with sp.If(i < end - 1):
                    for g in range(RAW):
                        load(MOE + FFN_G + g, w_moe[following, g], i)
                with sp.Else():
                    sp.nop()
                sp.nop()
            for t in range(NT):
                sp.wait_ge(out_ready, t + 1)
                sp.dma_start(out[t * P:(t + 1) * P, :], n_tok[:, t, :]).then_inc(stored, 16)
            sp.wait_ge(stored, 16 * NT)

        @block.gpsimd
        def _(pool):
            pool.memset(eps[:], EPS).then_inc(consts_built, 1)
            pool.memset(ones[:], 1.0).then_inc(consts_built, 1)
            pool.memset(ident[:], 0.0).then_inc(consts_built, 1)
            pool.memset(before[:], 1.0).then_inc(consts_built, 1)
            pool.memset(mask[:], 0.0).then_inc(consts_built, 1)
            pool.memset(u_pad[:, :, 0:META], 0.0).then_inc(consts_built, 1)
            pool.memset(win_a[:, :, 0:META], 0.0).then_inc(consts_built, 1)
            pool.memset(win_b[:, :, 0:META], 0.0).then_inc(consts_built, 1)
            pool.iota(slot_no[:], [[1, P]], base=0, channel_multiplier=0,
                      allow_small_or_imprecise_dtypes=True).then_inc(consts_built, 1)
            pool.iota(expert_no[:], [[0, NT], [1, EXPERTS]], base=0, channel_multiplier=0,
                      allow_small_or_imprecise_dtypes=True).then_inc(consts_built, 1)
            pool.iota(head_count[:], [[0, POOL_GROUPS], [1, META]], base=1, channel_multiplier=0,
                      allow_small_or_imprecise_dtypes=True).then_inc(consts_built, 1)
            pool.wait_ge(consts_built, 11)
            pool.affine_select(ident[:], ident[:], [[-1, P]], ALU.not_equal, 1.0, base=0,
                               channel_multiplier=1).then_inc(consts_built, 1)
            pool.affine_select(before[:], before[:], [[1, P]], ALU.is_gt, 0.0, base=0,
                               channel_multiplier=-1).then_inc(consts_built, 1)
            pool.wait_ge(consts_built, 13)
            pool.memset(mask[0:64, 0, META + CHUNK:META + 2 * CHUNK], NEG).then_inc(consts_built, 1)
            pool.wait_ge(consts_built, 14)
            pool.memset(mask[0:64, 1, META + 3 * CHUNK:L], NEG).then_inc(consts_built, 1)
            pool.wait_ge(consts_built, 15)
            pool.memset(mask[64:128, 1, META:META + CHUNK], NEG).then_inc(consts_built, 1)
            pool.wait_ge(consts_built, 16)
            for g in range(POOL_GROUPS):
                pool.tensor_scalar(head_count[:, g, :], head_count[:, g, :], float(2 << g), None,
                                   ALU.min).then_inc(consts_built, 1)

            def windows(l):
                pool.wait_ge(proj_evicted, 12 * l + 4)
                done = WINDOW_STEPS * l
                src = u_pad
                for s, dst in enumerate((win_a, win_b, win_a, win_b)):
                    lag = 1 << s
                    if s:
                        pool.wait_ge(window_step, done + s)
                    pool.tensor_tensor(dst[:, s:, META:], src[:, s:, META:],
                                       src[:, s:, META - lag:META + L - lag],
                                       ALU.add).then_inc(window_step, 1)
                    src = dst
                pool.wait_ge(window_step, done + 4)
                for g, win in enumerate((win_a, win_b, win_a, win_b)):
                    pool.tensor_scalar(pooled[:, g, META:], win[:, g, 2 * META:], 1.0 / (2 << g),
                                       None, ALU.mult).then_inc(window_step, 1)
                    pool.tensor_tensor(pooled[:, g, 0:META], win[:, g, META:2 * META],
                                       inv_count[:, g, :], ALU.mult).then_inc(window_step, 1)
                pool.wait_ge(window_step, done + 12)
                pool.tensor_tensor(pooled[:], pooled[:], u_pad[:, :, META:],
                                   ALU.subtract).then_inc(pooled_ready, 1)

            pool.wait_ge(inv_count_ready, 1)
            windows(0)
            pool.wait_ge(down_added, KT * STEPS)
            pool.memset(u_pad[:, :, 0:META], 0.0).then_inc(zeros_ready, 1)
            pool.memset(win_a[:, :, 0:META], 0.0).then_inc(zeros_ready, 1)
            pool.memset(win_b[:, :, 0:META], 0.0).then_inc(zeros_ready, 1)
            pool.wait_ge(zeros_ready, 3)
            windows(1)

        @block.tensor
        def _(pe):
            def split_product(o, a_hi, a_lo, b_hi, b_lo, start, stop):
                pe.matmul(o, a_hi, b_hi, start=start, stop=False)
                pe.matmul(o, a_hi, b_lo, start=False, stop=False)
                return pe.matmul(o, a_lo, b_hi, start=False, stop=stop)

            def weights(g, shape, i=None, **sizes):
                pe.wait_ge(lo_ready, g + 1 + (0 if i is None else FFN_G * i))
                return (w_hi[:, g % SPLIT, :].rearrange(shape, **sizes),
                        w_lo[:, g % SPLIT, :].rearrange(shape, **sizes))

            def square_sum(v):
                pe.wait_ge(squares_ready, v + 1)
                for k in range(KT):
                    m = pe.matmul(bank[:, 7, 0:L], ones[:], xn[:, k, :], start=k == 0, stop=k == KT - 1)
                m.then_inc(square_sum_ready, 1)

            def project(l):
                g0 = MIX1 * l
                pe.wait_ge(xn_lo_ready, 2 * (2 * l) + 2)

                def two_tiles(g, b0):
                    whi, wlo = weights(g, "p (c k m) -> p c k m", c=2, k=KT)
                    for c in range(2):
                        for k in range(KT):
                            m = split_product(bank[:, b0 + c, 0:L], whi[:, c, k], wlo[:, c, k],
                                              xn_hi[:, k, :], xn_lo[:, k, :], k == 0, k == KT - 1)
                    m.then_inc(weights_done, 1)

                two_tiles(g0, 0)
                two_tiles(g0 + 1, 2)
                whi, wlo = weights(g0 + 2, "p (k m) -> p k m", k=KT)
                for k in range(KT):
                    split_product(bank[:, 4, 0:L], whi[:, k, 0:P], wlo[:, k, 0:P],
                                  xn_hi[:, k, :], xn_lo[:, k, :], k == 0, k == KT - 1)
                for t in range(NT + 1):
                    cols = tile_cols(t) if t < NT else slice(0, P)
                    for k in range(KT):
                        m = split_product(bank[:, 5 + t, 0:P], xn_hi[:, k, cols], xn_lo[:, k, cols],
                                          whi[:, k, P:2 * P], wlo[:, k, P:2 * P], k == 0, k == KT - 1)
                m.then_inc(weights_done, 1)
                pe.wait_ge(proj_evicted, 12 * l + 2)
                two_tiles(g0 + 3, 0)
                pe.wait_ge(proj_evicted, 12 * l + 4)
                two_tiles(g0 + 4, 2)

            def attention(l):
                us, u0, p0 = units(l), UNIT0[l], PAIR0[l]
                main0, m0 = 2 * NT * HEADS // 2 * l, MIXED0[l]
                pe.wait_ge(proj_evicted, 12 * l + 12)
                for step in range(len(us) + 3):
                    if step < len(us):
                        t, j, b = us[step]
                        rows = slice(HD * b, HD * b + HD)
                        n = key_blocks(t)[-1][2]
                        m = P if t < NT else META
                        if step >= 3:
                            pe.wait_ge(masked_ready, u0 + step - 2)
                        pe.matmul(bank[0:m, step % 3, 0:n], q_t[rows, j, tile_cols(t)], k_t[rows, 0:n],
                                  start=True, stop=True).then_inc(scores_ready, 1)
                    u = step - 2
                    if 0 <= u < len(us):
                        t, j, b = us[u]
                        m = P if t < NT else META
                        pe.wait_ge(prob_ready, u0 + u + 1)
                        if u >= 2:
                            pe.wait_ge(prob_t_meta, u0 + u - 1)
                            pe.wait_ge(prob_t_main, main0 + min(u - 1, NT * HEADS))
                        for kt, c0, c1 in key_blocks(t):
                            o = bank[0:c1 - c0, 3 + u % 2, kt * P:kt * P + m]
                            if kt < NT:
                                mm = pe.transpose(o, prob[0:m, u % 3, c0:c1], ident[0:m, 0:m])
                            else:
                                mm = pe.matmul(o, prob[0:m, u % 3, c0:c1], ident[0:m, 0:m],
                                               start=True, stop=True)
                        mm.then_inc(prob_t_psum, 1)
                    u = step - 3
                    if u >= 0:
                        t, j, b = us[u]
                        rows = slice(HD * b, HD * b + HD)
                        m = P if t < NT else META
                        pe.wait_ge(prob_t_meta, u0 + u + 1)
                        pe.wait_ge(prob_t_main, main0 + min(u + 1, NT * HEADS))
                        pair = u // 2
                        if b == 0 and pair >= 2:
                            pe.wait_ge(mix_lo_ready, m0 + pair - 1)
                        blocks = key_blocks(t)
                        for n, (kt, c0, c1) in enumerate(blocks):
                            mm = pe.matmul(bank[rows, 5 + pair % 2, 0:m], v_tok[0:c1 - c0, kt, rows],
                                           prob_t[0:c1 - c0, u % 2, kt, 0:m], start=n == 0,
                                           stop=n == len(blocks) - 1)
                        mm.then_inc(head_out_ready, 1)

            def pool_maps(l):
                pe.wait_ge(pooled_ready, l + 1)
                for g in range(POOL_GROUPS):
                    pe.matmul(bank[:, g, 0:L], pw[:, POOL_GROUPS * l + g, :], pooled[:, g, :],
                              start=True, stop=True).then_inc(pool_out_ready, 1)

            pe.wait_ge(consts_built, CONSTS)
            square_sum(0)
            project(0)
            attention(0)
            pe.wait_ge(consts_loaded, 16 * LOADS)
            pool_maps(0)
            pe.wait_ge(mix_lo_ready, MIXED0[1])
            for gg in range(4):
                whi, wlo = weights(5 + gg, "p (c k m) -> p c k m", c=2, k=KT)
                for c in range(2):
                    for k in range(KT):
                        m = split_product(bank[:, 2 * gg + c, 0:L], whi[:, c, k], wlo[:, c, k],
                                          mix_hi[:, k, :], mix_lo[:, k, :], k == 0, k == KT - 1)
                m.then_inc(weights_done, 1)

            square_sum(1)
            pe.wait_ge(xn_lo_ready, 4)

            def hidden(g, b0):
                whi, wlo = weights(g, "p (c k m) -> p c k m", c=2, k=KT)
                for c in range(2):
                    for k in range(KT):
                        m = split_product(bank[:, b0 + c, 0:L], whi[:, c, k], wlo[:, c, k],
                                          xn_hi[:, k, :], xn_lo[:, k, :], k == 0, k == KT - 1)
                m.then_inc(weights_done, 1)

            def down(n, a, g):
                whi, wlo = weights(g, "p (d f m) -> p d f m", d=4, f=4)
                pe.wait_ge(ff_lo_ready, 2 * n + 2)
                q = 2 * n + a
                for d in range(4):
                    if q:
                        pe.wait_ge(down_added, 4 * (q - 1) + d + 1)
                    for f in range(4):
                        slot, c = (2 * n + f // 2) % 4, f % 2
                        m = split_product(bank[:, 4 + d, 0:L], whi[:, d, f], wlo[:, d, f],
                                          ff_hi[:, slot, c, :], ff_lo[:, slot, c, :], f == 0, f == 3)
                    m.then_inc(down_part if d < 3 else weights_done, 1)

            for n in range(STEPS):
                for s in range(2):
                    pair = 2 * n + s
                    if pair:
                        pe.wait_ge(silu_ready, pair)
                    hidden(ffn_gate(n, s), 0)
                    if pair:
                        pe.wait_ge(ff_h_ready, pair)
                    hidden(ffn_gate(n, s) + 1, 2)
                if n:
                    down(n - 1, 0, ffn_gate(n, 0) + 4)
                    down(n - 1, 1, ffn_gate(n, 0) + 5)
            down(STEPS - 1, 0, MIX1 - 2)
            down(STEPS - 1, 1, MIX1 - 1)

            square_sum(2)
            project(1)
            attention(1)
            pool_maps(1)
            pe.wait_ge(mix_lo_ready, MIXED0[1] + len(units(1)) // 2 + POOL_GROUPS)
            for n in range(2):
                for kh in range(2):
                    whi, wlo = weights(MIX1 + 5 + 2 * n + kh, "p (k m) -> p k m", k=4)
                    for t in range(NT):
                        for k in range(4):
                            kk = 4 * kh + k
                            m = split_product(bank[:, 2 * n + t, :], mix_hi[:, kk, tile_cols(t)],
                                              mix_lo[:, kk, tile_cols(t)], whi[:, k], wlo[:, k],
                                              kh == 0 and k == 0, False)
                    m.then_inc(weights_done, 1)
                for t in range(NT):
                    for k in range(4):
                        m = pe.matmul(bank[:, 2 * n + t, k * P:(k + 1) * P],
                                      h_t[:, 4 * n + k, tile_cols(t)], ident[:],
                                      start=False, stop=k == 3)
                    m.then_inc(out_tok_psum, 1)

            pe.wait_ge(n_tok_ready, NT)
            for kp in range(4):
                for k in range(2):
                    for t in range(NT):
                        m = pe.transpose(bank[:, 4 + kp, (NT * k + t) * P:(NT * k + t + 1) * P],
                                         n_tok[:, t, (2 * kp + k) * P:(2 * kp + k + 1) * P], ident[:])
                m.then_inc(xr_psum, 1)
            pe.wait_ge(xr_ready, KT)
            for t in range(NT):
                for k in range(KT):
                    m = pe.matmul(bank[:, 0, t * EXPERTS:(t + 1) * EXPERTS], xr[:, k, t * P:(t + 1) * P],
                                  router[:, k, :], start=k == 0, stop=k == KT - 1)
            m.then_inc(logits_psum, 1)
            pe.wait_ge(route_step, CHOSEN)
            pe.matmul(bank[:, 1, 0:8], before[:], chosen[:, 0, :], start=True, stop=True)
            pe.matmul(bank[:, 1, 8:16], before[:], chosen[:, 1, :], start=True, stop=False)
            pe.matmul(bank[:, 1, 8:16], ones[:], chosen[:, 0, :], start=False, stop=True)
            pe.matmul(bank[:, 1, 16:24], ones[:], chosen[:, 0, :], start=True, stop=False)
            pe.matmul(bank[:, 1, 16:24], ones[:], chosen[:, 1, :], start=False,
                      stop=True).then_inc(places_psum, 1)
            pe.wait_ge(route_step, ROUTED)
            end = pe.value_load(rounds[0:1, 0:1], min_val=EXPERTS, max_val=2 * EXPERTS)

            def gather(r):
                pe.wait_ge(pick_ready, NT * r + NT)
                for b in range(2):
                    for k in range(4):
                        cols = slice((4 * b + k) * P, (4 * b + k + 1) * P)
                        for t in range(NT):
                            pe.matmul(bank[:, 5 + b, k * P:(k + 1) * P], n_hi[:, t, cols], pick[:, t, :],
                                      start=t == 0, stop=False)
                            m = pe.matmul(bank[:, 5 + b, k * P:(k + 1) * P], n_lo[:, t, cols],
                                          pick[:, t, :], start=False, stop=t == NT - 1)
                    m.then_inc(gathered_psum, 1)

            pe.wait_ge(n_lo_ready, NT)
            gather(0)
            pe.nop().then_inc(ht_psum, 1)
            with pe.Fori(0, end) as i:
                def hidden_half(g, b):
                    whi, wlo = weights(MOE + g, "p (k m) -> p k m", i, k=4)
                    half = g % 2
                    for k in range(4):
                        kk = 4 * half + k
                        m = split_product(bank[:, b, :], xg_hi[:, kk, :], xg_lo[:, kk, :],
                                          whi[:, k], wlo[:, k], kk == 0, kk == KT - 1)
                    m.then_inc(weights_done, 1)

                def expert_down(n):
                    pe.wait_ge(ht_lo_ready, STEPS * i + n + 1)
                    for a in range(2):
                        whi, wlo = weights(MOE + e_down(n) + a, "p (f m) -> p f m", i, f=2)
                        for f in range(2):
                            ff = 2 * a + f
                            for c in range(2):
                                m = split_product(bank[:, 3 + c, :], ht_hi[:, ff, :], ht_lo[:, ff, :],
                                                  whi[:, f, c * 512:(c + 1) * 512],
                                                  wlo[:, f, c * 512:(c + 1) * 512],
                                                  n == 0 and ff == 0, n == STEPS - 1 and ff == 3)
                        m.then_inc(weights_done, 1)

                def turn_hidden(n):
                    pe.wait_ge(e_h_ready, 1 + STEPS * i + n + 1)
                    for f in range(4):
                        m = pe.transpose(bank[:, 2, f * P:(f + 1) * P], e_h[:, f * P:(f + 1) * P], ident[:])
                    m.then_inc(ht_psum, 1)

                pe.wait_ge(xg_lo_ready, i + 1)
                for n in range(STEPS):
                    pe.wait_ge(e_silu_ready, 1 + STEPS * i + n)
                    hidden_half(e_gate(n), 0)
                    hidden_half(e_gate(n) + 1, 0)
                    if n == 1:
                        turn_hidden(0)
                        pe.wait_ge(y_ready, 1 + 2 * i)
                    pe.wait_ge(e_h_ready, 1 + STEPS * i + n)
                    hidden_half(e_gate(n) + 2, 1)
                    hidden_half(e_gate(n) + 3, 1)
                    if n == 0:
                        pe.wait_ge(scatter_added, 1 + 4 * i)
                        pe.wait_ge(gate_col_ready, i + 1)
                        for t in range(NT):
                            pe.transpose(bank[:, 7, t * P:(t + 1) * P], pick[:, t, :].bitcast(F32), ident[:])
                        for t in range(NT):
                            m = pe.matmul(bank[:, 7, 256:257], pick[:, t, :].bitcast(F32),
                                          gate_col[:, t:t + 1], start=t == 0, stop=t == NT - 1)
                        m.then_inc(slots_psum, 1)
                    else:
                        expert_down(n - 1)
                        turn_hidden(n)
                    if n == 3:
                        with pe.If(i < end - 1):
                            gather(i + 1)
                        with pe.Else():
                            pe.nop()
                        pe.nop()
                expert_down(STEPS - 1)
                for c in range(2):
                    pe.wait_ge(y_lo_ready, 2 * i + c + 1)
                    for t in range(NT):
                        o = bank[:, (5, 6, 7, 2)[2 * c + t], :]
                        pe.matmul(o, pick_t[:, t * P:(t + 1) * P], y_hi[:, c, :], start=True, stop=False)
                        pe.matmul(o, pick_t[:, t * P:(t + 1) * P], y_lo[:, c, :], start=False,
                                  stop=True).then_inc(scattered_psum, 1)

        @block.scalar
        def _(act):
            def split(g, i=None):
                act.wait_ge(loaded[g % RAW], 16 * (g // RAW + 1) + (0 if i is None else 16 * (FFN_G // RAW) * i))
                if g >= SPLIT:
                    act.wait_ge(weights_done, g - SPLIT + 1 + (0 if i is None else FFN_G * i))
                act.activation(w_hi[:, g % SPLIT, :], raw[:, g % RAW, :], ACT.Copy).then_inc(hi_ready, 1)

            def square(v):
                act.activation(xn[:], h_t[:], ACT.Square).then_inc(squares_ready, 1)

            def norm(v):
                act.wait_ge(square_sum_ready, v + 1)
                act.activation(rms_t[:], bank[:, 7, 0:L], ACT.Sqrt, bias=eps[:], scale=1.0 / D).then_inc(rms_ready, 1)
                for b in range(2):
                    act.wait_ge(xn_ready, KT * v + 4 * (b + 1))
                    act.activation(xn_hi[:, 4 * b:4 * b + 4, :], xn[:, 4 * b:4 * b + 4, :],
                                   ACT.Copy).then_inc(xn_hi_ready, 1)

            def project(l):
                g0 = MIX1 * l
                for g in range(5):
                    split(g0 + g + AHEAD)
                    act.wait_ge(weights_done, g0 + g + 1)
                    if g < 2:
                        if l and not g:
                            act.wait_ge(zeros_ready, 3)
                        for c in range(2):
                            act.activation(u_pad[:, 2 * g + c, META:], bank[:, 2 * g + c, 0:L],
                                           ACT.Copy).then_inc(proj_evicted, 1)
                    elif g == 2:
                        act.activation(k_t[:], bank[:, 4, 0:L], ACT.Copy).then_inc(proj_evicted, 1)
                        for t in range(NT + 1):
                            m = P if t < NT else META
                            act.activation(v_tok[0:m, t, :], bank[0:m, 5 + t, 0:P],
                                           ACT.Copy).then_inc(proj_evicted, 1)
                    else:
                        for c in range(2):
                            j = 2 * (g - 3) + c
                            act.activation(q_t[:, j, :], bank[:, j, 0:L], ACT.Copy,
                                           scale=HD ** -0.5).then_inc(proj_evicted, 1)

            def attention(l):
                us, u0 = units(l), UNIT0[l]
                for step in range(len(us) + 4):
                    if step < len(us):
                        t, j, b = us[step]
                        m = P if t < NT else META
                        n = key_blocks(t)[-1][2]
                        head = l * HEADS + j + 4 * b
                        c = slice(step, step + 1)
                        act.wait_ge(neg_max_ready, u0 + step + 1)
                        act.activation(prob[0:m, step % 3, 0:n], prob[0:m, step % 3, 0:n], ACT.Exp,
                                       bias=neg_max[0:m, c], accum_out=exp_sum[0:m, c]).then_inc(exp_ready, 1)
                        act.activation(exp_sink[0:m, c], sink[0:m, head:head + 1], ACT.Exp,
                                       bias=neg_max[0:m, c]).then_inc(exp_sink_ready, 1)
                    u = step - 2
                    if 0 <= u < len(us):
                        t, j, b = us[u]
                        m = P if t < NT else META
                        act.wait_ge(prob_t_psum, u0 + u + 1)
                        if u >= 2:
                            act.wait_ge(head_out_ready, u0 + u - 1)
                        if t < NT:
                            act.activation(prob_t[:, u % 2, 0:t + 1, :],
                                           bank[:, 3 + u % 2, 0:(t + 1) * P].rearrange("p (a b) -> p a b", b=P),
                                           ACT.Copy).then_inc(prob_t_main, 1)
                        act.activation(prob_t[0:META, u % 2, NT, 0:m],
                                       bank[0:META, 3 + u % 2, NT * P:NT * P + m],
                                       ACT.Copy).then_inc(prob_t_meta, 1)
                    u = step - 4
                    if u >= 0 and u % 2:
                        t, j, b = us[u]
                        act.wait_ge(head_out_ready, u0 + u + 1)
                        w = P if t < NT else META
                        act.activation(mix_hi[:, j, tile_cols(t)], bank[:, 5 + u // 2 % 2, 0:w],
                                       ACT.Copy).then_inc(mix_hi_ready, 1)
                for g in range(POOL_GROUPS):
                    act.wait_ge(pool_out_ready, POOL_GROUPS * l + g + 1)
                    act.activation(mix_hi[:, 4 + g, :], bank[:, g, 0:L], ACT.Copy,
                                   scale=pscale[:, POOL_GROUPS * l + g:POOL_GROUPS * l + g + 1]
                                   ).then_inc(mix_hi_ready, 1)

            act.wait_ge(x_loaded, 16)
            square(0)
            split(0)
            split(1)
            act.wait_ge(consts_built, CONSTS)
            norm(0)
            project(0)
            act.wait_ge(consts_loaded, 16 * LOADS)
            attention(0)
            for gg in range(4):
                split(5 + gg + AHEAD)
            act.wait_ge(out_added, KT)
            square(1)
            norm(1)
            for n in range(STEPS):
                for s in range(2):
                    pair = 2 * n + s
                    g = ffn_gate(n, s)
                    split(g + AHEAD)
                    act.wait_ge(weights_done, g + 1)
                    if pair:
                        act.wait_ge(ff_h_ready, pair)
                    act.activation(ff_silu[:], bank[:, 0:2, 0:L], ACT.Silu).then_inc(silu_ready, 1)
                    split(g + 1 + AHEAD)
                    act.wait_ge(ff_h_ready, pair + 1)
                    act.activation(ff_hi[:, pair % 4], ff_h[:], ACT.Copy).then_inc(ff_hi_ready, 1)
                if n:
                    split(ffn_gate(n, 0) + 4 + AHEAD)
                    split(ffn_gate(n, 0) + 5 + AHEAD)
            split(MIX1)
            split(MIX1 + 1)

            act.wait_ge(down_added, KT * STEPS)
            square(2)
            norm(2)
            project(1)
            attention(1)
            for gg in range(4):
                split(MIX1 + 5 + gg + AHEAD)

            def token_rms(source, first):
                for t in range(NT):
                    act.activation(source(t), h_tok[:, t, :], ACT.Square,
                                   accum_out=sums[:, t:t + 1]).then_inc(tok_sum_ready, 1)
                act.wait_ge(tok_sum_ready, NT * (first + 1))
                act.activation(rms[:], sums[:], ACT.Sqrt, bias=eps[:], scale=1.0 / D).then_inc(tok_rms_ready, 1)

            act.wait_ge(h_tok_ready, 4)
            token_rms(lambda t: n_tok[:, t, :], 0)
            for t in range(NT):
                act.wait_ge(n_tok_ready, t + 1)
                act.activation(n_hi[:, t, :], n_tok[:, t, :], ACT.Copy).then_inc(n_hi_ready, 1)
            for k in range(KT):
                act.wait_ge(xr_psum, k // 2 + 1)
                act.activation(xr[:, k, :], bank[:, 4 + k // 2, (k % 2) * SEQ:(k % 2 + 1) * SEQ], ACT.Copy,
                               scale=gain[:, 3, k:k + 1]).then_inc(xr_ready, 1)
            act.wait_ge(route_step, GAP)
            act.activation(e2[:], gap[:], ACT.Exp).then_inc(gap_exp_ready, 1)
            act.wait_ge(route_step, ROUTED)
            end = act.value_load(rounds[0:1, 0:1], min_val=EXPERTS, max_val=2 * EXPERTS)

            act.wait_ge(xg_ready, 2)
            act.activation(xg_hi[:], xg[:], ACT.Copy).then_inc(xg_hi_ready, 1)
            act.nop().then_inc(e_silu_ready, 1)
            act.nop().then_inc(y_ready, 1)
            with act.Fori(0, end) as i:
                def step_of(j):
                    for n in range(STEPS):
                        if j == e_gate(n) + 1:
                            act.wait_ge(weights_done, MOE + j + 1 + FFN_G * i)
                            act.wait_ge(e_h_ready, 1 + STEPS * i + n)
                            act.activation(e_silu[:], bank[:, 0, :], ACT.Silu).then_inc(e_silu_ready, 1)
                        if j == (e_gate(1) + 1 if n == 0 else e_down(n - 1) + 1):
                            act.wait_ge(ht_psum, 1 + STEPS * i + n + 1)
                            act.activation(ht_hi[:], bank[:, 2, :].rearrange("p (f m) -> p f m", f=4),
                                           ACT.Copy).then_inc(ht_hi_ready, 1)
                    if j == 4:
                        act.wait_ge(slots_psum, i + 1)
                        act.activation(pick_t[:], bank[:, 7, 0:SEQ], ACT.Copy).then_inc(slots_ready, 1)
                        act.activation(slot_gate[:], bank[:, 7, SEQ:SEQ + 1], ACT.Copy).then_inc(slots_ready, 1)
                    if j == FFN_G - 4:
                        with act.If(i < end - 1):
                            act.wait_ge(weights_done, MOE + e_gate(STEPS - 1) + 4 + FFN_G * i)
                            act.wait_ge(xg_ready, 2 * i + 4)
                            act.activation(xg_hi[:], xg[:], ACT.Copy).then_inc(xg_hi_ready, 1)
                        with act.Else():
                            act.nop()
                        act.nop()

                for j in range(FFN_G - AHEAD):
                    split(MOE + j + AHEAD, i)
                    step_of(j)
                with act.If(i < end - 1):
                    split(MOE + FFN_G, i)
                    split(MOE + FFN_G + 1, i)
                with act.Else():
                    act.nop()
                act.nop()
                act.wait_ge(weights_done, MOE + FFN_G + FFN_G * i)
                act.wait_ge(slots_ready, 2 * i + 2)
                for c in range(2):
                    act.activation(y[:, c, :], bank[:, 3 + c, :], ACT.Copy, scale=slot_gate[:]).then_inc(y_ready, 1)
                for c in range(2):
                    act.wait_ge(y_ready, 1 + 2 * i + c + 1)
                    act.activation(y_hi[:, c, :], y[:, c, :], ACT.Copy).then_inc(y_hi_ready, 1)

            act.wait_ge(scatter_added, 1 + 4 * end)
            token_rms(lambda t: n_tok[:, t, :], 1)

        @block.vector
        def _(dve):
            def split(g, i=None):
                dve.wait_ge(hi_ready, g + 1 + (0 if i is None else FFN_G * i))
                dve.tensor_tensor(w_lo[:, g % SPLIT, :], raw[:, g % RAW, :],
                                  w_hi[:, g % SPLIT, :].bitcast(F32), ALU.subtract).then_inc(lo_ready, 1)

            def norm(v):
                dve.wait_ge(rms_ready, v + 1)
                dve.reciprocal(rstd[:], rms_t[:]).then_inc(rstd_ready, 1)
                dve.wait_ge(rstd_ready, v + 1)
                for k in range(KT):
                    dve.scalar_tensor_tensor(xn[:, k, :], h_t[:, k, :], gain[:, NORM_GAIN[v], k:k + 1],
                                             rstd[:], ALU.mult, ALU.mult).then_inc(xn_ready, 1)
                for b in range(2):
                    dve.wait_ge(xn_hi_ready, 2 * v + b + 1)
                    dve.tensor_tensor(xn_lo[:, 4 * b:4 * b + 4, :], xn[:, 4 * b:4 * b + 4, :],
                                      xn_hi[:, 4 * b:4 * b + 4, :].bitcast(F32),
                                      ALU.subtract).then_inc(xn_lo_ready, 1)

            def attention(l):
                us, u0, m0 = units(l), UNIT0[l], MIXED0[l]
                for step in range(len(us) + 5):
                    if step < len(us):
                        t, j, b = us[step]
                        m = P if t < NT else META
                        n = key_blocks(t)[-1][2]
                        head = l * HEADS + j + 4 * b
                        c = slice(step, step + 1)
                        dve.wait_ge(scores_ready, u0 + step + 1)
                        if step >= 3:
                            dve.wait_ge(prob_t_psum, u0 + step - 2)
                        dve.tensor_tensor_reduce(prob[0:m, step % 3, 0:n], bank[0:m, step % 3, 0:n],
                                                 mask[0:m, t % NT, 0:n], 1.0, sink[0:m, head:head + 1],
                                                 ALU.add, ALU.max, row_max[0:m, c]).then_inc(masked_ready, 1)
                        dve.wait_ge(masked_ready, u0 + step + 1)
                        dve.tensor_scalar(neg_max[0:m, c], row_max[0:m, c], -1.0, None,
                                          ALU.mult).then_inc(neg_max_ready, 1)
                    u = step - 1
                    if 0 <= u < len(us):
                        t, j, b = us[u]
                        m = P if t < NT else META
                        n = key_blocks(t)[-1][2]
                        c = slice(u, u + 1)
                        dve.wait_ge(exp_ready, u0 + u + 1)
                        dve.wait_ge(exp_sink_ready, u0 + u + 1)
                        dve.tensor_tensor(den[0:m, c], exp_sum[0:m, c], exp_sink[0:m, c],
                                          ALU.add).then_inc(den_ready, 1)
                        dve.wait_ge(den_ready, u0 + u + 1)
                        dve.reciprocal(inv_den[0:m, c], den[0:m, c]).then_inc(inv_den_ready, 1)
                        dve.wait_ge(inv_den_ready, u0 + u + 1)
                        dve.tensor_scalar(prob[0:m, u % 3, 0:n], prob[0:m, u % 3, 0:n], inv_den[0:m, c],
                                          None, ALU.mult).then_inc(prob_ready, 1)
                    u = step - 5
                    if u >= 0 and u % 2:
                        t, j, b = us[u]
                        dve.wait_ge(mix_hi_ready, m0 + u // 2 + 1)
                        w = P if t < NT else META
                        dve.tensor_tensor(mix_lo[:, j, tile_cols(t)], bank[:, 5 + u // 2 % 2, 0:w],
                                          mix_hi[:, j, tile_cols(t)].bitcast(F32),
                                          ALU.subtract).then_inc(mix_lo_ready, 1)
                u = len(us) - 1
                t, j, b = us[u]
                w = P if t < NT else META
                for g in range(POOL_GROUPS):
                    dve.wait_ge(mix_hi_ready, m0 + len(us) // 2 + g + 1)
                    dve.scalar_tensor_tensor(mix_lo[:, 4 + g, :], bank[:, g, 0:L],
                                             pscale[:, POOL_GROUPS * l + g:POOL_GROUPS * l + g + 1],
                                             mix_hi[:, 4 + g, :].bitcast(F32), ALU.mult,
                                             ALU.subtract).then_inc(mix_lo_ready, 1)

            dve.wait_ge(consts_built, CONSTS)
            dve.reciprocal(inv_count[:], head_count[:]).then_inc(inv_count_ready, 1)
            dve.wait_ge(consts_loaded, 16)
            split(0)
            split(1)
            dve.wait_ge(x_loaded, 16)
            dve.wait_ge(consts_loaded, 16 * LOADS)
            norm(0)
            for g in range(5):
                split(g + AHEAD)
            attention(0)
            for gg in range(4):
                split(5 + gg + AHEAD)
                dve.wait_ge(weights_done, 5 + gg + 1)
                for c in range(2):
                    dt = 2 * gg + c
                    dve.tensor_tensor(h_t[:, dt, :], h_t[:, dt, :], bank[:, dt, 0:L],
                                      ALU.add).then_inc(out_added, 1)
            norm(1)

            def add_down(q, g):
                for d in range(4):
                    if d < 3:
                        dve.wait_ge(down_part, 3 * q + d + 1)
                    else:
                        dve.wait_ge(weights_done, g + 1)
                    if q >= 2:
                        dve.wait_ge(down_added, 4 * (q - 2) + d + 1)
                    dt = 4 * (q % 2) + d
                    dve.tensor_tensor(h_t[:, dt, :], h_t[:, dt, :], bank[:, 4 + d, 0:L],
                                      ALU.add).then_inc(down_added, 1)

            def hidden_rest(pair):
                dve.wait_ge(ff_hi_ready, pair + 1)
                dve.tensor_tensor(ff_lo[:, pair % 4], ff_h[:], ff_hi[:, pair % 4].bitcast(F32),
                                  ALU.subtract).then_inc(ff_lo_ready, 1)

            for n in range(STEPS):
                for s in range(2):
                    pair = 2 * n + s
                    g = ffn_gate(n, s)
                    split(g + AHEAD)
                    if s:
                        hidden_rest(pair - 1)
                    split(g + 1 + AHEAD)
                    dve.wait_ge(weights_done, g + 2)
                    dve.wait_ge(silu_ready, pair + 1)
                    if pair:
                        dve.wait_ge(ff_lo_ready, pair)
                    dve.tensor_tensor(ff_h[:], ff_silu[:], bank[:, 2:4, 0:L], ALU.mult).then_inc(ff_h_ready, 1)
                if n:
                    split(ffn_gate(n, 0) + 4 + AHEAD)
                    hidden_rest(2 * n + 1)
                    add_down(2 * n - 2, ffn_gate(n, 0) + 4)
                    split(ffn_gate(n, 0) + 5 + AHEAD)
                    add_down(2 * n - 1, ffn_gate(n, 0) + 5)
                else:
                    hidden_rest(1)
            split(MIX1)
            add_down(2 * STEPS - 2, MIX1 - 2)
            split(MIX1 + 1)
            add_down(2 * STEPS - 1, MIX1 - 1)

            norm(2)
            for g in range(5):
                split(MIX1 + g + AHEAD)
            attention(1)
            for gg in range(4):
                split(MIX1 + 5 + gg + AHEAD)
            for n in range(2):
                for t in range(NT):
                    dve.wait_ge(out_tok_psum, 2 * n + t + 1)
                    dve.tensor_copy(h_tok[:, t, 512 * n:512 * n + 512], bank[:, 2 * n + t, :]
                                    ).then_inc(h_tok_ready, 1)

            def token_rstd(first):
                dve.wait_ge(tok_rms_ready, first + 1)
                dve.reciprocal(rstd2[:], rms[:]).then_inc(tok_rstd_ready, 1)
                dve.wait_ge(tok_rstd_ready, first + 1)

            token_rstd(0)
            for t in range(NT):
                dve.tensor_scalar(n_tok[:, t, :], h_tok[:, t, :], rstd2[:, t:t + 1], None,
                                  ALU.mult).then_inc(n_tok_ready, 1)
            for t in range(NT):
                dve.wait_ge(n_hi_ready, t + 1)
                dve.tensor_tensor(n_lo[:, t, :], n_tok[:, t, :], n_hi[:, t, :].bitcast(F32),
                                  ALU.subtract).then_inc(n_lo_ready, 1)

            def wide(a):
                return a[:].unsqueeze(2).to_broadcast([P, NT, EXPERTS])

            def by_token(a, first):
                return a[:, first:first + EXPERTS, :].rearrange("p e t -> p t e")

            dve.wait_ge(logits_psum, 1)
            dve.tensor_copy(lg[:], bank[:, 0, 0:NT * EXPERTS].rearrange("p (t e) -> p t e", t=NT)).then_inc(route_step, 1)
            dve.wait_ge(route_step, 1)
            dve.tensor_reduce(m1[:], lg[:], AXX, ALU.max).then_inc(route_step, 1)
            dve.wait_ge(route_step, 2)
            dve.tensor_tensor(eq[:], lg[:], wide(m1), ALU.is_equal).then_inc(route_step, 1)
            dve.wait_ge(route_step, 3)
            dve.scalar_tensor_tensor(cand[:], eq[:], -100.0, expert_no[:], ALU.mult, ALU.add).then_inc(route_step, 1)
            dve.wait_ge(route_step, 4)
            dve.tensor_reduce(least[:], cand[:], AXX, ALU.min).then_inc(route_step, 1)
            dve.wait_ge(route_step, 5)
            dve.tensor_tensor(oh1[:], cand[:], wide(least), ALU.is_equal).then_inc(route_step, 1)
            dve.wait_ge(route_step, 6)
            dve.scalar_tensor_tensor(l2[:], oh1[:], -3e38, lg[:], ALU.mult, ALU.add).then_inc(route_step, 1)
            dve.wait_ge(route_step, 7)
            dve.tensor_reduce(m2[:], l2[:], AXX, ALU.max).then_inc(route_step, 1)
            dve.wait_ge(route_step, 8)
            dve.tensor_tensor(gap[:], m2[:], m1[:], ALU.subtract).then_inc(route_step, 1)
            dve.tensor_tensor(eq[:], l2[:], wide(m2), ALU.is_equal).then_inc(route_step, 1)
            dve.wait_ge(route_step, 10)
            dve.scalar_tensor_tensor(cand[:], eq[:], -100.0, expert_no[:], ALU.mult, ALU.add).then_inc(route_step, 1)
            dve.wait_ge(route_step, 11)
            dve.tensor_reduce(least[:], cand[:], AXX, ALU.min).then_inc(route_step, 1)
            dve.wait_ge(route_step, 12)
            dve.tensor_tensor(oh2[:], cand[:], wide(least), ALU.is_equal).then_inc(route_step, 1)
            dve.wait_ge(route_step, 13)
            dve.tensor_tensor(chosen[:], oh1[:], oh2[:], ALU.add).then_inc(route_step, 1)
            dve.wait_ge(gap_exp_ready, 1)
            dve.tensor_scalar(den2[:], e2[:], 1.0, None, ALU.add).then_inc(route_step, 1)
            dve.wait_ge(route_step, 15)
            dve.reciprocal(g1[:], den2[:]).then_inc(route_step, 1)
            dve.wait_ge(route_step, 16)
            dve.tensor_tensor(g2[:], e2[:], g1[:], ALU.mult).then_inc(route_step, 1)
            dve.tensor_tensor(ga[:], oh1[:], wide(g1), ALU.mult).then_inc(route_step, 1)
            dve.wait_ge(route_step, 18)
            dve.tensor_tensor(gb[:], oh2[:], wide(g2), ALU.mult).then_inc(route_step, 1)
            dve.wait_ge(route_step, 19)
            for q in range(2):
                dve.tensor_tensor(by_token(gates, EXPERTS * q), ga[:], gb[:], ALU.add).then_inc(route_step, 1)
            dve.wait_ge(places_psum, 1)
            dve.scalar_tensor_tensor(posa[:], bank[:, 1, 0:16].rearrange("p (t e) -> p t e", t=NT), 1000.0,
                                     chosen[:], ALU.add, ALU.mult).then_inc(route_step, 1)
            dve.tensor_reduce(most[:], bank[:, 1, 16:24], AXX, ALU.max).then_inc(route_step, 1)
            dve.wait_ge(route_step, 23)
            for q in range(2):
                dve.tensor_scalar(by_token(place, EXPERTS * q), posa[:], -1000.0 - P * q, None,
                                  ALU.add).then_inc(route_step, 1)
            dve.tensor_scalar(rounds_f[:], most[:], float(P), float(EXPERTS), ALU.is_gt,
                              ALU.mult).then_inc(route_step, 1)
            dve.wait_ge(route_step, 26)
            dve.tensor_scalar(rounds[:], rounds_f[:], float(EXPERTS), None, ALU.add).then_inc(route_step, 1)
            dve.wait_ge(route_step, ROUTED)
            end = dve.value_load(rounds[0:1, 0:1], min_val=EXPERTS, max_val=2 * EXPERTS)

            def choose(r):
                for t in range(NT):
                    dve.tensor_scalar(pick[:, t, :], slot_no[:], place[:, bass.ds(r, 1), t], None,
                                      ALU.is_equal).then_inc(pick_ready, 1)
                dve.tensor_copy(gate_col[:], gates[:, bass.ds(r, 1), :].rearrange("p a t -> p (a t)")
                                ).then_inc(gate_col_ready, 1)

            def gained(r, k0):
                for b in range(2):
                    dve.wait_ge(gathered_psum, k0 + b)
                    dve.tensor_tensor(xg[:, 4 * b:4 * b + 4, :],
                                      bank[:, 5 + b, :].rearrange("p (k m) -> p k m", k=4),
                                      gain[:, 3, 4 * b:4 * b + 4].unsqueeze(2).to_broadcast([P, 4, P]),
                                      ALU.mult).then_inc(xg_ready, 1)

            choose(0)
            gained(0, 1)
            dve.wait_ge(xg_hi_ready, 1)
            dve.tensor_tensor(xg_lo[:], xg[:], xg_hi[:].bitcast(F32), ALU.subtract).then_inc(xg_lo_ready, 1)
            dve.nop().then_inc(e_h_ready, 1)
            dve.nop().then_inc(scatter_added, 1)
            with dve.Fori(0, end) as i:
                def step_of(j):
                    for n in range(STEPS):
                        if j == e_gate(n) + 3:
                            dve.wait_ge(weights_done, MOE + j + 1 + FFN_G * i)
                            dve.wait_ge(e_silu_ready, 1 + STEPS * i + n + 1)
                            dve.wait_ge(ht_psum, 1 + STEPS * i + n)
                            dve.tensor_tensor(e_h[:], e_silu[:], bank[:, 1, :], ALU.mult).then_inc(e_h_ready, 1)
                        if j == (e_gate(1) + 1 if n == 0 else e_down(n - 1) + 1):
                            dve.wait_ge(ht_hi_ready, STEPS * i + n + 1)
                            dve.tensor_tensor(ht_lo[:], bank[:, 2, :].rearrange("p (f m) -> p f m", f=4),
                                              ht_hi[:].bitcast(F32), ALU.subtract).then_inc(ht_lo_ready, 1)
                    if j == 12:
                        with dve.If(i < end - 1):
                            dve.wait_ge(slots_psum, i + 1)
                            choose(i + 1)
                        with dve.Else():
                            dve.nop()
                        dve.nop()
                    if j == e_down(3) - 4:
                        with dve.If(i < end - 1):
                            gained(i + 1, 2 * i + 3)
                        with dve.Else():
                            dve.nop()
                        dve.nop()
                    if j == FFN_G - 3:
                        with dve.If(i < end - 1):
                            dve.wait_ge(xg_hi_ready, i + 2)
                            dve.tensor_tensor(xg_lo[:], xg[:], xg_hi[:].bitcast(F32),
                                              ALU.subtract).then_inc(xg_lo_ready, 1)
                        with dve.Else():
                            dve.nop()
                        dve.nop()

                for j in range(FFN_G - AHEAD):
                    split(MOE + j + AHEAD, i)
                    step_of(j)
                with dve.If(i < end - 1):
                    split(MOE + FFN_G, i)
                    split(MOE + FFN_G + 1, i)
                with dve.Else():
                    dve.nop()
                dve.nop()
                for c in range(2):
                    dve.wait_ge(y_hi_ready, 2 * i + c + 1)
                    dve.tensor_tensor(y_lo[:, c, :], y[:, c, :], y_hi[:, c, :].bitcast(F32),
                                      ALU.subtract).then_inc(y_lo_ready, 1)
                dve.wait_ge(scatter_added, 1 + 4 * i)
                for c in range(2):
                    for t in range(NT):
                        dve.wait_ge(scattered_psum, 4 * i + 2 * c + t + 1)
                        dve.tensor_tensor(h_tok[:, t, 512 * c:512 * c + 512], h_tok[:, t, 512 * c:512 * c + 512],
                                          bank[:, (5, 6, 7, 2)[2 * c + t], :], ALU.add).then_inc(scatter_added, 1)

            token_rstd(1)
            for t in range(NT):
                dve.scalar_tensor_tensor(n_tok[:, t, :], h_tok[:, t, :], rstd2[:, t:t + 1], g_final[:],
                                         ALU.mult, ALU.mult).then_inc(out_ready, 1)


def kernel(x, meta_tokens, norm_mix_g, w_in, attn_sinks, pool_w, pool_scale, w_out, norm_ffn_g,
           dense_w_gate, dense_w_up, dense_w_down, moe_w_router, moe_w_gate, moe_w_up, moe_w_down,
           final_norm_g):
    import numpy as np
    import concourse.bacc as bacc
    from concourse.bass_utils import run_bass_kernel_spmd

    (x, meta_tokens, norm_mix_g, w_in, attn_sinks, pool_w, pool_scale, w_out, norm_ffn_g, dense_w_gate,
     dense_w_up, dense_w_down, moe_w_router, moe_w_gate, moe_w_up, moe_w_down, final_norm_g) = (
        np.asarray(a) for a in (
            x, meta_tokens, norm_mix_g, w_in, attn_sinks, pool_w, pool_scale, w_out, norm_ffn_g,
            dense_w_gate, dense_w_up, dense_w_down, moe_w_router, moe_w_gate, moe_w_up, moe_w_down,
            final_norm_g))

    h0 = np.concatenate([meta_tokens, x[0]], axis=0)
    x_t = np.ascontiguousarray(h0.T.reshape(KT, P, L).transpose(1, 0, 2))
    gains = np.ascontiguousarray(
        np.concatenate([norm_mix_g, norm_ffn_g], axis=0).reshape(4, KT, P).transpose(2, 0, 1))
    sinks = np.ascontiguousarray(attn_sinks.reshape(-1))
    pw = np.ascontiguousarray(pool_w.reshape(2 * POOL_GROUPS, P, P).transpose(1, 0, 2))
    pscale = np.ascontiguousarray(pool_scale.reshape(2 * POOL_GROUPS, P).T)
    router = np.ascontiguousarray(moe_w_router[0].reshape(KT, P, EXPERTS).transpose(1, 0, 2))

    heads = [h for j in range(HEADS // 2) for h in (j, j + HEADS // 2)]
    qcols = np.concatenate([np.arange(HD * h, HD * h + HD) for h in heads])
    d_attn = HEADS * HD

    def col_tiles(w):
        n = w.shape[1] // (2 * P)
        return w.reshape(KT, P, n, 2, P).transpose(2, 1, 3, 0, 4).reshape(n, P, GW)

    w_mix = np.empty((2, MIX_G, P, GW), w_in.dtype)
    for l in range(2):
        w_mix[l, 0:2] = col_tiles(w_in[l][:, d_attn + 2 * P:])
        w_mix[l, 2] = w_in[l][:, d_attn:d_attn + 2 * P].reshape(KT, P, 2 * P).transpose(1, 0, 2).reshape(P, GW)
        w_mix[l, 3:5] = col_tiles(w_in[l][:, qcols])
        wo = np.concatenate([w_out[l][qcols], w_out[l][d_attn:]], axis=0)
        if l == 0:
            w_mix[l, 5:9] = col_tiles(wo)
        else:
            w_mix[l, 5:9] = wo.reshape(2, 4, P, 2, 512).transpose(3, 0, 2, 1, 4).reshape(4, P, GW)

    w_ffn = np.empty((FFN_G, P, GW), dense_w_gate.dtype)
    gate, up = col_tiles(dense_w_gate[0]), col_tiles(dense_w_up[0])
    down = dense_w_down[0].reshape(STEPS, 4, P, 2, 4, P).transpose(0, 3, 2, 4, 1, 5).reshape(STEPS, 2, P, GW)
    for n in range(STEPS):
        g = 0 if n == 0 else 4 + 6 * (n - 1)
        for s in range(2):
            w_ffn[g + 2 * s] = gate[2 * n + s]
            w_ffn[g + 2 * s + 1] = up[2 * n + s]
        d = 8 + 6 * n if n < STEPS - 1 else FFN_G - 2
        w_ffn[d:d + 2] = down[n]

    w_moe = np.empty((EXPERTS, FFN_G, P, GW), moe_w_gate.dtype)
    gate, up = (w[0].reshape(EXPERTS, 2, 4, P, STEPS, 512).transpose(0, 4, 1, 3, 2, 5).reshape(
        EXPERTS, STEPS, 2, P, GW) for w in (moe_w_gate, moe_w_up))
    down = moe_w_down[0].reshape(EXPERTS, STEPS, 2, 2, P, D).transpose(0, 1, 2, 4, 3, 5).reshape(
        EXPERTS, STEPS, 2, P, GW)
    for n in range(STEPS):
        g = 0 if n == 0 else 4 + 6 * (n - 1)
        w_moe[:, g:g + 2] = gate[:, n]
        w_moe[:, g + 2:g + 4] = up[:, n]
        d = 8 + 6 * n if n < STEPS - 1 else FFN_G - 2
        w_moe[:, d:d + 2] = down[:, n]

    arrays = {
        "x_t": x_t, "gains": gains, "sinks": sinks, "pool_w": pw, "pool_scale": pscale,
        "final_g": np.ascontiguousarray(final_norm_g), "w_router": router, "w_mix": w_mix,
        "w_ffn": w_ffn, "w_moe": w_moe,
    }
    nc = bacc.Bacc("TRN2", target_bir_lowering=False, num_devices=1)
    args = [nc.dram_tensor(n, a.shape, mybir.dt.from_np(a.dtype), kind="ExternalInput").ap()
            for n, a in arrays.items()]
    out = nc.dram_tensor("out", (SEQ, D), F32, kind="ExternalOutput").ap()
    build(nc, *args, out)
    r = run_bass_kernel_spmd(nc, [arrays], core_ids=[0])
    return r.results[0]["out"].reshape(1, SEQ, D)
```

```python
from contextlib import ExitStack

import concourse.bass as bass
from concourse import mybir

F32 = mybir.dt.float32
F32R = mybir.dt.float32r
I32 = mybir.dt.int32
U32 = mybir.dt.uint32
ALU = mybir.AluOpType
ACT = mybir.ActivationFunctionType
AXX = mybir.AxisListType.X

P = 128
D = 1024
KT = D // P
META, SEQ, CHUNK = 16, 256, 64
L = META + SEQ
NT = SEQ // P
HEADS, HD = 8, 64
POOL_GROUPS = 4
FF = 3584
STEPS = FF // 512
EXPERTS = 8
EPS = 1e-5
NEG = -1e30

GW = 2048
RAW = 7
SPLIT = 3
MIX_G = 9
FFN_G = 6 * STEPS
FFN0 = MIX_G
MIX1 = MIX_G + FFN_G
MOE = MIX1 + MIX_G
LOADS = 5
CONSTS = 20
WINDOW_STEPS = 12
GAP, CHOSEN, ROUTED = 5, 11, 17
GATED = 24
AHEAD = 2


def build(nc, x_t, gains, sinks, pool_w, pool_scale, final_g, w_router, w_mix, w_ffn, w_moe, out):
    with ExitStack() as ctx:
        def sb(name, shape, dt=F32):
            return ctx.enter_context(nc.sbuf_tensor(name, shape, dt))

        def sem(name):
            return ctx.enter_context(nc.semaphore(name))

        bank = ctx.enter_context(nc.psum_tensor("bank", [P, 8, 512], F32))

        raw = sb("raw", [P, RAW, GW])
        w_hi = sb("w_hi", [P, SPLIT, GW], F32R)
        w_lo = sb("w_lo", [P, SPLIT, GW], F32R)
        h_t = sb("h_t", [P, KT, L])
        gain = sb("gain", [P, 4, KT])
        sink = sb("sink", [P, 2 * HEADS])
        pw = sb("pw", [P, 2 * POOL_GROUPS, P])
        pscale = sb("pscale", [P, 2 * POOL_GROUPS])
        router = sb("router", [P, KT, EXPERTS])
        g_final = sb("g_final", [P, D])
        eps = sb("eps", [P, 1])
        ones = sb("ones", [P, P])
        ident = sb("ident", [P, P])
        before = sb("before", [P, P])
        slot_no = sb("slot_no", [P, P])
        expert_no = sb("expert_no", [P, NT, EXPERTS])
        mask = sb("mask", [P, NT, L])
        head_count = sb("head_count", [P, POOL_GROUPS, META])
        inv_count = sb("inv_count", [P, POOL_GROUPS, META])
        sums = sb("sums", [P, 2, NT])
        total = sb("total", [P, NT])
        rms = sb("rms", [P, 2])
        rstd2 = sb("rstd2", [P, 2])
        rstd = sb("rstd", [P, L])
        rms_t = sb("rms_t", [P, L])
        rms_v = sb("rms_v", [P, NT + 1])
        rstd_v = sb("rstd_v", [P, NT + 1])

        with ExitStack() as r1:
            sq, xn_hi, xn_lo = (r1.enter_context(nc.sbuf_tensor(n, [P, KT, L], t))
                                for n, t in (("sq", F32), ("xn_hi", F32R), ("xn_lo", F32R)))
        with ExitStack() as r1:
            h_tok, n_tok, n_lo = (r1.enter_context(nc.sbuf_tensor(n, [P, NT, D], t))
                                  for n, t in (("h_tok", F32), ("n_tok", F32), ("n_lo", F32R)))
        sb("region1", [P, 3 * KT * L])

        with ExitStack() as r2:
            def r(name, shape, dt=F32):
                return r2.enter_context(nc.sbuf_tensor(name, shape, dt))
            mix_hi = r("mix_hi", [P, KT, L], F32R)
            mix_lo = r("mix_lo", [P, KT, L], F32R)
            u_pad = r("u_pad", [P, POOL_GROUPS, META + L])
            win_a = r("win_a", [P, POOL_GROUPS, META + L])
            win_b = r("win_b", [P, POOL_GROUPS, META + L])
            pooled = r("pooled", [P, POOL_GROUPS, L])
            q_t = r("q_t", [P, HEADS // 2, L])
            k_t = r("k_t", [P, L])
            v_tok = r("v_tok", [P, NT + 1, P])
            prob = r("prob", [P, 3, L])
            prob_t = r("prob_t", [P, 2, NT + 1, P])
            row_max = r("row_max", [P, 24])
            neg_max = r("neg_max", [P, 24])
            exp_sum = r("exp_sum", [P, 24])
            exp_sink = r("exp_sink", [P, 24])
            den = r("den", [P, 24])
            inv_den = r("inv_den", [P, 24])
        with ExitStack() as r2:
            ff_hi = r2.enter_context(nc.sbuf_tensor("ff_hi", [P, 4, 2, L], F32R))
            ff_lo = r2.enter_context(nc.sbuf_tensor("ff_lo", [P, 4, 2, L], F32R))
            ff_silu = r2.enter_context(nc.sbuf_tensor("ff_silu", [P, 2, L], F32))
            ff_h = r2.enter_context(nc.sbuf_tensor("ff_h", [P, 2, L], F32))
        with ExitStack() as r2:
            def r(name, shape, dt=F32):
                return r2.enter_context(nc.sbuf_tensor(name, shape, dt))
            n_hi = r("n_hi", [P, NT, D], F32R)
            xr = r("xr", [P, KT, SEQ])
            xg = r("xg", [P, KT, P])
            xg_hi = r("xg_hi", [P, KT, P], F32R)
            xg_lo = r("xg_lo", [P, KT, P], F32R)
            pick = r("pick", [P, NT, P], F32R)
            pick_t = r("pick_t", [P, NT * P], F32R)
            gate_col = r("gate_col", [P, NT])
            slot_gate = r("slot_gate", [P, 1])
            e_silu = r("e_silu", [P, 512])
            e_h = r("e_h", [P, 512])
            ht_hi = r("ht_hi", [P, 4, P], F32R)
            ht_lo = r("ht_lo", [P, 4, P], F32R)
            y = r("y", [P, 2, 512])
            y_hi = r("y_hi", [P, 2, 512], F32R)
            y_lo = r("y_lo", [P, 2, 512], F32R)
            lg, top, oh1, oh2, ga, gb, chosen, posa = (
                r(n, [P, NT, EXPERTS]) for n in
                ("lg", "top", "oh1", "oh2", "ga", "gb", "chosen", "posa"))
            top_at = r("top_at", [P, NT, EXPERTS], U32)
            top_no = r("top_no", [P, NT, 2])
            gap, e2, den2, g1, g2 = (r(n, [P, NT]) for n in ("gap", "e2", "den2", "g1", "g2"))
            gates = r("gates", [P, 2 * EXPERTS + 1, NT])
            place = r("place", [P, 2 * EXPERTS + 1, NT])
            most = r("most", [P, 1])
            rounds_f = r("rounds_f", [P, 1])
            rounds = r("rounds", [P, 1], I32)

        x_loaded = [sem("x_loaded0"), sem("x_loaded1")]
        consts_loaded = sem("consts_loaded")
        loaded = [sem(f"loaded{s}") for s in range(RAW)]
        consts_built = sem("consts_built")
        hi_ready = sem("hi_ready")
        lo_ready = sem("lo_ready")
        weights_done = sem("weights_done")
        squares_ready = sem("squares_ready")
        square_sum_ready = sem("square_sum_ready")
        rms_ready = sem("rms_ready")
        rstd_ready = sem("rstd_ready")
        square_part = sem("square_part")
        v_evicted = sem("v_evicted")
        gate_scaled = sem("gate_scaled")
        up_scaled = sem("up_scaled")
        total_ready = sem("total_ready")
        gain_loaded = sem("gain_loaded")
        xn_hi_ready = sem("xn_hi_ready")
        xn_lo_ready = sem("xn_lo_ready")
        proj_evicted = sem("proj_evicted")
        window_step = sem("window_step")
        inv_count_ready = sem("inv_count_ready")
        zeros_ready = sem("zeros_ready")
        pooled_ready = sem("pooled_ready")
        scores_ready = sem("scores_ready")
        masked_ready = sem("masked_ready")
        neg_max_ready = sem("neg_max_ready")
        exp_ready = sem("exp_ready")
        exp_sink_ready = sem("exp_sink_ready")
        den_ready = sem("den_ready")
        inv_den_ready = sem("inv_den_ready")
        prob_ready = sem("prob_ready")
        prob_t_psum = sem("prob_t_psum")
        prob_t_main = sem("prob_t_main")
        prob_t_meta = sem("prob_t_meta")
        head_out_ready = sem("head_out_ready")
        pool_out_ready = sem("pool_out_ready")
        mix_hi_ready = sem("mix_hi_ready")
        mix_lo_ready = sem("mix_lo_ready")
        out_added = sem("out_added")
        silu_ready = sem("silu_ready")
        ff_h_ready = sem("ff_h_ready")
        ff_hi_ready = sem("ff_hi_ready")
        ff_lo_ready = sem("ff_lo_ready")
        down_part = sem("down_part")
        down_added = sem("down_added")
        out_tok_psum = sem("out_tok_psum")
        h_tok_ready = sem("h_tok_ready")
        tok_sum_ready = sem("tok_sum_ready")
        tok_rms_ready = sem("tok_rms_ready")
        tok_rstd_ready = sem("tok_rstd_ready")
        n_tok_ready = sem("n_tok_ready")
        n_hi_ready = sem("n_hi_ready")
        n_lo_ready = sem("n_lo_ready")
        xr_psum = sem("xr_psum")
        xr_ready = sem("xr_ready")
        xr_late_ready = sem("xr_late_ready")
        logits_psum = sem("logits_psum")
        route_step = sem("route_step")
        gap_exp_ready = sem("gap_exp_ready")
        places_psum = sem("places_psum")
        pick_ready = sem("pick_ready")
        gate_col_ready = sem("gate_col_ready")
        slots_psum = sem("slots_psum")
        slots_ready = sem("slots_ready")
        gathered_psum = sem("gathered_psum")
        xg_ready = sem("xg_ready")
        xg_hi_ready = sem("xg_hi_ready")
        xg_lo_ready = sem("xg_lo_ready")
        e_silu_ready = sem("e_silu_ready")
        e_h_ready = sem("e_h_ready")
        ht_psum = sem("ht_psum")
        ht_hi_ready = sem("ht_hi_ready")
        ht_lo_ready = sem("ht_lo_ready")
        y_ready = sem("y_ready")
        y_hi_ready = sem("y_hi_ready")
        y_lo_ready = sem("y_lo_ready")
        scattered_psum = sem("scattered_psum")
        scatter_added = sem("scatter_added")
        out_ready = sem("out_ready")
        stored = sem("stored")

        NORM_GAIN = (0, 2, 1)

        def tile_cols(t):
            return slice(META + t * P, META + (t + 1) * P) if t < NT else slice(0, META)

        def key_blocks(t):
            blocks = [(NT, 0, META)]
            if t < NT:
                blocks += [(kt, META + kt * P, META + (kt + 1) * P) for kt in range(t + 1)]
            return blocks

        def units(l):
            return [(t, j, b) for t in range(NT + 1 - l) for j in range(HEADS // 2) for b in range(2)]

        UNIT0 = (0, len(units(0)))
        PAIR0 = (0, len(units(0)) // 2)
        MIXED0 = (0, len(units(0)) // 2 + POOL_GROUPS)

        def ffn_gate(n, s):
            return FFN0 + 2 * s + (0 if n == 0 else 4 + 6 * (n - 1))

        def e_gate(n):
            return 0 if n == 0 else 4 + 6 * (n - 1)

        def e_down(n):
            return 8 + 6 * n if n < STEPS - 1 else FFN_G - 2

        block = ctx.enter_context(nc.Block())

        @block.sync
        def _(sp):
            def load(g, src, i=None):
                if g >= RAW or i is not None:
                    sp.wait_ge(lo_ready, g - RAW + 1 + (0 if i is None else FFN_G * i))
                sp.dma_start(raw[:, g % RAW, :], src).then_inc(loaded[g % RAW], 16)

            sp.dma_start(gain[:], gains).then_inc(gain_loaded, 16)
            for b in range(2):
                sp.dma_start(h_t[:, 4 * b:4 * b + 4, :], x_t[:, 4 * b:4 * b + 4, :]).then_inc(x_loaded[b], 16)
            load(0, w_mix[0, 0])
            load(1, w_mix[0, 1])
            sp.dma_start(sink[:], sinks.partition_broadcast(P)).then_inc(consts_loaded, 16)
            load(2, w_mix[0, 2])
            sp.dma_start(pw[:], pool_w).then_inc(consts_loaded, 16)
            sp.dma_start(pscale[:], pool_scale).then_inc(consts_loaded, 16)
            sp.dma_start(router[:], w_router).then_inc(consts_loaded, 16)
            sp.dma_start(g_final[:], final_g.partition_broadcast(P)).then_inc(consts_loaded, 16)
            for g in range(3, MIX_G):
                load(g, w_mix[0, g])
            for g in range(FFN_G):
                load(FFN0 + g, w_ffn[g])
            for g in range(MIX_G):
                load(MIX1 + g, w_mix[1, g])
            for g in range(RAW):
                load(MOE + g, w_moe[0, g])
            sp.wait_ge(route_step, ROUTED)
            end = sp.value_load(rounds[0:1, 0:1], min_val=EXPERTS, max_val=2 * EXPERTS)
            with sp.Fori(0, end) as i:
                this = sp.snap(i % EXPERTS)
                for g in range(RAW, FFN_G):
                    load(MOE + g, w_moe[this, g], i)
                following = sp.snap((i + 1) % EXPERTS)
                with sp.If(i < end - 1):
                    for g in range(RAW):
                        load(MOE + FFN_G + g, w_moe[following, g], i)
                with sp.Else():
                    sp.nop()
                sp.nop()
            for t in range(NT):
                sp.wait_ge(out_ready, t + 1)
                sp.dma_start(out[t * P:(t + 1) * P, :], n_tok[:, t, :]).then_inc(stored, 16)
            sp.wait_ge(stored, 16 * NT)

        @block.gpsimd
        def _(pool):
            pool.memset(eps[:], EPS).then_inc(consts_built, 1)
            pool.memset(ones[:], 1.0).then_inc(consts_built, 1)
            pool.memset(ident[:], 0.0).then_inc(consts_built, 1)
            pool.memset(before[:], 1.0).then_inc(consts_built, 1)
            pool.memset(mask[:], 0.0).then_inc(consts_built, 1)
            pool.memset(u_pad[:, :, 0:META], 0.0).then_inc(consts_built, 1)
            pool.memset(win_a[:, :, 0:META], 0.0).then_inc(consts_built, 1)
            pool.memset(win_b[:, :, 0:META], 0.0).then_inc(consts_built, 1)
            pool.iota(slot_no[:], [[1, P]], base=0, channel_multiplier=0,
                      allow_small_or_imprecise_dtypes=True).then_inc(consts_built, 1)
            pool.iota(expert_no[:], [[0, NT], [1, EXPERTS]], base=0, channel_multiplier=0,
                      allow_small_or_imprecise_dtypes=True).then_inc(consts_built, 1)
            pool.iota(head_count[:], [[0, POOL_GROUPS], [1, META]], base=1, channel_multiplier=0,
                      allow_small_or_imprecise_dtypes=True).then_inc(consts_built, 1)
            pool.wait_ge(consts_built, 11)
            pool.affine_select(ident[:], ident[:], [[-1, P]], ALU.not_equal, 1.0, base=0,
                               channel_multiplier=1).then_inc(consts_built, 1)
            pool.affine_select(before[:], before[:], [[1, P]], ALU.is_gt, 0.0, base=0,
                               channel_multiplier=-1).then_inc(consts_built, 1)
            pool.wait_ge(consts_built, 13)
            pool.memset(mask[0:64, 0, META + CHUNK:META + 2 * CHUNK], NEG).then_inc(consts_built, 1)
            pool.wait_ge(consts_built, 14)
            pool.memset(mask[0:64, 1, META + 3 * CHUNK:L], NEG).then_inc(consts_built, 1)
            pool.wait_ge(consts_built, 15)
            pool.memset(mask[64:128, 1, META:META + CHUNK], NEG).then_inc(consts_built, 1)
            pool.wait_ge(consts_built, 16)
            for g in range(POOL_GROUPS):
                pool.tensor_scalar(head_count[:, g, :], head_count[:, g, :], float(2 << g), None,
                                   ALU.min).then_inc(consts_built, 1)

            def windows(l):
                pool.wait_ge(proj_evicted, 9 * l + 4)
                done = WINDOW_STEPS * l
                src = u_pad
                for s, dst in enumerate((win_a, win_b, win_a, win_b)):
                    lag = 1 << s
                    if s:
                        pool.wait_ge(window_step, done + s)
                    pool.tensor_tensor(dst[:, s:, META:], src[:, s:, META:],
                                       src[:, s:, META - lag:META + L - lag],
                                       ALU.add).then_inc(window_step, 1)
                    src = dst
                pool.wait_ge(window_step, done + 4)
                for g, win in enumerate((win_a, win_b, win_a, win_b)):
                    pool.tensor_scalar(pooled[:, g, META:], win[:, g, 2 * META:], 1.0 / (2 << g),
                                       None, ALU.mult).then_inc(window_step, 1)
                    pool.tensor_tensor(pooled[:, g, 0:META], win[:, g, META:2 * META],
                                       inv_count[:, g, :], ALU.mult).then_inc(window_step, 1)
                pool.wait_ge(window_step, done + 12)
                pool.tensor_tensor(pooled[:], pooled[:], u_pad[:, :, META:],
                                   ALU.subtract).then_inc(pooled_ready, 1)

            pool.wait_ge(inv_count_ready, 1)
            windows(0)
            pool.wait_ge(down_added, KT * STEPS)
            pool.memset(u_pad[:, :, 0:META], 0.0).then_inc(zeros_ready, 1)
            pool.memset(win_a[:, :, 0:META], 0.0).then_inc(zeros_ready, 1)
            pool.memset(win_b[:, :, 0:META], 0.0).then_inc(zeros_ready, 1)
            pool.wait_ge(zeros_ready, 3)
            windows(1)

        @block.tensor
        def _(pe):
            def split_product(o, a_hi, a_lo, b_hi, b_lo, start, stop):
                pe.matmul(o, a_hi, b_hi, start=start, stop=False)
                pe.matmul(o, a_hi, b_lo, start=False, stop=False)
                return pe.matmul(o, a_lo, b_hi, start=False, stop=stop)

            def weights(g, shape, i=None, **sizes):
                pe.wait_ge(lo_ready, g + 1 + (0 if i is None else FFN_G * i))
                return (w_hi[:, g % SPLIT, :].rearrange(shape, **sizes),
                        w_lo[:, g % SPLIT, :].rearrange(shape, **sizes))

            def square_sum(v):
                pe.wait_ge(square_part, 3 * v + 3)
                m = pe.matmul(bank[:, 7, 0:L], ones[:], sq[:, 0, :], start=True, stop=True)
                if NORM_GAIN[v] < 2:
                    for t in range(NT + 1):
                        cols = tile_cols(t) if t < NT else slice(0, P)
                        m = pe.matmul(bank[:, 7, L + t:L + t + 1], sq[:, 0, cols], ones[:, 0:1],
                                      start=True, stop=True)
                m.then_inc(square_sum_ready, 1)

            def two_tiles(g, b0, first=None):
                whi, wlo = weights(g, "p (c k m) -> p c k m", c=2, k=KT)
                for c in range(2):
                    for k in range(KT):
                        if first is not None and c == 0:
                            pe.wait_ge(xn_lo_ready, KT * first + k + 1)
                        m = split_product(bank[:, b0 + c, 0:L], whi[:, c, k], wlo[:, c, k],
                                          xn_hi[:, k, :], xn_lo[:, k, :], k == 0, k == KT - 1)
                m.then_inc(weights_done, 1)

            def project(l):
                g0 = MIX1 * l
                two_tiles(g0, 0, 2 * l)
                square_sum(2 * l)
                two_tiles(g0 + 1, 2)
                pe.wait_ge(rms_ready, 2 * l + 1 + l + 1)
                whi, wlo = weights(g0 + 2, "p (k m) -> p k m", k=KT)
                for k in range(KT):
                    split_product(bank[:, 4, 0:L], whi[:, k, 0:P], wlo[:, k, 0:P],
                                  xn_hi[:, k, :], xn_lo[:, k, :], k == 0, k == KT - 1)
                for t in range(NT + 1):
                    cols = tile_cols(t) if t < NT else slice(0, P)
                    for k in range(KT):
                        m = split_product(bank[:, 5 + t, 0:P], xn_hi[:, k, cols], xn_lo[:, k, cols],
                                          whi[:, k, P:2 * P], wlo[:, k, P:2 * P], k == 0, k == KT - 1)
                m.then_inc(weights_done, 1)
                pe.wait_ge(proj_evicted, 9 * l + 2)
                two_tiles(g0 + 3, 0)
                pe.wait_ge(proj_evicted, 9 * l + 4)
                two_tiles(g0 + 4, 2)

            def attention(l):
                us, u0, p0 = units(l), UNIT0[l], PAIR0[l]
                main0, m0 = 2 * NT * HEADS // 2 * l, MIXED0[l]
                pe.wait_ge(proj_evicted, 9 * l + 9)
                pe.wait_ge(v_evicted, (NT + 1) * (l + 1))
                for step in range(len(us) + 3):
                    if step < len(us):
                        t, j, b = us[step]
                        rows = slice(HD * b, HD * b + HD)
                        n = key_blocks(t)[-1][2]
                        m = P if t < NT else META
                        if step >= 3:
                            pe.wait_ge(masked_ready, u0 + step - 2)
                        pe.matmul(bank[0:m, step % 3, 0:n], q_t[rows, j, tile_cols(t)], k_t[rows, 0:n],
                                  start=True, stop=True).then_inc(scores_ready, 1)
                    u = step - 2
                    if 0 <= u < len(us):
                        t, j, b = us[u]
                        m = P if t < NT else META
                        pe.wait_ge(prob_ready, u0 + u + 1)
                        if u >= 2:
                            pe.wait_ge(prob_t_meta, u0 + u - 1)
                            pe.wait_ge(prob_t_main, main0 + min(u - 1, NT * HEADS))
                        for kt, c0, c1 in key_blocks(t):
                            o = bank[0:c1 - c0, 3 + u % 2, kt * P:kt * P + m]
                            if kt < NT:
                                mm = pe.transpose(o, prob[0:m, u % 3, c0:c1], ident[0:m, 0:m])
                            else:
                                mm = pe.matmul(o, prob[0:m, u % 3, c0:c1], ident[0:m, 0:m],
                                               start=True, stop=True)
                        mm.then_inc(prob_t_psum, 1)
                    u = step - 3
                    if u >= 0:
                        t, j, b = us[u]
                        rows = slice(HD * b, HD * b + HD)
                        m = P if t < NT else META
                        pe.wait_ge(prob_t_meta, u0 + u + 1)
                        pe.wait_ge(prob_t_main, main0 + min(u + 1, NT * HEADS))
                        pair = u // 2
                        if b == 0 and pair >= 2:
                            pe.wait_ge(mix_lo_ready, m0 + pair - 1)
                        blocks = key_blocks(t)
                        for n, (kt, c0, c1) in enumerate(blocks):
                            mm = pe.matmul(bank[rows, 5 + pair % 2, 0:m], v_tok[0:c1 - c0, kt, rows],
                                           prob_t[0:c1 - c0, u % 2, kt, 0:m], start=n == 0,
                                           stop=n == len(blocks) - 1)
                        mm.then_inc(head_out_ready, 1)

            def pool_maps(l):
                pe.wait_ge(pooled_ready, l + 1)
                for g in range(POOL_GROUPS):
                    pe.matmul(bank[:, g, 0:L], pw[:, POOL_GROUPS * l + g, :], pooled[:, g, :],
                              start=True, stop=True).then_inc(pool_out_ready, 1)

            pe.wait_ge(consts_built, CONSTS)
            project(0)
            attention(0)
            pe.wait_ge(consts_loaded, 16 * LOADS)
            pool_maps(0)
            pe.wait_ge(mix_lo_ready, MIXED0[1])
            for gg in range(4):
                whi, wlo = weights(5 + gg, "p (c k m) -> p c k m", c=2, k=KT)
                for c in range(2):
                    for k in range(KT):
                        m = split_product(bank[:, 2 * gg + c, 0:L], whi[:, c, k], wlo[:, c, k],
                                          mix_hi[:, k, :], mix_lo[:, k, :], k == 0, k == KT - 1)
                m.then_inc(weights_done, 1)

            def down(n, a, g):
                whi, wlo = weights(g, "p (d f m) -> p d f m", d=4, f=4)
                pe.wait_ge(ff_lo_ready, 2 * n + 2)
                q = 2 * n + a
                for d in range(4):
                    if q:
                        pe.wait_ge(down_added, 4 * (q - 1) + d + 1)
                    elif d == 3:
                        pe.wait_ge(rms_ready, 3)
                    for f in range(4):
                        slot, c = (2 * n + f // 2) % 4, f % 2
                        m = split_product(bank[:, 4 + d, 0:L], whi[:, d, f], wlo[:, d, f],
                                          ff_hi[:, slot, c, :], ff_lo[:, slot, c, :], f == 0, f == 3)
                    m.then_inc(down_part if d < 3 else weights_done, 1)

            for n in range(STEPS):
                for s in range(2):
                    pair = 2 * n + s
                    if pair:
                        pe.wait_ge(gate_scaled, pair)
                    else:
                        pe.wait_ge(out_added, 2)
                    two_tiles(ffn_gate(n, s), 0, None if pair else 1)
                    if pair:
                        pe.wait_ge(up_scaled, pair)
                    else:
                        square_sum(1)
                    two_tiles(ffn_gate(n, s) + 1, 2)
                if n:
                    down(n - 1, 0, ffn_gate(n, 0) + 4)
                    down(n - 1, 1, ffn_gate(n, 0) + 5)
            down(STEPS - 1, 0, MIX1 - 2)
            down(STEPS - 1, 1, MIX1 - 1)

            project(1)
            attention(1)
            pool_maps(1)
            pe.wait_ge(mix_lo_ready, MIXED0[1] + len(units(1)) // 2 + POOL_GROUPS)
            for n in range(2):
                for kh in range(2):
                    whi, wlo = weights(MIX1 + 5 + 2 * n + kh, "p (k m) -> p k m", k=4)
                    for t in range(NT):
                        for k in range(4):
                            kk = 4 * kh + k
                            m = split_product(bank[:, 2 * n + t, :], mix_hi[:, kk, tile_cols(t)],
                                              mix_lo[:, kk, tile_cols(t)], whi[:, k], wlo[:, k],
                                              kh == 0 and k == 0, False)
                    m.then_inc(weights_done, 1)
                for t in range(NT):
                    for k in range(4):
                        m = pe.matmul(bank[:, 2 * n + t, k * P:(k + 1) * P],
                                      h_t[:, 4 * n + k, tile_cols(t)], ident[:],
                                      start=False, stop=k == 3)
                    m.then_inc(out_tok_psum, 1)

            for kp in range(4):
                pe.wait_ge(h_tok_ready, 2 if kp < 2 else 4)
                for k in range(2):
                    for t in range(NT):
                        m = pe.transpose(bank[:, 4 + kp, (NT * k + t) * P:(NT * k + t + 1) * P],
                                         h_tok[:, t, (2 * kp + k) * P:(2 * kp + k + 1) * P], ident[:])
                m.then_inc(xr_psum, 1)
            pe.wait_ge(xr_ready, 4)
            pe.wait_ge(xr_late_ready, 2)
            for t in range(NT):
                for k in range(KT):
                    m = pe.matmul(bank[:, 0, t * EXPERTS:(t + 1) * EXPERTS], xr[:, k, t * P:(t + 1) * P],
                                  router[:, k, :], start=k == 0, stop=k == KT - 1)
            m.then_inc(logits_psum, 1)
            pe.wait_ge(route_step, CHOSEN)
            pe.matmul(bank[:, 1, 0:8], before[:], chosen[:, 0, :], start=True, stop=True)
            pe.matmul(bank[:, 1, 8:16], before[:], chosen[:, 1, :], start=True, stop=False)
            pe.matmul(bank[:, 1, 8:16], ones[:], chosen[:, 0, :], start=False, stop=True)
            pe.matmul(bank[:, 1, 16:24], ones[:], chosen[:, 0, :], start=True, stop=False)
            pe.matmul(bank[:, 1, 16:24], ones[:], chosen[:, 1, :], start=False,
                      stop=True).then_inc(places_psum, 1)
            pe.wait_ge(route_step, ROUTED)
            end = pe.value_load(rounds[0:1, 0:1], min_val=EXPERTS, max_val=2 * EXPERTS)

            def gather(r):
                pe.wait_ge(pick_ready, NT * r + NT)
                for b in range(2):
                    for k in range(4):
                        cols = slice((4 * b + k) * P, (4 * b + k + 1) * P)
                        for t in range(NT):
                            pe.matmul(bank[:, 5 + b, k * P:(k + 1) * P], n_hi[:, t, cols], pick[:, t, :],
                                      start=t == 0, stop=False)
                            m = pe.matmul(bank[:, 5 + b, k * P:(k + 1) * P], n_lo[:, t, cols],
                                          pick[:, t, :], start=False, stop=t == NT - 1)
                    m.then_inc(gathered_psum, 1)

            def scatter(r):
                for c in range(2):
                    pe.wait_ge(y_lo_ready, 2 * r + c + 3)
                    for t in range(NT):
                        o = bank[:, (5, 6, 7, 2)[2 * c + t], :]
                        pe.matmul(o, pick_t[:, t * P:(t + 1) * P], y_hi[:, c, :], start=True, stop=False)
                        pe.matmul(o, pick_t[:, t * P:(t + 1) * P], y_lo[:, c, :], start=False,
                                  stop=True).then_inc(scattered_psum, 1)

            pe.wait_ge(n_lo_ready, NT)
            gather(0)
            pe.nop().then_inc(ht_psum, 1)
            pe.nop().then_inc(scattered_psum, 4)
            with pe.Fori(0, end) as i:
                def hidden_half(g, b):
                    whi, wlo = weights(MOE + g, "p (k m) -> p k m", i, k=4)
                    half = g % 2
                    if g in (0, 1):
                        pe.wait_ge(xg_lo_ready, 2 * i + g + 1)
                    for k in range(4):
                        kk = 4 * half + k
                        m = split_product(bank[:, b, :], xg_hi[:, kk, :], xg_lo[:, kk, :],
                                          whi[:, k], wlo[:, k], kk == 0, kk == KT - 1)
                    m.then_inc(weights_done, 1)

                def expert_down(n):
                    pe.wait_ge(ht_lo_ready, STEPS * i + n + 1)
                    for a in range(2):
                        whi, wlo = weights(MOE + e_down(n) + a, "p (f m) -> p f m", i, f=2)
                        for f in range(2):
                            ff = 2 * a + f
                            for c in range(2):
                                m = split_product(bank[:, 3 + c, :], ht_hi[:, ff, :], ht_lo[:, ff, :],
                                                  whi[:, f, c * 512:(c + 1) * 512],
                                                  wlo[:, f, c * 512:(c + 1) * 512],
                                                  n == 0 and ff == 0, n == STEPS - 1 and ff == 3)
                        m.then_inc(weights_done, 1)

                def turn_hidden(n):
                    pe.wait_ge(e_h_ready, 1 + STEPS * i + n + 1)
                    for f in range(4):
                        m = pe.transpose(bank[:, 2, f * P:(f + 1) * P], e_h[:, f * P:(f + 1) * P], ident[:])
                    m.then_inc(ht_psum, 1)

                for n in range(STEPS):
                    pe.wait_ge(e_silu_ready, 1 + STEPS * i + n)
                    hidden_half(e_gate(n), 0)
                    hidden_half(e_gate(n) + 1, 0)
                    if n == 0:
                        with pe.If(i > 0):
                            scatter(i - 1)
                        with pe.Else():
                            pe.nop()
                        pe.nop()
                    if n == 1:
                        turn_hidden(0)
                        pe.wait_ge(y_ready, 1 + 2 * i)
                    pe.wait_ge(e_h_ready, 1 + STEPS * i + n)
                    hidden_half(e_gate(n) + 2, 1)
                    hidden_half(e_gate(n) + 3, 1)
                    if n == 0:
                        pe.wait_ge(scatter_added, 5 + 4 * i)
                        pe.wait_ge(gate_col_ready, i + 1)
                        for t in range(NT):
                            pe.transpose(bank[:, 7, t * P:(t + 1) * P], pick[:, t, :].bitcast(F32), ident[:])
                        for t in range(NT):
                            m = pe.matmul(bank[:, 7, 256:257], pick[:, t, :].bitcast(F32),
                                          gate_col[:, t:t + 1], start=t == 0, stop=t == NT - 1)
                        m.then_inc(slots_psum, 1)
                    else:
                        expert_down(n - 1)
                        turn_hidden(n)
                    if n == 3:
                        with pe.If(i < end - 1):
                            gather(i + 1)
                        with pe.Else():
                            pe.nop()
                        pe.nop()
                expert_down(STEPS - 1)
            scatter(end - 1)

        @block.scalar
        def _(act):
            def split(g, i=None):
                act.wait_ge(loaded[g % RAW], 16 * (g // RAW + 1) + (0 if i is None else 16 * (FFN_G // RAW) * i))
                if g >= SPLIT:
                    act.wait_ge(weights_done, g - SPLIT + 1 + (0 if i is None else FFN_G * i))
                act.activation(w_hi[:, g % SPLIT, :], raw[:, g % RAW, :], ACT.Copy).then_inc(hi_ready, 1)

            def gained(v, k):
                act.activation(xn_hi[:, k, :], h_t[:, k, :], ACT.Copy,
                               scale=gain[:, NORM_GAIN[v], k:k + 1]).then_inc(xn_hi_ready, 1)

            def square(b):
                act.activation(sq[:, 4 * b:4 * b + 4, :], h_t[:, 4 * b:4 * b + 4, :],
                               ACT.Square).then_inc(squares_ready, 1)

            def rms_of(v):
                act.wait_ge(square_sum_ready, v + 1)
                act.activation(rms_t[:], bank[:, 7, 0:L], ACT.Sqrt, bias=eps[:],
                               scale=1.0 / D).then_inc(rms_ready, 1)
                if NORM_GAIN[v] < 2:
                    act.activation(rms_v[:], bank[:, 7, L:L + NT + 1], ACT.Sqrt, bias=eps[:],
                                   scale=1.0 / D).then_inc(rms_ready, 1)

            def project(l):
                g0 = MIX1 * l
                rms_of(2 * l)
                for g in range(5):
                    split(g0 + g + AHEAD)
                    if g == 2:
                        act.wait_ge(weights_done, g0 + g + 1)
                        act.wait_ge(rstd_ready, 3 * l + 2)
                        for t in range(NT + 1):
                            m = P if t < NT else META
                            act.activation(v_tok[0:m, t, :], bank[0:m, 5 + t, 0:P], ACT.Copy,
                                           scale=rstd_v[0:m, t:t + 1]).then_inc(v_evicted, 1)

            def attention(l):
                us, u0 = units(l), UNIT0[l]
                for step in range(len(us) + 4):
                    if step < len(us):
                        t, j, b = us[step]
                        m = P if t < NT else META
                        n = key_blocks(t)[-1][2]
                        head = l * HEADS + j + 4 * b
                        c = slice(step, step + 1)
                        act.wait_ge(neg_max_ready, u0 + step + 1)
                        act.activation(prob[0:m, step % 3, 0:n], prob[0:m, step % 3, 0:n], ACT.Exp,
                                       bias=neg_max[0:m, c], accum_out=exp_sum[0:m, c]).then_inc(exp_ready, 1)
                        act.activation(exp_sink[0:m, c], sink[0:m, head:head + 1], ACT.Exp,
                                       bias=neg_max[0:m, c]).then_inc(exp_sink_ready, 1)
                    u = step - 2
                    if 0 <= u < len(us):
                        t, j, b = us[u]
                        m = P if t < NT else META
                        act.wait_ge(prob_t_psum, u0 + u + 1)
                        if u >= 2:
                            act.wait_ge(head_out_ready, u0 + u - 1)
                        if t < NT:
                            act.activation(prob_t[:, u % 2, 0:t + 1, :],
                                           bank[:, 3 + u % 2, 0:(t + 1) * P].rearrange("p (a b) -> p a b", b=P),
                                           ACT.Copy).then_inc(prob_t_main, 1)
                        act.activation(prob_t[0:META, u % 2, NT, 0:m],
                                       bank[0:META, 3 + u % 2, NT * P:NT * P + m],
                                       ACT.Copy).then_inc(prob_t_meta, 1)
                    u = step - 4
                    if u >= 0 and u % 2:
                        t, j, b = us[u]
                        act.wait_ge(head_out_ready, u0 + u + 1)
                        w = P if t < NT else META
                        act.activation(mix_hi[:, j, tile_cols(t)], bank[:, 5 + u // 2 % 2, 0:w],
                                       ACT.Copy).then_inc(mix_hi_ready, 1)
                for g in range(POOL_GROUPS):
                    act.wait_ge(pool_out_ready, POOL_GROUPS * l + g + 1)
                    act.activation(mix_hi[:, 4 + g, :], bank[:, g, 0:L], ACT.Copy,
                                   scale=pscale[:, POOL_GROUPS * l + g:POOL_GROUPS * l + g + 1]
                                   ).then_inc(mix_hi_ready, 1)

            act.wait_ge(gain_loaded, 16)
            for b in range(2):
                act.wait_ge(x_loaded[b], 16)
                for k in range(4 * b, 4 * b + 4):
                    gained(0, k)
                if b == 0:
                    split(0)
            square(0)
            square(1)
            split(1)
            act.wait_ge(consts_built, CONSTS)
            project(0)
            act.wait_ge(consts_loaded, 16 * LOADS)
            attention(0)
            for gg in range(4):
                split(5 + gg + AHEAD)
                for k in (2 * gg, 2 * gg + 1):
                    act.wait_ge(out_added, k + 1)
                    gained(1, k)
                if gg == 1:
                    square(0)
            square(1)
            for n in range(STEPS):
                for s in range(2):
                    pair = 2 * n + s
                    g = ffn_gate(n, s)
                    split(g + AHEAD)
                    if not pair:
                        rms_of(1)
                    act.wait_ge(gate_scaled, pair + 1)
                    act.activation(ff_silu[:], ff_silu[:], ACT.Silu).then_inc(silu_ready, 1)
                    split(g + 1 + AHEAD)
                    act.wait_ge(ff_h_ready, pair + 1)
                    act.activation(ff_hi[:, pair % 4], ff_h[:], ACT.Copy).then_inc(ff_hi_ready, 1)
                if n:
                    split(ffn_gate(n, 0) + 4 + AHEAD)
                    split(ffn_gate(n, 0) + 5 + AHEAD)
            for b in range(2):
                split(MIX1 + b)
                for k in range(4 * b, 4 * b + 4):
                    act.wait_ge(down_added, KT * (STEPS - 1) + k + 1)
                    gained(2, k)
                square(b)
            project(1)
            attention(1)
            for gg in range(4):
                split(MIX1 + 5 + gg + AHEAD)

            def token_squares(n, t, source):
                act.activation(source, h_tok[:, t, 512 * n:512 * n + 512], ACT.Square,
                               accum_out=sums[:, n, t:t + 1]).then_inc(tok_sum_ready, 1)

            def token_rms(first):
                act.wait_ge(total_ready, first + 1)
                act.activation(rms[:], total[:], ACT.Sqrt, bias=eps[:], scale=1.0 / D).then_inc(tok_rms_ready, 1)

            def turned(k):
                act.wait_ge(xr_psum, k // 2 + 1)
                act.activation(xr[:, k, :], bank[:, 4 + k // 2, (k % 2) * SEQ:(k % 2 + 1) * SEQ], ACT.Copy,
                               scale=gain[:, 3, k:k + 1]).then_inc(xr_ready, 1)

            for n in range(2):
                for t in range(NT):
                    act.wait_ge(h_tok_ready, NT * n + t + 1)
                    token_squares(n, t, n_tok[:, t, 512 * n:512 * n + 512])
            token_rms(0)
            for k in range(4):
                turned(k)
            act.wait_ge(tok_rstd_ready, 1)
            for t in range(NT):
                act.activation(n_tok[:, t, :], h_tok[:, t, :], ACT.Copy,
                               scale=rstd2[:, t:t + 1]).then_inc(n_tok_ready, 1)
                if t == 0:
                    act.wait_ge(n_tok_ready, 1)
                    act.activation(n_hi[:, 0, :], n_tok[:, 0, :], ACT.Copy).then_inc(n_hi_ready, 1)
            act.wait_ge(n_tok_ready, 2)
            act.activation(n_hi[:, 1, :], n_tok[:, 1, :], ACT.Copy).then_inc(n_hi_ready, 1)
            act.wait_ge(route_step, GAP)
            act.activation(e2[:], gap[:], ACT.Exp).then_inc(gap_exp_ready, 1)
            act.wait_ge(route_step, ROUTED)
            end = act.value_load(rounds[0:1, 0:1], min_val=EXPERTS, max_val=2 * EXPERTS)

            def gathered_high(b):
                act.activation(xg_hi[:, 4 * b:4 * b + 4, :], xg[:, 4 * b:4 * b + 4, :],
                               ACT.Copy).then_inc(xg_hi_ready, 1)

            for b in range(2):
                act.wait_ge(xg_ready, b + 1)
                gathered_high(b)
            act.nop().then_inc(e_silu_ready, 1)
            act.nop().then_inc(y_ready, 1)
            with act.Fori(0, end) as i:
                def step_of(j):
                    for n in range(STEPS):
                        if j == e_gate(n) + 1:
                            act.wait_ge(weights_done, MOE + j + 1 + FFN_G * i)
                            act.wait_ge(e_h_ready, 1 + STEPS * i + n)
                            act.activation(e_silu[:], bank[:, 0, :], ACT.Silu).then_inc(e_silu_ready, 1)
                        if j == (e_gate(1) + 1 if n == 0 else e_down(n - 1) + 1):
                            act.wait_ge(ht_psum, 1 + STEPS * i + n + 1)
                            act.activation(ht_hi[:], bank[:, 2, :].rearrange("p (f m) -> p f m", f=4),
                                           ACT.Copy).then_inc(ht_hi_ready, 1)
                    if j == 4:
                        act.wait_ge(slots_psum, i + 1)
                        act.activation(pick_t[:], bank[:, 7, 0:SEQ], ACT.Copy).then_inc(slots_ready, 1)
                        act.activation(slot_gate[:], bank[:, 7, SEQ:SEQ + 1], ACT.Copy).then_inc(slots_ready, 1)
                    if j == FFN_G - 4:
                        with act.If(i < end - 1):
                            act.wait_ge(weights_done, MOE + e_gate(STEPS - 1) + 4 + FFN_G * i)
                            act.wait_ge(xg_ready, 2 * i + 4)
                            gathered_high(0)
                            gathered_high(1)
                        with act.Else():
                            act.nop()
                        act.nop()

                for j in range(FFN_G - AHEAD):
                    split(MOE + j + AHEAD, i)
                    step_of(j)
                with act.If(i < end - 1):
                    split(MOE + FFN_G, i)
                    split(MOE + FFN_G + 1, i)
                with act.Else():
                    act.nop()
                act.nop()
                act.wait_ge(weights_done, MOE + FFN_G + FFN_G * i)
                act.wait_ge(slots_ready, 2 * i + 2)
                for c in range(2):
                    act.activation(y[:, c, :], bank[:, 3 + c, :], ACT.Copy, scale=slot_gate[:]).then_inc(y_ready, 1)
                for c in range(2):
                    act.wait_ge(y_ready, 1 + 2 * i + c + 1)
                    act.activation(y_hi[:, c, :], y[:, c, :], ACT.Copy).then_inc(y_hi_ready, 1)

            for n in range(2):
                for t in range(NT):
                    act.wait_ge(scatter_added, 4 * end + NT * n + t + 2)
                    token_squares(n, t, n_tok[:, t, 512 * n:512 * n + 512])
            token_rms(1)

        @block.vector
        def _(dve):
            def split(g, i=None):
                dve.wait_ge(hi_ready, g + 1 + (0 if i is None else FFN_G * i))
                dve.tensor_tensor(w_lo[:, g % SPLIT, :], raw[:, g % RAW, :],
                                  w_hi[:, g % SPLIT, :].bitcast(F32), ALU.subtract).then_inc(lo_ready, 1)

            def gained_rest(v, k):
                dve.wait_ge(xn_hi_ready, KT * v + k + 1)
                dve.scalar_tensor_tensor(xn_lo[:, k, :], h_t[:, k, :], gain[:, NORM_GAIN[v], k:k + 1],
                                         xn_hi[:, k, :].bitcast(F32), ALU.mult,
                                         ALU.subtract).then_inc(xn_lo_ready, 1)

            def add_squares(v):
                dve.wait_ge(squares_ready, 2 * v + 2)
                for s, n in enumerate((4, 2, 1)):
                    if s:
                        dve.wait_ge(square_part, 3 * v + s)
                    dve.tensor_tensor(sq[:, 0:n, :], sq[:, 0:n, :], sq[:, n:2 * n, :],
                                      ALU.add).then_inc(square_part, 1)

            RSTD0 = (0, 2, 3)

            def rstd_of(v):
                r0 = RSTD0[v]
                dve.wait_ge(rms_ready, r0 + 1)
                dve.reciprocal(rstd[:], rms_t[:]).then_inc(rstd_ready, 1)
                if NORM_GAIN[v] < 2:
                    dve.wait_ge(rms_ready, r0 + 2)
                    dve.reciprocal(rstd_v[:], rms_v[:]).then_inc(rstd_ready, 1)
                dve.wait_ge(rstd_ready, r0 + 1)

            def project(l):
                g0 = MIX1 * l
                add_squares(2 * l)
                split(g0 + AHEAD)
                rstd_of(2 * l)
                for g in range(5):
                    if g:
                        split(g0 + g + AHEAD)
                    dve.wait_ge(weights_done, g0 + g + 1)
                    if g < 2:
                        if l and not g:
                            dve.wait_ge(zeros_ready, 3)
                        for c in range(2):
                            dve.tensor_tensor(u_pad[:, 2 * g + c, META:], bank[:, 2 * g + c, 0:L],
                                              rstd[:], ALU.mult).then_inc(proj_evicted, 1)
                    elif g == 2:
                        dve.tensor_tensor(k_t[:], bank[:, 4, 0:L], rstd[:], ALU.mult).then_inc(proj_evicted, 1)
                    else:
                        for c in range(2):
                            j = 2 * (g - 3) + c
                            dve.scalar_tensor_tensor(q_t[:, j, :], bank[:, j, 0:L], HD ** -0.5, rstd[:],
                                                     ALU.mult, ALU.mult).then_inc(proj_evicted, 1)

            def attention(l):
                us, u0, m0 = units(l), UNIT0[l], MIXED0[l]
                for step in range(len(us) + 5):
                    if step < len(us):
                        t, j, b = us[step]
                        m = P if t < NT else META
                        n = key_blocks(t)[-1][2]
                        head = l * HEADS + j + 4 * b
                        c = slice(step, step + 1)
                        dve.wait_ge(scores_ready, u0 + step + 1)
                        if step >= 3:
                            dve.wait_ge(prob_t_psum, u0 + step - 2)
                        dve.tensor_tensor_reduce(prob[0:m, step % 3, 0:n], bank[0:m, step % 3, 0:n],
                                                 mask[0:m, t % NT, 0:n], 1.0, sink[0:m, head:head + 1],
                                                 ALU.add, ALU.max, row_max[0:m, c]).then_inc(masked_ready, 1)
                        dve.wait_ge(masked_ready, u0 + step + 1)
                        dve.tensor_scalar(neg_max[0:m, c], row_max[0:m, c], -1.0, None,
                                          ALU.mult).then_inc(neg_max_ready, 1)
                    u = step - 1
                    if 0 <= u < len(us):
                        t, j, b = us[u]
                        m = P if t < NT else META
                        n = key_blocks(t)[-1][2]
                        c = slice(u, u + 1)
                        dve.wait_ge(exp_ready, u0 + u + 1)
                        dve.wait_ge(exp_sink_ready, u0 + u + 1)
                        dve.tensor_tensor(den[0:m, c], exp_sum[0:m, c], exp_sink[0:m, c],
                                          ALU.add).then_inc(den_ready, 1)
                        dve.wait_ge(den_ready, u0 + u + 1)
                        dve.reciprocal(inv_den[0:m, c], den[0:m, c]).then_inc(inv_den_ready, 1)
                        dve.wait_ge(inv_den_ready, u0 + u + 1)
                        dve.tensor_scalar(prob[0:m, u % 3, 0:n], prob[0:m, u % 3, 0:n], inv_den[0:m, c],
                                          None, ALU.mult).then_inc(prob_ready, 1)
                    u = step - 5
                    if u >= 0 and u % 2:
                        t, j, b = us[u]
                        dve.wait_ge(mix_hi_ready, m0 + u // 2 + 1)
                        w = P if t < NT else META
                        dve.tensor_tensor(mix_lo[:, j, tile_cols(t)], bank[:, 5 + u // 2 % 2, 0:w],
                                          mix_hi[:, j, tile_cols(t)].bitcast(F32),
                                          ALU.subtract).then_inc(mix_lo_ready, 1)
                u = len(us) - 1
                t, j, b = us[u]
                w = P if t < NT else META
                for g in range(POOL_GROUPS):
                    dve.wait_ge(mix_hi_ready, m0 + len(us) // 2 + g + 1)
                    dve.scalar_tensor_tensor(mix_lo[:, 4 + g, :], bank[:, g, 0:L],
                                             pscale[:, POOL_GROUPS * l + g:POOL_GROUPS * l + g + 1],
                                             mix_hi[:, 4 + g, :].bitcast(F32), ALU.mult,
                                             ALU.subtract).then_inc(mix_lo_ready, 1)

            dve.wait_ge(consts_built, CONSTS)
            dve.reciprocal(inv_count[:], head_count[:]).then_inc(inv_count_ready, 1)
            dve.wait_ge(gain_loaded, 16)
            for b in range(2):
                for k in range(4 * b, 4 * b + 4):
                    gained_rest(0, k)
                if b == 0:
                    split(0)
            split(1)
            project(0)
            dve.wait_ge(consts_loaded, 16 * LOADS)
            attention(0)
            for gg in range(4):
                split(5 + gg + AHEAD)
                dve.wait_ge(weights_done, 5 + gg + 1)
                for c in range(2):
                    dt = 2 * gg + c
                    dve.tensor_tensor(h_t[:, dt, :], h_t[:, dt, :], bank[:, dt, 0:L],
                                      ALU.add).then_inc(out_added, 1)
                if gg:
                    gained_rest(1, 2 * gg - 2)
                    gained_rest(1, 2 * gg - 1)
            gained_rest(1, 6)
            gained_rest(1, 7)
            add_squares(1)

            def add_down(q, g):
                for d in range(4):
                    if d < 3:
                        dve.wait_ge(down_part, 3 * q + d + 1)
                    else:
                        dve.wait_ge(weights_done, g + 1)
                    if q >= 2:
                        dve.wait_ge(down_added, 4 * (q - 2) + d + 1)
                    dt = 4 * (q % 2) + d
                    dve.tensor_tensor(h_t[:, dt, :], h_t[:, dt, :], bank[:, 4 + d, 0:L],
                                      ALU.add).then_inc(down_added, 1)

            def hidden_rest(pair):
                dve.wait_ge(ff_hi_ready, pair + 1)
                dve.tensor_tensor(ff_lo[:, pair % 4], ff_h[:], ff_hi[:, pair % 4].bitcast(F32),
                                  ALU.subtract).then_inc(ff_lo_ready, 1)

            for n in range(STEPS):
                for s in range(2):
                    pair = 2 * n + s
                    g = ffn_gate(n, s)
                    split(g + AHEAD)
                    if s:
                        hidden_rest(pair - 1)
                    if not pair:
                        rstd_of(1)
                    both = rstd[:].unsqueeze(1).to_broadcast([P, 2, L])
                    dve.wait_ge(weights_done, g + 1)
                    if pair:
                        dve.wait_ge(ff_h_ready, pair)
                    dve.tensor_tensor(ff_silu[:], bank[:, 0:2, 0:L], both, ALU.mult).then_inc(gate_scaled, 1)
                    split(g + 1 + AHEAD)
                    dve.wait_ge(weights_done, g + 2)
                    if pair:
                        dve.wait_ge(ff_lo_ready, pair)
                    dve.tensor_tensor(ff_h[:], bank[:, 2:4, 0:L], both, ALU.mult).then_inc(up_scaled, 1)
                    dve.wait_ge(up_scaled, pair + 1)
                    dve.wait_ge(silu_ready, pair + 1)
                    dve.tensor_tensor(ff_h[:], ff_silu[:], ff_h[:], ALU.mult).then_inc(ff_h_ready, 1)
                if n:
                    split(ffn_gate(n, 0) + 4 + AHEAD)
                    hidden_rest(2 * n + 1)
                    add_down(2 * n - 2, ffn_gate(n, 0) + 4)
                    split(ffn_gate(n, 0) + 5 + AHEAD)
                    add_down(2 * n - 1, ffn_gate(n, 0) + 5)
                else:
                    hidden_rest(1)
            split(MIX1)
            add_down(2 * STEPS - 2, MIX1 - 2)
            for k in range(4):
                gained_rest(2, k)
            split(MIX1 + 1)
            add_down(2 * STEPS - 1, MIX1 - 1)
            for k in range(4, KT):
                gained_rest(2, k)

            project(1)
            attention(1)
            for gg in range(4):
                split(MIX1 + 5 + gg + AHEAD)
            for n in range(2):
                for t in range(NT):
                    dve.wait_ge(out_tok_psum, 2 * n + t + 1)
                    dve.tensor_copy(h_tok[:, t, 512 * n:512 * n + 512], bank[:, 2 * n + t, :]
                                    ).then_inc(h_tok_ready, 1)

            def token_rstd(first):
                dve.wait_ge(tok_sum_ready, 4 * first + 4)
                dve.tensor_tensor(total[:], sums[:, 0, :], sums[:, 1, :], ALU.add).then_inc(total_ready, 1)
                dve.wait_ge(tok_rms_ready, first + 1)
                dve.reciprocal(rstd2[:], rms[:]).then_inc(tok_rstd_ready, 1)
                dve.wait_ge(tok_rstd_ready, first + 1)

            for kp in (2, 3):
                dve.wait_ge(xr_psum, kp + 1)
                dve.tensor_tensor(xr[:, 2 * kp:2 * kp + 2, :],
                                  bank[:, 4 + kp, :].rearrange("p (k m) -> p k m", k=2),
                                  gain[:, 3, 2 * kp:2 * kp + 2].unsqueeze(2).to_broadcast([P, 2, SEQ]),
                                  ALU.mult).then_inc(xr_late_ready, 1)
            token_rstd(0)

            def wide(a):
                return a.to_broadcast([P, NT, EXPERTS])

            def by_token(a, first):
                return a[:, first:first + EXPERTS, :].rearrange("p e t -> p t e")

            dve.wait_ge(logits_psum, 1)
            for t in range(NT):
                dve.tensor_scalar(lg[:, t, :], bank[:, 0, t * EXPERTS:(t + 1) * EXPERTS], rstd2[:, t:t + 1],
                                  None, ALU.mult).then_inc(route_step, 1)
            for t in range(NT):
                dve.wait_ge(route_step, t + 1)
                dve.max(top[:, t, :], lg[:, t, :]).then_inc(route_step, 1)
            dve.wait_ge(route_step, 4)
            dve.tensor_tensor(gap[:], top[:, :, 1], top[:, :, 0], ALU.subtract).then_inc(route_step, 1)
            for t in range(NT):
                dve.max_index(top_at[:, t, :], top[:, t, :], lg[:, t, :]).then_inc(route_step, 1)
            dve.wait_ge(route_step, 7)
            dve.tensor_copy(top_no[:], top_at[:, :, 0:2]).then_inc(route_step, 1)
            dve.wait_ge(route_step, 8)
            dve.tensor_tensor(oh1[:], expert_no[:], wide(top_no[:, :, 0:1]), ALU.is_equal).then_inc(route_step, 1)
            dve.tensor_tensor(oh2[:], expert_no[:], wide(top_no[:, :, 1:2]), ALU.is_equal).then_inc(route_step, 1)
            dve.wait_ge(route_step, 10)
            dve.tensor_tensor(chosen[:], oh1[:], oh2[:], ALU.add).then_inc(route_step, 1)
            dve.wait_ge(places_psum, 1)
            dve.wait_ge(route_step, CHOSEN)
            dve.scalar_tensor_tensor(posa[:], bank[:, 1, 0:16].rearrange("p (t e) -> p t e", t=NT), 1000.0,
                                     chosen[:], ALU.add, ALU.mult).then_inc(route_step, 1)
            dve.tensor_reduce(most[:], bank[:, 1, 16:24], AXX, ALU.max).then_inc(route_step, 1)
            dve.wait_ge(route_step, 12)
            for q in range(2):
                dve.tensor_scalar(by_token(place, EXPERTS * q), posa[:], -1000.0 - P * q, None,
                                  ALU.add).then_inc(route_step, 1)
            dve.wait_ge(route_step, 13)
            dve.tensor_scalar(rounds_f[:], most[:], float(P), float(EXPERTS), ALU.is_gt,
                              ALU.mult).then_inc(route_step, 1)
            dve.wait_ge(route_step, 16)
            dve.tensor_scalar(rounds[:], rounds_f[:], float(EXPERTS), None, ALU.add).then_inc(route_step, 1)

            def choose(r):
                for t in range(NT):
                    dve.tensor_scalar(pick[:, t, :], slot_no[:], place[:, bass.ds(r, 1), t], None,
                                      ALU.is_equal).then_inc(pick_ready, 1)

            def gates_of(r):
                dve.tensor_copy(gate_col[:], gates[:, bass.ds(r, 1), :].rearrange("p a t -> p (a t)")
                                ).then_inc(gate_col_ready, 1)

            def gained(r, k0):
                for b in range(2):
                    dve.wait_ge(gathered_psum, k0 + b)
                    dve.tensor_tensor(xg[:, 4 * b:4 * b + 4, :],
                                      bank[:, 5 + b, :].rearrange("p (k m) -> p k m", k=4),
                                      gain[:, 3, 4 * b:4 * b + 4].unsqueeze(2).to_broadcast([P, 4, P]),
                                      ALU.mult).then_inc(xg_ready, 1)

            def gathered_rest(r, b):
                dve.wait_ge(xg_hi_ready, 2 * r + b + 1)
                dve.tensor_tensor(xg_lo[:, 4 * b:4 * b + 4, :], xg[:, 4 * b:4 * b + 4, :],
                                  xg_hi[:, 4 * b:4 * b + 4, :].bitcast(F32),
                                  ALU.subtract).then_inc(xg_lo_ready, 1)

            dve.wait_ge(route_step, 15)
            choose(0)
            for t in range(NT):
                dve.wait_ge(n_hi_ready, t + 1)
                dve.tensor_tensor(n_lo[:, t, :], n_tok[:, t, :], n_hi[:, t, :].bitcast(F32),
                                  ALU.subtract).then_inc(n_lo_ready, 1)
            dve.wait_ge(gap_exp_ready, 1)
            dve.tensor_scalar(den2[:], e2[:], 1.0, None, ALU.add).then_inc(route_step, 1)
            dve.wait_ge(route_step, ROUTED + 1)
            dve.reciprocal(g1[:], den2[:]).then_inc(route_step, 1)
            dve.wait_ge(route_step, ROUTED + 2)
            dve.tensor_tensor(g2[:], e2[:], g1[:], ALU.mult).then_inc(route_step, 1)
            dve.tensor_tensor(ga[:], oh1[:], wide(g1[:].unsqueeze(2)), ALU.mult).then_inc(route_step, 1)
            dve.wait_ge(route_step, ROUTED + 3)
            dve.tensor_tensor(gb[:], oh2[:], wide(g2[:].unsqueeze(2)), ALU.mult).then_inc(route_step, 1)
            dve.wait_ge(route_step, ROUTED + 5)
            for q in range(2):
                dve.tensor_tensor(by_token(gates, EXPERTS * q), ga[:], gb[:], ALU.add).then_inc(route_step, 1)
            gained(0, 1)
            dve.wait_ge(route_step, GATED)
            gates_of(0)
            end = dve.value_load(rounds[0:1, 0:1], min_val=EXPERTS, max_val=2 * EXPERTS)
            gathered_rest(0, 0)
            gathered_rest(0, 1)
            dve.nop().then_inc(e_h_ready, 1)
            dve.nop().then_inc(scatter_added, 5)
            dve.nop().then_inc(y_lo_ready, 2)
            def add_round(r):
                dve.wait_ge(scatter_added, 4 * r + 5)
                for c in range(2):
                    for t in range(NT):
                        dve.wait_ge(scattered_psum, 4 * r + 2 * c + t + 5)
                        dve.tensor_tensor(h_tok[:, t, 512 * c:512 * c + 512], h_tok[:, t, 512 * c:512 * c + 512],
                                          bank[:, (5, 6, 7, 2)[2 * c + t], :], ALU.add).then_inc(scatter_added, 1)

            with dve.Fori(0, end) as i:
                def step_of(j):
                    if j == 1:
                        with dve.If(i > 0):
                            add_round(i - 1)
                        with dve.Else():
                            dve.nop()
                        dve.nop()
                    for n in range(STEPS):
                        if j == e_gate(n) + 3:
                            dve.wait_ge(weights_done, MOE + j + 1 + FFN_G * i)
                            dve.wait_ge(e_silu_ready, 1 + STEPS * i + n + 1)
                            dve.wait_ge(ht_psum, 1 + STEPS * i + n)
                            dve.tensor_tensor(e_h[:], e_silu[:], bank[:, 1, :], ALU.mult).then_inc(e_h_ready, 1)
                        if j == (e_gate(1) + 1 if n == 0 else e_down(n - 1) + 1):
                            dve.wait_ge(ht_hi_ready, STEPS * i + n + 1)
                            dve.tensor_tensor(ht_lo[:], bank[:, 2, :].rearrange("p (f m) -> p f m", f=4),
                                              ht_hi[:].bitcast(F32), ALU.subtract).then_inc(ht_lo_ready, 1)
                    if j == 12:
                        with dve.If(i < end - 1):
                            dve.wait_ge(slots_psum, i + 1)
                            choose(i + 1)
                            gates_of(i + 1)
                        with dve.Else():
                            dve.nop()
                        dve.nop()
                    if j == e_down(3) - 4:
                        with dve.If(i < end - 1):
                            gained(i + 1, 2 * i + 3)
                        with dve.Else():
                            dve.nop()
                        dve.nop()
                    if j == FFN_G - 3:
                        with dve.If(i < end - 1):
                            gathered_rest(i + 1, 0)
                            gathered_rest(i + 1, 1)
                        with dve.Else():
                            dve.nop()
                        dve.nop()

                for j in range(FFN_G - AHEAD):
                    split(MOE + j + AHEAD, i)
                    step_of(j)
                with dve.If(i < end - 1):
                    split(MOE + FFN_G, i)
                    split(MOE + FFN_G + 1, i)
                with dve.Else():
                    dve.nop()
                dve.nop()
                for c in range(2):
                    dve.wait_ge(y_hi_ready, 2 * i + c + 1)
                    dve.tensor_tensor(y_lo[:, c, :], y[:, c, :], y_hi[:, c, :].bitcast(F32),
                                      ALU.subtract).then_inc(y_lo_ready, 1)
            add_round(end - 1)

            token_rstd(1)
            for t in range(NT):
                dve.scalar_tensor_tensor(n_tok[:, t, :], h_tok[:, t, :], rstd2[:, t:t + 1], g_final[:],
                                         ALU.mult, ALU.mult).then_inc(out_ready, 1)


def kernel(x, meta_tokens, norm_mix_g, w_in, attn_sinks, pool_w, pool_scale, w_out, norm_ffn_g,
           dense_w_gate, dense_w_up, dense_w_down, moe_w_router, moe_w_gate, moe_w_up, moe_w_down,
           final_norm_g):
    import numpy as np
    import concourse.bacc as bacc
    from concourse.bass_utils import run_bass_kernel_spmd

    (x, meta_tokens, norm_mix_g, w_in, attn_sinks, pool_w, pool_scale, w_out, norm_ffn_g, dense_w_gate,
     dense_w_up, dense_w_down, moe_w_router, moe_w_gate, moe_w_up, moe_w_down, final_norm_g) = (
        np.asarray(a) for a in (
            x, meta_tokens, norm_mix_g, w_in, attn_sinks, pool_w, pool_scale, w_out, norm_ffn_g,
            dense_w_gate, dense_w_up, dense_w_down, moe_w_router, moe_w_gate, moe_w_up, moe_w_down,
            final_norm_g))

    h0 = np.concatenate([meta_tokens, x[0]], axis=0)
    x_t = np.ascontiguousarray(h0.T.reshape(KT, P, L).transpose(1, 0, 2))
    gains = np.ascontiguousarray(
        np.concatenate([norm_mix_g, norm_ffn_g], axis=0).reshape(4, KT, P).transpose(2, 0, 1))
    sinks = np.ascontiguousarray(attn_sinks.reshape(-1))
    pw = np.ascontiguousarray(pool_w.reshape(2 * POOL_GROUPS, P, P).transpose(1, 0, 2))
    pscale = np.ascontiguousarray(pool_scale.reshape(2 * POOL_GROUPS, P).T)
    router = np.ascontiguousarray(moe_w_router[0].reshape(KT, P, EXPERTS).transpose(1, 0, 2))

    heads = [h for j in range(HEADS // 2) for h in (j, j + HEADS // 2)]
    qcols = np.concatenate([np.arange(HD * h, HD * h + HD) for h in heads])
    d_attn = HEADS * HD

    def col_tiles(w):
        n = w.shape[1] // (2 * P)
        return w.reshape(KT, P, n, 2, P).transpose(2, 1, 3, 0, 4).reshape(n, P, GW)

    w_mix = np.empty((2, MIX_G, P, GW), w_in.dtype)
    for l in range(2):
        w_mix[l, 0:2] = col_tiles(w_in[l][:, d_attn + 2 * P:])
        w_mix[l, 2] = w_in[l][:, d_attn:d_attn + 2 * P].reshape(KT, P, 2 * P).transpose(1, 0, 2).reshape(P, GW)
        w_mix[l, 3:5] = col_tiles(w_in[l][:, qcols])
        wo = np.concatenate([w_out[l][qcols], w_out[l][d_attn:]], axis=0)
        if l == 0:
            w_mix[l, 5:9] = col_tiles(wo)
        else:
            w_mix[l, 5:9] = wo.reshape(2, 4, P, 2, 512).transpose(3, 0, 2, 1, 4).reshape(4, P, GW)

    w_ffn = np.empty((FFN_G, P, GW), dense_w_gate.dtype)
    gate, up = col_tiles(dense_w_gate[0]), col_tiles(dense_w_up[0])
    down = dense_w_down[0].reshape(STEPS, 4, P, 2, 4, P).transpose(0, 3, 2, 4, 1, 5).reshape(STEPS, 2, P, GW)
    for n in range(STEPS):
        g = 0 if n == 0 else 4 + 6 * (n - 1)
        for s in range(2):
            w_ffn[g + 2 * s] = gate[2 * n + s]
            w_ffn[g + 2 * s + 1] = up[2 * n + s]
        d = 8 + 6 * n if n < STEPS - 1 else FFN_G - 2
        w_ffn[d:d + 2] = down[n]

    w_moe = np.empty((EXPERTS, FFN_G, P, GW), moe_w_gate.dtype)
    gate, up = (w[0].reshape(EXPERTS, 2, 4, P, STEPS, 512).transpose(0, 4, 1, 3, 2, 5).reshape(
        EXPERTS, STEPS, 2, P, GW) for w in (moe_w_gate, moe_w_up))
    down = moe_w_down[0].reshape(EXPERTS, STEPS, 2, 2, P, D).transpose(0, 1, 2, 4, 3, 5).reshape(
        EXPERTS, STEPS, 2, P, GW)
    for n in range(STEPS):
        g = 0 if n == 0 else 4 + 6 * (n - 1)
        w_moe[:, g:g + 2] = gate[:, n]
        w_moe[:, g + 2:g + 4] = up[:, n]
        d = 8 + 6 * n if n < STEPS - 1 else FFN_G - 2
        w_moe[:, d:d + 2] = down[:, n]

    arrays = {
        "x_t": x_t, "gains": gains, "sinks": sinks, "pool_w": pw, "pool_scale": pscale,
        "final_g": np.ascontiguousarray(final_norm_g), "w_router": router, "w_mix": w_mix,
        "w_ffn": w_ffn, "w_moe": w_moe,
    }
    nc = bacc.Bacc("TRN2", target_bir_lowering=False, num_devices=1)
    args = [nc.dram_tensor(n, a.shape, mybir.dt.from_np(a.dtype), kind="ExternalInput").ap()
            for n, a in arrays.items()]
    out = nc.dram_tensor("out", (SEQ, D), F32, kind="ExternalOutput").ap()
    build(nc, *args, out)
    r = run_bass_kernel_spmd(nc, [arrays], core_ids=[0])
    return r.results[0]["out"].reshape(1, SEQ, D)
```

```python
from contextlib import ExitStack

import concourse.bass as bass
from concourse import mybir

F32 = mybir.dt.float32
F32R = mybir.dt.float32r
I32 = mybir.dt.int32
U32 = mybir.dt.uint32
ALU = mybir.AluOpType
ACT = mybir.ActivationFunctionType
AXX = mybir.AxisListType.X

P = 128
D = 1024
KT = D // P
META, SEQ, CHUNK = 16, 256, 64
L = META + SEQ
NT = SEQ // P
HEADS, HD = 8, 64
POOL_GROUPS = 4
FF = 3584
STEPS = FF // 512
EXPERTS = 8
EPS = 1e-5
NEG = -1e30

GW = 2048
RAW = 7
SPLIT = 3
MIX_G = 9
FFN_G = 6 * STEPS
FFN0 = MIX_G
MIX1 = MIX_G + FFN_G
MOE = MIX1 + MIX_G
LOADS = 5
CONSTS = 20
WINDOW_STEPS = 12
GAP, CHOSEN, ROUTED = 5, 11, 17
GATED = 24
AHEAD = 2


def build(nc, x_t, gains, sinks, pool_w, pool_scale, final_g, w_router, w_mix, w_ffn, w_moe, out):
    with ExitStack() as ctx:
        def sb(name, shape, dt=F32):
            return ctx.enter_context(nc.sbuf_tensor(name, shape, dt))

        def sem(name):
            return ctx.enter_context(nc.semaphore(name))

        bank = ctx.enter_context(nc.psum_tensor("bank", [P, 8, 512], F32))

        raw = sb("raw", [P, RAW, GW])
        w_hi = sb("w_hi", [P, SPLIT, GW], F32R)
        w_lo = sb("w_lo", [P, SPLIT, GW], F32R)
        h_t = sb("h_t", [P, KT, L])
        gain = sb("gain", [P, 4, KT])
        sink = sb("sink", [P, 2 * HEADS])
        neg_sink = sb("neg_sink", [P, 2 * HEADS])
        warm = sb("warm", [P, 5])
        pw = sb("pw", [P, 2 * POOL_GROUPS, P])
        pscale = sb("pscale", [P, 2 * POOL_GROUPS])
        router = sb("router", [P, KT, EXPERTS])
        g_final = sb("g_final", [P, D])
        eps = sb("eps", [P, 1])
        ones = sb("ones", [P, P])
        ident = sb("ident", [P, P])
        before = sb("before", [P, P])
        slot_no = sb("slot_no", [P, P])
        expert_no = sb("expert_no", [P, NT, EXPERTS])
        mask = sb("mask", [P, NT, L])
        head_count = sb("head_count", [P, POOL_GROUPS, META])
        inv_count = sb("inv_count", [P, POOL_GROUPS, META])
        sums = sb("sums", [P, 2, NT])
        total = sb("total", [P, NT])
        rms = sb("rms", [P, 2])
        rstd2 = sb("rstd2", [P, 2])
        rstd = sb("rstd", [P, L])
        rms_t = sb("rms_t", [P, L])

        with ExitStack() as r1:
            sq, xn_hi, xn_lo = (r1.enter_context(nc.sbuf_tensor(n, [P, KT, L], t))
                                for n, t in (("sq", F32), ("xn_hi", F32R), ("xn_lo", F32R)))
        with ExitStack() as r1:
            h_tok, n_tok, x_tok = (r1.enter_context(nc.sbuf_tensor(n, [P, NT, D], F32))
                                   for n in ("h_tok", "n_tok", "x_tok"))
        sb("region1", [P, 3 * KT * L])

        with ExitStack() as r2:
            def r(name, shape, dt=F32):
                return r2.enter_context(nc.sbuf_tensor(name, shape, dt))
            mix_hi = r("mix_hi", [P, KT, L], F32R)
            mix_lo = r("mix_lo", [P, KT, L], F32R)
            u_pad = r("u_pad", [P, POOL_GROUPS, META + L])
            win_a = r("win_a", [P, POOL_GROUPS, META + L])
            win_b = r("win_b", [P, POOL_GROUPS, META + L])
            pooled = r("pooled", [P, POOL_GROUPS, L])
            q_t = r("q_t", [P, HEADS // 2, L])
            k_t = r("k_t", [P, L])
            v_t = r("v_t", [P, L])
            v_tok = r("v_tok", [P, NT + 1, P])
            prob = r("prob", [P, 3, L])
            prob_t = r("prob_t", [P, 2, NT + 1, P])
            o_tok = r("o_tok", [P, 2, P])
            neg_max = r("neg_max", [P, 24])
            exp_sum = r("exp_sum", [P, 24])
            exp_sink = r("exp_sink", [P, 24])
            den = r("den", [P, 24])
            inv_den = r("inv_den", [P, 24])
        with ExitStack() as r2:
            ff_hi = r2.enter_context(nc.sbuf_tensor("ff_hi", [P, 4, 2, L], F32R))
            ff_lo = r2.enter_context(nc.sbuf_tensor("ff_lo", [P, 4, 2, L], F32R))
            ff_silu = r2.enter_context(nc.sbuf_tensor("ff_silu", [P, 2, L], F32))
            ff_h = r2.enter_context(nc.sbuf_tensor("ff_h", [P, 2, L], F32))
        with ExitStack() as r2:
            def r(name, shape, dt=F32):
                return r2.enter_context(nc.sbuf_tensor(name, shape, dt))
            xg = r("xg", [P, KT, P])
            xg_hi = r("xg_hi", [P, KT, P], F32R)
            xg_lo = r("xg_lo", [P, KT, P], F32R)
            pick = r("pick", [P, NT, P])
            pick_t = r("pick_t", [P, NT * P], F32R)
            gate_col = r("gate_col", [P, NT])
            slot_gate = r("slot_gate", [P, 1])
            slot_rstd = r("slot_rstd", [P, 1])
            e_silu = r("e_silu", [P, 512])
            e_h = r("e_h", [P, 512])
            xr = r("xr", [P, KT, SEQ])
            ht_hi = r("ht_hi", [P, 2, 4, P], F32R)
            ht_lo = r("ht_lo", [P, 2, 4, P], F32R)
            y = r("y", [P, 2, 512])
            y_hi = r("y_hi", [P, 2, 512], F32R)
            y_lo = r("y_lo", [P, 2, 512], F32R)
            lg, top, oh1, oh2, ga, gb, chosen, posa = (
                r(n, [P, NT, EXPERTS]) for n in
                ("lg", "top", "oh1", "oh2", "ga", "gb", "chosen", "posa"))
            top_at = r("top_at", [P, NT, EXPERTS], U32)
            top_no = r("top_no", [P, NT, 2])
            gap, e2, den2, g1, g2 = (r(n, [P, NT]) for n in ("gap", "e2", "den2", "g1", "g2"))
            gates = r("gates", [P, 2 * EXPERTS + 1, NT])
            place = r("place", [P, 2 * EXPERTS + 1, NT])
            most = r("most", [P, 1])
            rounds_f = r("rounds_f", [P, 1])
            rounds = r("rounds", [P, 1], I32)

        x_loaded = [sem("x_loaded0"), sem("x_loaded1")]
        consts_loaded = sem("consts_loaded")
        loaded = [sem(f"loaded{s}") for s in range(RAW)]
        consts_built = sem("consts_built")
        hi_ready = sem("hi_ready")
        lo_ready = sem("lo_ready")
        weights_done = sem("weights_done")
        squares_ready = sem("squares_ready")
        square_sum_ready = sem("square_sum_ready")
        rms_ready = sem("rms_ready")
        rstd_ready = sem("rstd_ready")
        square_part = sem("square_part")
        v_turned = sem("v_turned")
        v_evicted = sem("v_evicted")
        gate_scaled = sem("gate_scaled")
        up_scaled = sem("up_scaled")
        total_ready = sem("total_ready")
        gain_loaded = sem("gain_loaded")
        xn_hi_ready = sem("xn_hi_ready")
        xn_lo_ready = sem("xn_lo_ready")
        proj_evicted = sem("proj_evicted")
        window_step = sem("window_step")
        inv_count_ready = sem("inv_count_ready")
        zeros_ready = sem("zeros_ready")
        pooled_ready = sem("pooled_ready")
        scores_ready = sem("scores_ready")
        masked_ready = sem("masked_ready")
        neg_sink_ready = sem("neg_sink_ready")
        exp_ready = sem("exp_ready")
        exp_sink_ready = sem("exp_sink_ready")
        den_ready = sem("den_ready")
        inv_den_ready = sem("inv_den_ready")
        prob_t_psum = sem("prob_t_psum")
        prob_t_ready = [sem("prob_t_even"), sem("prob_t_odd")]
        head_norm_ready = sem("head_norm_ready")
        pair_turned = sem("pair_turned")
        pool_hi_ready = sem("pool_hi_ready")
        pool_lo_ready = sem("pool_lo_ready")
        head_out_ready = sem("head_out_ready")
        pool_out_ready = sem("pool_out_ready")
        mix_hi_ready = sem("mix_hi_ready")
        mix_lo_ready = sem("mix_lo_ready")
        out_added = sem("out_added")
        silu_ready = sem("silu_ready")
        ff_h_ready = sem("ff_h_ready")
        ff_hi_ready = sem("ff_hi_ready")
        ff_lo_ready = sem("ff_lo_ready")
        down_part = sem("down_part")
        down_added = sem("down_added")
        out_tok_psum = sem("out_tok_psum")
        h_tok_ready = sem("h_tok_ready")
        tok_sum_ready = sem("tok_sum_ready")
        tok_rms_ready = sem("tok_rms_ready")
        tok_rstd_ready = sem("tok_rstd_ready")
        x_tok_ready = sem("x_tok_ready")
        xr_psum = sem("xr_psum")
        xr_ready = sem("xr_ready")
        xr_late_ready = sem("xr_late_ready")
        logits_psum = sem("logits_psum")
        route_step = sem("route_step")
        gap_exp_ready = sem("gap_exp_ready")
        places_psum = sem("places_psum")
        pick_ready = sem("pick_ready")
        gate_col_ready = sem("gate_col_ready")
        slots_psum = sem("slots_psum")
        slots_ready = sem("slots_ready")
        slot_rstd_ready = sem("slot_rstd_ready")
        gathered_psum = sem("gathered_psum")
        xg_ready = sem("xg_ready")
        xg_hi_ready = sem("xg_hi_ready")
        xg_lo_ready = sem("xg_lo_ready")
        e_silu_ready = sem("e_silu_ready")
        e_h_ready = sem("e_h_ready")
        ht_psum = sem("ht_psum")
        ht_hi_ready = sem("ht_hi_ready")
        ht_lo_ready = sem("ht_lo_ready")
        y_ready = sem("y_ready")
        y_hi_ready = sem("y_hi_ready")
        y_lo_ready = sem("y_lo_ready")
        scattered_psum = sem("scattered_psum")
        scatter_added = sem("scatter_added")
        out_ready = sem("out_ready")
        stored = sem("stored")

        NORM_GAIN = (0, 2, 1)

        def tile_cols(t):
            return slice(META + t * P, META + (t + 1) * P) if t < NT else slice(0, META)

        def key_blocks(t):
            blocks = [(NT, 0, META)]
            if t < NT:
                blocks += [(kt, META + kt * P, META + (kt + 1) * P) for kt in range(t + 1)]
            return blocks

        def units(l):
            return [(t, j, b) for j in range(HEADS // 2) for t in range(NT + 1 - l) for b in range(2)]

        UNIT0 = (0, len(units(0)))
        PAIR0 = (0, len(units(0)) // 2)

        def wait_rest(engine, g, i=None):
            engine.wait_ge(lo_ready, g + 1 + (0 if i is None else FFN_G * i))

        def ffn_gate(n, s):
            return FFN0 + (2 * s if n == 0 else 4 + 6 * (n - 1) + 3 * s)

        def e_gate(n):
            return 0 if n == 0 else 4 + 6 * (n - 1)

        def e_down(n):
            return 8 + 6 * n if n < STEPS - 1 else FFN_G - 2

        def e_turned(n):
            return (e_gate(1) + 1, *(e_down(m) + 1 for m in range(STEPS - 2)), e_down(STEPS - 2))[n]

        def copy_turned(u, t, copy):
            m = P if t < NT else META
            if t < NT:
                copy(prob_t[:, u % 2, 0:t + 1, :],
                     bank[:, 3 + u % 2, 0:(t + 1) * P].rearrange("p (a b) -> p a b", b=P))
            return copy(prob_t[0:META, u % 2, NT, 0:m], bank[0:META, 3 + u % 2, NT * P:NT * P + m])

        block = ctx.enter_context(nc.Block())

        @block.sync
        def _(sp):
            def load(g, src, i=None):
                if g >= RAW or i is not None:
                    wait_rest(sp, g - RAW, i)
                sp.dma_start(raw[:, g % RAW, :], src).then_inc(loaded[g % RAW], 16)

            sp.dma_start(gain[:], gains).then_inc(gain_loaded, 16)
            for b in range(2):
                sp.dma_start(h_t[:, 4 * b:4 * b + 4, :], x_t[:, 4 * b:4 * b + 4, :]).then_inc(x_loaded[b], 16)
            load(0, w_mix[0, 0])
            load(1, w_mix[0, 1])
            sp.dma_start(sink[:], sinks.partition_broadcast(P)).then_inc(consts_loaded, 16)
            load(2, w_mix[0, 2])
            sp.dma_start(pw[:], pool_w).then_inc(consts_loaded, 16)
            sp.dma_start(pscale[:], pool_scale).then_inc(consts_loaded, 16)
            sp.dma_start(router[:], w_router).then_inc(consts_loaded, 16)
            sp.dma_start(g_final[:], final_g.partition_broadcast(P)).then_inc(consts_loaded, 16)
            for g in range(3, MIX_G):
                load(g, w_mix[0, g])
            for g in range(FFN_G):
                load(FFN0 + g, w_ffn[g])
            for g in range(MIX_G):
                load(MIX1 + g, w_mix[1, g])
            for g in range(RAW):
                load(MOE + g, w_moe[0, g])
            sp.wait_ge(route_step, ROUTED)
            end = sp.value_load(rounds[0:1, 0:1], min_val=EXPERTS, max_val=2 * EXPERTS)
            with sp.Fori(0, end) as i:
                this = sp.snap(i % EXPERTS)
                for g in range(RAW, FFN_G):
                    load(MOE + g, w_moe[this, g], i)
                following = sp.snap((i + 1) % EXPERTS)
                with sp.If(i < end - 1):
                    for g in range(RAW):
                        load(MOE + FFN_G + g, w_moe[following, g], i)
                with sp.Else():
                    sp.nop()
                sp.nop()
            for t in range(NT):
                sp.wait_ge(out_ready, t + 1)
                sp.dma_start(out[t * P:(t + 1) * P, :], n_tok[:, t, :]).then_inc(stored, 16)
            sp.wait_ge(stored, 16 * NT)

        @block.gpsimd
        def _(pool):
            pool.memset(eps[:], EPS).then_inc(consts_built, 1)
            pool.memset(ones[:], 1.0).then_inc(consts_built, 1)
            pool.memset(ident[:], 0.0).then_inc(consts_built, 1)
            pool.memset(before[:], 1.0).then_inc(consts_built, 1)
            pool.memset(mask[:], 0.0).then_inc(consts_built, 1)
            pool.memset(u_pad[:, :, 0:META], 0.0).then_inc(consts_built, 1)
            pool.memset(win_a[:, :, 0:META], 0.0).then_inc(consts_built, 1)
            pool.memset(win_b[:, :, 0:META], 0.0).then_inc(consts_built, 1)
            pool.iota(slot_no[:], [[1, P]], base=0, channel_multiplier=0,
                      allow_small_or_imprecise_dtypes=True).then_inc(consts_built, 1)
            pool.iota(expert_no[:], [[0, NT], [1, EXPERTS]], base=0, channel_multiplier=0,
                      allow_small_or_imprecise_dtypes=True).then_inc(consts_built, 1)
            pool.iota(head_count[:], [[0, POOL_GROUPS], [1, META]], base=1, channel_multiplier=0,
                      allow_small_or_imprecise_dtypes=True).then_inc(consts_built, 1)
            pool.wait_ge(consts_built, 11)
            pool.affine_select(ident[:], ident[:], [[-1, P]], ALU.not_equal, 1.0, base=0,
                               channel_multiplier=1).then_inc(consts_built, 1)
            pool.affine_select(before[:], before[:], [[1, P]], ALU.is_gt, 0.0, base=0,
                               channel_multiplier=-1).then_inc(consts_built, 1)
            pool.wait_ge(consts_built, 13)
            pool.memset(mask[0:64, 0, META + CHUNK:META + 2 * CHUNK], NEG).then_inc(consts_built, 1)
            pool.wait_ge(consts_built, 14)
            pool.memset(mask[0:64, 1, META + 3 * CHUNK:L], NEG).then_inc(consts_built, 1)
            pool.wait_ge(consts_built, 15)
            pool.memset(mask[64:128, 1, META:META + CHUNK], NEG).then_inc(consts_built, 1)
            pool.wait_ge(consts_built, 16)
            for g in range(POOL_GROUPS):
                pool.tensor_scalar(head_count[:, g, :], head_count[:, g, :], float(2 << g), None,
                                   ALU.min).then_inc(consts_built, 1)

            def windows(l):
                pool.wait_ge(proj_evicted, 10 * l + 4)
                done = WINDOW_STEPS * l
                src = u_pad
                for s, dst in enumerate((win_a, win_b, win_a, win_b)):
                    lag = 1 << s
                    if s:
                        pool.wait_ge(window_step, done + s)
                    pool.tensor_tensor(dst[:, s:, META:], src[:, s:, META:],
                                       src[:, s:, META - lag:META + L - lag],
                                       ALU.add).then_inc(window_step, 1)
                    src = dst
                pool.wait_ge(window_step, done + 4)
                for g, win in enumerate((win_a, win_b, win_a, win_b)):
                    pool.tensor_scalar(pooled[:, g, META:], win[:, g, 2 * META:], 1.0 / (2 << g),
                                       None, ALU.mult).then_inc(window_step, 1)
                    pool.tensor_tensor(pooled[:, g, 0:META], win[:, g, META:2 * META],
                                       inv_count[:, g, :], ALU.mult).then_inc(window_step, 1)
                pool.wait_ge(window_step, done + 12)
                pool.tensor_tensor(pooled[:], pooled[:], u_pad[:, :, META:],
                                   ALU.subtract).then_inc(pooled_ready, 1)

            pool.wait_ge(inv_count_ready, 1)
            windows(0)
            pool.wait_ge(down_added, KT * STEPS)
            pool.memset(u_pad[:, :, 0:META], 0.0).then_inc(zeros_ready, 1)
            pool.memset(win_a[:, :, 0:META], 0.0).then_inc(zeros_ready, 1)
            pool.memset(win_b[:, :, 0:META], 0.0).then_inc(zeros_ready, 1)
            pool.wait_ge(zeros_ready, 3)
            windows(1)

        @block.tensor
        def _(pe):
            def split_product(o, a_hi, a_lo, b_hi, b_lo, start, stop):
                pe.matmul(o, a_hi, b_hi, start=start, stop=False)
                pe.matmul(o, a_hi, b_lo, start=False, stop=False)
                return pe.matmul(o, a_lo, b_hi, start=False, stop=stop)

            def keep_clock(b, n):
                for _ in range(n):
                    pe.matmul(bank[:, b, 0:L], ones[:], mask[:, 0, :], start=True, stop=True)

            def weights(g, shape, i=None, **sizes):
                wait_rest(pe, g, i)
                return (w_hi[:, g % SPLIT, :].rearrange(shape, **sizes),
                        w_lo[:, g % SPLIT, :].rearrange(shape, **sizes))

            def square_sum(v):
                pe.wait_ge(square_part, 3 * v + 3)
                m = pe.matmul(bank[:, 7, 0:L], ones[:], sq[:, 0, :], start=True, stop=True)
                m.then_inc(square_sum_ready, 1)

            def two_tiles(g, b0, first=None):
                whi, wlo = weights(g, "p (c k m) -> p c k m", c=2, k=KT)
                for c in range(2):
                    for k in range(KT):
                        if first is not None and c == 0:
                            pe.wait_ge(xn_lo_ready, KT * first + k + 1)
                        m = split_product(bank[:, b0 + c, 0:L], whi[:, c, k], wlo[:, c, k],
                                          xn_hi[:, k, :], xn_lo[:, k, :], k == 0, k == KT - 1)
                m.then_inc(weights_done, 1)

            def project(l):
                g0 = MIX1 * l
                two_tiles(g0, 0, 2 * l)
                square_sum(2 * l)
                two_tiles(g0 + 1, 2)
                whi, wlo = weights(g0 + 2, "p (k m) -> p k m", k=KT)
                for c in range(2):
                    cols = slice(c * P, (c + 1) * P)
                    for k in range(KT):
                        m = split_product(bank[:, 4 + c, 0:L], whi[:, k, cols], wlo[:, k, cols],
                                          xn_hi[:, k, :], xn_lo[:, k, :], k == 0, k == KT - 1)
                m.then_inc(weights_done, 1)
                pe.wait_ge(proj_evicted, 10 * l + 2)
                two_tiles(g0 + 3, 0)
                pe.wait_ge(proj_evicted, 10 * l + 6)
                for t in range(NT + 1):
                    m = P if t < NT else META
                    mm = pe.transpose(bank[0:m, 6, t * P:(t + 1) * P], v_t[:, tile_cols(t)], ident[:])
                mm.then_inc(v_turned, 1)
                pe.wait_ge(proj_evicted, 10 * l + 4)
                two_tiles(g0 + 4, 2)

            def attention(l, early_output):
                us, u0, p0 = units(l), UNIT0[l], PAIR0[l]
                keep_clock(7, 2)
                pe.wait_ge(proj_evicted, 10 * l + 10)
                pe.wait_ge(v_evicted, 2 * (l + 1))
                for step in range(len(us) + 5):
                    if step < len(us):
                        t, j, b = us[step]
                        rows = slice(HD * b, HD * b + HD)
                        n = key_blocks(t)[-1][2]
                        m = P if t < NT else META
                        if step >= 2:
                            pe.wait_ge(masked_ready, u0 + step - 1)
                        pe.matmul(bank[0:m, step % 2, 0:n], q_t[rows, j, tile_cols(t)], k_t[rows, 0:n],
                                  start=True, stop=True).then_inc(scores_ready, 1)
                    if step == 2:
                        keep_clock(7, 2)
                    u = step - 2
                    if 0 <= u < len(us):
                        t, j, b = us[u]
                        m = P if t < NT else META
                        pe.wait_ge(exp_ready, u0 + u + 1)
                        if u >= 2:
                            pe.wait_ge(prob_t_ready[u % 2], (u0 + u) // 2)
                        for kt, c0, c1 in key_blocks(t):
                            mm = pe.transpose(bank[0:c1 - c0, 3 + u % 2, kt * P:kt * P + m],
                                              prob[0:m, u % 3, c0:c1], ident[0:m, 0:m])
                        mm.then_inc(prob_t_psum, 1)
                    u = step - 3
                    if 0 <= u < len(us):
                        t, j, b = us[u]
                        rows = slice(HD * b, HD * b + HD)
                        m = P if t < NT else META
                        pe.wait_ge(prob_t_ready[u % 2], (u0 + u) // 2 + 1)
                        pair = u // 2
                        if b == 0 and pair >= 2:
                            pe.wait_ge(head_norm_ready, p0 + pair - 1)
                        blocks = key_blocks(t)
                        for n, (kt, c0, c1) in enumerate(blocks):
                            mm = pe.matmul(bank[0:m, 5 + pair % 2, rows], prob_t[0:c1 - c0, u % 2, kt, 0:m],
                                           v_tok[0:c1 - c0, kt, rows], start=n == 0,
                                           stop=n == len(blocks) - 1)
                        mm.then_inc(head_out_ready, 1)
                    u = step - 5
                    if u >= 0 and u % 2:
                        t, j, b = us[u]
                        m = P if t < NT else META
                        pair = u // 2
                        pe.wait_ge(head_norm_ready, p0 + pair + 1)
                        if pair:
                            pe.wait_ge(mix_lo_ready, p0 + pair)
                        pe.transpose(bank[:, 7, 0:m], o_tok[0:m, pair % 2, :],
                                     ident[0:m, 0:m]).then_inc(pair_turned, 1)
                    if step >= len(us) + 3:
                        early_output(step - len(us) - 3)
                    g = (step - 6) // 3
                    if step >= 6 and step % 3 == 0 and g < POOL_GROUPS:
                        pe.wait_ge(pooled_ready, l + 1)
                        if g:
                            pe.wait_ge(pool_lo_ready, POOL_GROUPS * l + g)
                        pe.matmul(bank[:, 2, 0:L], pw[:, POOL_GROUPS * l + g, :], pooled[:, g, :],
                                  start=True, stop=True).then_inc(pool_out_ready, 1)

            def wait_mixed(l, k):
                if k < POOL_GROUPS:
                    pe.wait_ge(pool_lo_ready, POOL_GROUPS * l + k + 1)
                else:
                    pe.wait_ge(mix_lo_ready, PAIR0[l] + (NT + 1 - l) * (k - POOL_GROUPS + 1))

            pe.wait_ge(consts_built, CONSTS)
            pe.wait_ge(xn_lo_ready, 4)
            keep_clock(7, 7)
            project(0)
            pe.wait_ge(consts_loaded, 16 * LOADS)

            def out_features(gg, cs, ks):
                whi, wlo = weights(5 + gg, "p (c k m) -> p c k m", c=2, k=KT)
                for c in cs:
                    for k in ks:
                        if gg == 0 and c == 0:
                            wait_mixed(0, k)
                        m = split_product(bank[:, 2 * gg + c, 0:L], whi[:, c, k], wlo[:, c, k],
                                          mix_hi[:, k, :], mix_lo[:, k, :], k == 0, k == KT - 1)
                return m

            attention(0, lambda c: out_features(0, [c], range(KT - 1)))
            out_features(0, range(2), [KT - 1]).then_inc(weights_done, 1)
            for gg in range(1, 4):
                out_features(gg, range(2), range(KT)).then_inc(weights_done, 1)

            def down(n, a, g):
                whi, wlo = weights(g, "p (d f m) -> p d f m", d=4, f=4)
                pe.wait_ge(ff_lo_ready, 2 * n + 2)
                q = 2 * n + a
                for d in range(4):
                    if q:
                        pe.wait_ge(down_added, 4 * (q - 1) + d + 1)
                    elif d == 3:
                        pe.wait_ge(rms_ready, 2)
                    for f in range(4):
                        slot, c = (2 * n + f // 2) % 4, f % 2
                        m = split_product(bank[:, 4 + d, 0:L], whi[:, d, f], wlo[:, d, f],
                                          ff_hi[:, slot, c, :], ff_lo[:, slot, c, :], f == 0, f == 3)
                    m.then_inc(down_part if d < 3 else weights_done, 1)

            for n in range(STEPS):
                for s in range(2):
                    pair = 2 * n + s
                    if pair:
                        pe.wait_ge(gate_scaled, pair)
                    else:
                        pe.wait_ge(out_added, 2)
                    two_tiles(ffn_gate(n, s), 0, None if pair else 1)
                    if pair:
                        pe.wait_ge(up_scaled, pair)
                    else:
                        square_sum(1)
                    two_tiles(ffn_gate(n, s) + 1, 2)
                    if n:
                        down(n - 1, s, ffn_gate(n, s) + 2)
            down(STEPS - 1, 0, MIX1 - 2)
            down(STEPS - 1, 1, MIX1 - 1)

            project(1)
            def out_rows(n, kh, ts=range(NT)):
                whi, wlo = weights(MIX1 + 5 + 2 * n + kh, "p (k m) -> p k m", k=4)
                for t in ts:
                    for k in range(4):
                        kk = 4 * kh + k
                        if n == 0 and t == 0:
                            wait_mixed(1, kk)
                        m = split_product(bank[:, 2 * n + t, :], mix_hi[:, kk, tile_cols(t)],
                                          mix_lo[:, kk, tile_cols(t)], whi[:, k], wlo[:, k],
                                          kh == 0 and k == 0, False)
                if ts[-1] == NT - 1:
                    m.then_inc(weights_done, 1)

            attention(1, lambda t: out_rows(0, 0, [t]))

            def turn_residual(kp):
                pe.wait_ge(h_tok_ready, 2 if kp < 2 else 4)
                for k in range(2):
                    for t in range(NT):
                        m = pe.transpose(bank[:, 4 + kp, (NT * k + t) * P:(NT * k + t + 1) * P],
                                         h_tok[:, t, (2 * kp + k) * P:(2 * kp + k + 1) * P], ident[:])
                m.then_inc(xr_psum, 1)

            for n in range(2):
                for kh in range(1 if n == 0 else 0, 2):
                    out_rows(n, kh)
                    if n == 1 and kh == 0:
                        turn_residual(0)
                        turn_residual(1)
                for t in range(NT):
                    for k in range(4):
                        m = pe.matmul(bank[:, 2 * n + t, k * P:(k + 1) * P],
                                      h_t[:, 4 * n + k, tile_cols(t)], ident[:],
                                      start=False, stop=k == 3)
                    m.then_inc(out_tok_psum, 1)

            def logits(k0):
                for k in range(k0, k0 + 4):
                    if k == 6:
                        pe.wait_ge(xr_ready, 6)
                    for t in range(NT):
                        m = pe.matmul(bank[:, t, 0:EXPERTS], xr[:, k, t * P:(t + 1) * P],
                                      router[:, k, :], start=k == 0, stop=k == KT - 1)
                return m

            pe.wait_ge(xr_ready, 4)
            logits(0)
            turn_residual(2)
            turn_residual(3)
            keep_clock(3, 2)
            pe.wait_ge(xr_late_ready, 1)
            logits(4).then_inc(logits_psum, 1)
            keep_clock(3, 4)
            pe.wait_ge(route_step, CHOSEN)
            pe.matmul(bank[:, 1, 0:8], before[:], chosen[:, 0, :], start=True, stop=True)
            pe.matmul(bank[:, 1, 8:16], before[:], chosen[:, 1, :], start=True, stop=False)
            pe.matmul(bank[:, 1, 8:16], ones[:], chosen[:, 0, :], start=False, stop=True)
            pe.matmul(bank[:, 1, 16:24], ones[:], chosen[:, 0, :], start=True, stop=False)
            pe.matmul(bank[:, 1, 16:24], ones[:], chosen[:, 1, :], start=False,
                      stop=True).then_inc(places_psum, 1)
            keep_clock(3, 2)

            def gather(r):
                pe.wait_ge(pick_ready, NT * r + NT)
                for t in range(NT):
                    m = pe.matmul(bank[:, 7, SEQ + 2:SEQ + 3], pick[:, t, :],
                                  rstd2[:, t:t + 1], start=t == 0, stop=t == NT - 1)
                for b in range(2):
                    for k in range(4):
                        cols = slice((4 * b + k) * P, (4 * b + k + 1) * P)
                        for t in range(NT):
                            m = pe.matmul(bank[:, 5 + b, k * P:(k + 1) * P], x_tok[:, t, cols],
                                          pick[:, t, :], start=t == 0, stop=t == NT - 1)
                    m.then_inc(gathered_psum, 1)

            def scatter(r):
                for c in range(2):
                    pe.wait_ge(y_lo_ready, 2 * r + c + 3)
                    for t in range(NT):
                        o = bank[:, (5, 6, 7, 2)[2 * c + t], :]
                        pe.matmul(o, pick_t[:, t * P:(t + 1) * P], y_hi[:, c, :], start=True, stop=False)
                        pe.matmul(o, pick_t[:, t * P:(t + 1) * P], y_lo[:, c, :], start=False,
                                  stop=True).then_inc(scattered_psum, 1)

            pe.wait_ge(x_tok_ready, 2 * NT)
            gather(0)
            keep_clock(3, 3)
            pe.wait_ge(route_step, ROUTED)
            end = pe.value_load(rounds[0:1, 0:1], min_val=EXPERTS, max_val=2 * EXPERTS)
            pe.nop().then_inc(ht_psum, 1)
            pe.nop().then_inc(scattered_psum, 4)
            with pe.Fori(0, end) as i:
                def hidden_half(g, b):
                    whi, wlo = weights(MOE + g, "p (k m) -> p k m", i, k=4)
                    half = g % 2
                    if g in (0, 1):
                        pe.wait_ge(xg_lo_ready, 2 * i + g + 1)
                    for k in range(4):
                        kk = 4 * half + k
                        m = split_product(bank[:, b, :], xg_hi[:, kk, :], xg_lo[:, kk, :],
                                          whi[:, k], wlo[:, k], kk == 0, kk == KT - 1)
                    m.then_inc(weights_done, 1)

                def expert_down(n):
                    pe.wait_ge(ht_lo_ready, STEPS * i + n + 1)
                    for a in range(2):
                        whi, wlo = weights(MOE + e_down(n) + a, "p (f m) -> p f m", i, f=2)
                        for f in range(2):
                            ff = 2 * a + f
                            for c in range(2):
                                m = split_product(bank[:, 3 + c, :], ht_hi[:, n % 2, ff, :],
                                                  ht_lo[:, n % 2, ff, :],
                                                  whi[:, f, c * 512:(c + 1) * 512],
                                                  wlo[:, f, c * 512:(c + 1) * 512],
                                                  n == 0 and ff == 0, n == STEPS - 1 and ff == 3)
                        m.then_inc(weights_done, 1)
                        if n == STEPS - 2 and a == 0:
                            turn_hidden(STEPS - 1)

                def turn_hidden(n):
                    pe.wait_ge(e_h_ready, 1 + STEPS * i + n + 1)
                    for f in range(4):
                        m = pe.transpose(bank[:, 2, f * P:(f + 1) * P], e_h[:, f * P:(f + 1) * P], ident[:])
                    m.then_inc(ht_psum, 1)

                for n in range(STEPS):
                    pe.wait_ge(e_silu_ready, 1 + STEPS * i + n)
                    hidden_half(e_gate(n), 0)
                    hidden_half(e_gate(n) + 1, 0)
                    if n == 0:
                        with pe.If(i > 0):
                            scatter(i - 1)
                        with pe.Else():
                            pe.nop()
                        pe.nop()
                    if n == 1:
                        turn_hidden(0)
                        pe.wait_ge(y_ready, 1 + 2 * i)
                    pe.wait_ge(e_h_ready, 1 + STEPS * i + n)
                    hidden_half(e_gate(n) + 2, 1)
                    hidden_half(e_gate(n) + 3, 1)
                    if n == 0:
                        pe.wait_ge(scatter_added, 5 + 4 * i)
                        pe.wait_ge(gate_col_ready, i + 1)
                        for t in range(NT):
                            pe.transpose(bank[:, 7, t * P:(t + 1) * P], pick[:, t, :], ident[:])
                        for t in range(NT):
                            m = pe.matmul(bank[:, 7, 256:257], pick[:, t, :],
                                          gate_col[:, t:t + 1], start=t == 0, stop=t == NT - 1)
                        m.then_inc(slots_psum, 1)
                    else:
                        expert_down(n - 1)
                        if n < STEPS - 1:
                            turn_hidden(n)
                    if n == 3:
                        with pe.If(i < end - 1):
                            pe.wait_ge(slots_ready, 2 * i + 2)
                            gather(i + 1)
                        with pe.Else():
                            pe.nop()
                        pe.nop()
                expert_down(STEPS - 1)
            keep_clock(0, 4)
            scatter(end - 1)

        @block.scalar
        def _(act):
            def split(g, i=None):
                act.wait_ge(loaded[g % RAW], 16 * (g // RAW + 1) + (0 if i is None else 16 * (FFN_G // RAW) * i))
                if g >= SPLIT:
                    act.wait_ge(weights_done, g - SPLIT + 1 + (0 if i is None else FFN_G * i))
                act.activation(w_hi[:, g % SPLIT, :], raw[:, g % RAW, :], ACT.Copy).then_inc(hi_ready, 1)

            def gained(v, k):
                act.activation(xn_hi[:, k, :], h_t[:, k, :], ACT.Copy,
                               scale=gain[:, NORM_GAIN[v], k:k + 1]).then_inc(xn_hi_ready, 1)

            def square(b):
                act.activation(sq[:, 4 * b:4 * b + 4, :], h_t[:, 4 * b:4 * b + 4, :],
                               ACT.Square).then_inc(squares_ready, 1)

            def rms_of(v):
                act.wait_ge(square_sum_ready, v + 1)
                act.activation(rms_t[:], bank[:, 7, 0:L], ACT.Sqrt, bias=eps[:],
                               scale=1.0 / D).then_inc(rms_ready, 1)

            def project(l):
                g0 = MIX1 * l
                rms_of(2 * l)
                for g in range(5):
                    split(g0 + g + AHEAD)
                    if g == 3:
                        act.wait_ge(v_turned, l + 1)
                        act.activation(v_tok[:, 0:NT, :],
                                       bank[:, 6, 0:NT * P].rearrange("p (t m) -> p t m", t=NT),
                                       ACT.Copy).then_inc(v_evicted, 1)
                        act.activation(v_tok[0:META, NT, :], bank[0:META, 6, NT * P:(NT + 1) * P],
                                       ACT.Copy).then_inc(v_evicted, 1)

            def warm_sqrt(n):
                act.activation(warm[:, n:n + 1], eps[:], ACT.Sqrt)

            def attention(l):
                us, u0, p0 = units(l), UNIT0[l], PAIR0[l]
                for step in range(len(us) + 6):
                    if step < len(us):
                        t, j, b = us[step]
                        m = P if t < NT else META
                        n = key_blocks(t)[-1][2]
                        head = l * HEADS + j + 4 * b
                        c = slice(step, step + 1)
                        act.wait_ge(masked_ready, u0 + step + 1)
                        act.activation(prob[0:m, step % 3, 0:n], prob[0:m, step % 3, 0:n], ACT.Exp,
                                       bias=neg_max[0:m, c], scale=-1.0,
                                       accum_out=exp_sum[0:m, c]).then_inc(exp_ready, 1)
                        act.activation(exp_sink[0:m, c], sink[0:m, head:head + 1], ACT.Exp,
                                       bias=neg_max[0:m, c]).then_inc(exp_sink_ready, 1)
                    u = step - 2
                    if 0 <= u < len(us) and u % 2 == 0:
                        act.wait_ge(prob_t_psum, u0 + u + 1)
                        if u >= 2:
                            act.wait_ge(head_out_ready, u0 + u - 1)
                        copy_turned(u, us[u][0], lambda o, a: act.activation(o, a, ACT.Copy)
                                    ).then_inc(prob_t_ready[0], 1)
                    if step == len(us) + 1:
                        split(MIX1 * l + 5 + AHEAD)
                    u = step - 6
                    if u >= 0 and u % 2:
                        t, j, b = us[u]
                        act.wait_ge(pair_turned, p0 + u // 2 + 1)
                        w = P if t < NT else META
                        act.activation(mix_hi[:, POOL_GROUPS + j, tile_cols(t)], bank[:, 7, 0:w],
                                       ACT.Copy).then_inc(mix_hi_ready, 1)
                    g = (step - 7) // 3
                    if step >= 7 and step % 3 == 1 and g < POOL_GROUPS:
                        act.wait_ge(pool_out_ready, POOL_GROUPS * l + g + 1)
                        act.activation(mix_hi[:, g, :], bank[:, 2, 0:L], ACT.Copy,
                                       scale=pscale[:, POOL_GROUPS * l + g:POOL_GROUPS * l + g + 1]
                                       ).then_inc(pool_hi_ready, 1)

            act.wait_ge(gain_loaded, 16)
            for b in range(2):
                act.wait_ge(x_loaded[b], 16)
                for k in range(4 * b, 4 * b + 4):
                    gained(0, k)
                if b == 0:
                    split(0)
            square(0)
            square(1)
            split(1)
            act.wait_ge(consts_built, CONSTS)
            project(0)
            act.wait_ge(consts_loaded, 16 * LOADS)
            attention(0)
            warm_sqrt(0)
            for gg in range(4):
                if gg:
                    split(5 + gg + AHEAD)
                for k in (2 * gg, 2 * gg + 1):
                    act.wait_ge(out_added, k + 1)
                    gained(1, k)
                if gg == 1:
                    square(0)
            square(1)
            for n in range(STEPS):
                for s in range(2):
                    pair = 2 * n + s
                    g = ffn_gate(n, s)
                    split(g + AHEAD)
                    if not pair:
                        rms_of(1)
                    act.wait_ge(gate_scaled, pair + 1)
                    act.activation(ff_silu[:], ff_silu[:], ACT.Silu).then_inc(silu_ready, 1)
                    split(g + 1 + AHEAD)
                    act.wait_ge(ff_h_ready, pair + 1)
                    act.activation(ff_hi[:, pair % 4], ff_h[:], ACT.Copy).then_inc(ff_hi_ready, 1)
                    if n:
                        split(g + 2 + AHEAD)
            warm_sqrt(1)
            for b in range(2):
                split(MIX1 + b)
                for k in range(4 * b, 4 * b + 4):
                    act.wait_ge(down_added, KT * (STEPS - 1) + k + 1)
                    gained(2, k)
                square(b)
            project(1)
            attention(1)
            warm_sqrt(2)

            def token_squares(n, t, source):
                act.activation(source, h_tok[:, t, 512 * n:512 * n + 512], ACT.Square,
                               accum_out=sums[:, n, t:t + 1]).then_inc(tok_sum_ready, 1)

            def token_rms(first):
                act.wait_ge(total_ready, first + 1)
                act.activation(rms[:], total[:], ACT.Sqrt, bias=eps[:], scale=1.0 / D).then_inc(tok_rms_ready, 1)

            def turned(k):
                act.wait_ge(xr_psum, k // 2 + 1)
                act.activation(xr[:, k, :], bank[:, 4 + k // 2, (k % 2) * SEQ:(k % 2 + 1) * SEQ], ACT.Copy,
                               scale=gain[:, 3, k:k + 1]).then_inc(xr_ready, 1)

            def keep_input(n, t):
                cols = slice(512 * n, 512 * n + 512)
                act.activation(x_tok[:, t, cols], h_tok[:, t, cols], ACT.Copy).then_inc(x_tok_ready, 1)

            for gg in range(4):
                if gg:
                    split(MIX1 + 5 + gg + AHEAD)
                if gg == 2:
                    for t in range(NT):
                        act.wait_ge(h_tok_ready, t + 1)
                        token_squares(0, t, n_tok[:, t, 0:512])
            for k in range(4):
                turned(k)
            for t in range(NT):
                keep_input(0, t)
            for t in range(NT):
                act.wait_ge(h_tok_ready, NT + t + 1)
                token_squares(1, t, n_tok[:, t, 512:D])
            for k in (6, 7):
                turned(k)
            token_rms(0)
            for t in range(NT):
                keep_input(1, t)
            split(MOE + 2)
            act.wait_ge(route_step, GAP)
            act.activation(e2[:], gap[:], ACT.Exp).then_inc(gap_exp_ready, 1)
            act.activation(warm[:, 3:4], eps[:], ACT.Silu)
            def gathered_high(b):
                act.activation(xg_hi[:, 4 * b:4 * b + 4, :], xg[:, 4 * b:4 * b + 4, :],
                               ACT.Copy).then_inc(xg_hi_ready, 1)

            def slot_norms():
                act.activation(slot_rstd[:], bank[:, 7, SEQ + 2:SEQ + 3], ACT.Copy).then_inc(slot_rstd_ready, 1)

            for b in range(2):
                act.wait_ge(xg_ready, b + 1)
                gathered_high(b)
            slot_norms()
            act.wait_ge(route_step, ROUTED)
            end = act.value_load(rounds[0:1, 0:1], min_val=EXPERTS, max_val=2 * EXPERTS)
            act.nop().then_inc(e_silu_ready, 1)
            act.nop().then_inc(y_ready, 1)
            with act.Fori(0, end) as i:
                def step_of(j):
                    for n in range(STEPS):
                        if j == e_gate(n) + 1:
                            act.wait_ge(weights_done, MOE + j + 1 + FFN_G * i)
                            act.wait_ge(e_h_ready, 1 + STEPS * i + n)
                            if n == 0:
                                act.wait_ge(slot_rstd_ready, i + 1)
                            act.activation(e_silu[:], bank[:, 0, :], ACT.Silu,
                                           scale=slot_rstd[:]).then_inc(e_silu_ready, 1)
                        if j == e_turned(n):
                            act.wait_ge(ht_psum, 1 + STEPS * i + n + 1)
                            act.activation(ht_hi[:, n % 2], bank[:, 2, :].rearrange("p (f m) -> p f m", f=4),
                                           ACT.Copy).then_inc(ht_hi_ready, 1)
                    if j == 4:
                        act.wait_ge(slots_psum, i + 1)
                        act.activation(pick_t[:], bank[:, 7, 0:SEQ], ACT.Copy).then_inc(slots_ready, 1)
                        act.activation(slot_gate[:], bank[:, 7, SEQ:SEQ + 1], ACT.Copy).then_inc(slots_ready, 1)
                    if j == FFN_G - 4:
                        with act.If(i < end - 1):
                            act.wait_ge(weights_done, MOE + e_gate(STEPS - 1) + 4 + FFN_G * i)
                            act.wait_ge(xg_ready, 2 * i + 4)
                            gathered_high(0)
                            gathered_high(1)
                            act.wait_ge(e_h_ready, 1 + STEPS * (i + 1))
                            slot_norms()
                        with act.Else():
                            act.nop()
                        act.nop()

                for j in range(FFN_G):
                    step_of(j)
                    if j + SPLIT < FFN_G:
                        split(MOE + j + SPLIT, i)
                    elif j < FFN_G - 1:
                        with act.If(i < end - 1):
                            split(MOE + j + SPLIT, i)
                        with act.Else():
                            act.nop()
                        act.nop()
                act.wait_ge(weights_done, MOE + FFN_G + FFN_G * i)
                act.wait_ge(slots_ready, 2 * i + 2)
                for c in range(2):
                    act.activation(y[:, c, :], bank[:, 3 + c, :], ACT.Copy, scale=slot_gate[:]).then_inc(y_ready, 1)
                    act.wait_ge(y_ready, 1 + 2 * i + c + 1)
                    act.activation(y_hi[:, c, :], y[:, c, :], ACT.Copy).then_inc(y_hi_ready, 1)
                with act.If(i < end - 1):
                    split(MOE + FFN_G + SPLIT - 1, i)
                with act.Else():
                    act.nop()
                act.nop()
            warm_sqrt(4)

            for n in range(2):
                for t in range(NT):
                    act.wait_ge(scatter_added, 4 * end + NT * n + t + 2)
                    token_squares(n, t, n_tok[:, t, 512 * n:512 * n + 512])
            token_rms(1)

        @block.vector
        def _(dve):
            def split(g, i=None):
                dve.wait_ge(hi_ready, g + 1 + (0 if i is None else FFN_G * i))
                dve.tensor_tensor(w_lo[:, g % SPLIT, :], raw[:, g % RAW, :],
                                  w_hi[:, g % SPLIT, :].bitcast(F32), ALU.subtract).then_inc(lo_ready, 1)

            def gained_rest(v, k):
                dve.wait_ge(xn_hi_ready, KT * v + k + 1)
                dve.scalar_tensor_tensor(xn_lo[:, k, :], h_t[:, k, :], gain[:, NORM_GAIN[v], k:k + 1],
                                         xn_hi[:, k, :].bitcast(F32), ALU.mult,
                                         ALU.subtract).then_inc(xn_lo_ready, 1)

            def add_squares(v):
                dve.wait_ge(squares_ready, 2 * v + 2)
                for s, n in enumerate((4, 2, 1)):
                    if s:
                        dve.wait_ge(square_part, 3 * v + s)
                    dve.tensor_tensor(sq[:, 0:n, :], sq[:, 0:n, :], sq[:, n:2 * n, :],
                                      ALU.add).then_inc(square_part, 1)

            def rstd_of(v):
                dve.wait_ge(rms_ready, v + 1)
                dve.reciprocal(rstd[:], rms_t[:]).then_inc(rstd_ready, 1)
                dve.wait_ge(rstd_ready, v + 1)

            def project(l):
                g0 = MIX1 * l
                add_squares(2 * l)
                split(g0 + AHEAD)
                rstd_of(2 * l)
                for g in range(5):
                    if g:
                        split(g0 + g + AHEAD)
                    dve.wait_ge(weights_done, g0 + g + 1)
                    if g < 2:
                        if l and not g:
                            dve.wait_ge(zeros_ready, 3)
                        for c in range(2):
                            dve.tensor_tensor(u_pad[:, 2 * g + c, META:], bank[:, 2 * g + c, 0:L],
                                              rstd[:], ALU.mult).then_inc(proj_evicted, 1)
                    elif g == 2:
                        dve.tensor_tensor(k_t[:], bank[:, 4, 0:L], rstd[:], ALU.mult).then_inc(proj_evicted, 1)
                        dve.tensor_tensor(v_t[:], bank[:, 5, 0:L], rstd[:], ALU.mult).then_inc(proj_evicted, 1)
                    else:
                        for c in range(2):
                            j = 2 * (g - 3) + c
                            dve.scalar_tensor_tensor(q_t[:, j, :], bank[:, j, 0:L], HD ** -0.5, rstd[:],
                                                     ALU.mult, ALU.mult).then_inc(proj_evicted, 1)

            def attention(l):
                us, u0, p0 = units(l), UNIT0[l], PAIR0[l]
                for step in range(len(us) + 7):
                    if step < len(us):
                        t, j, b = us[step]
                        m = P if t < NT else META
                        n = key_blocks(t)[-1][2]
                        head = l * HEADS + j + 4 * b
                        dve.wait_ge(scores_ready, u0 + step + 1)
                        if step >= 3:
                            dve.wait_ge(prob_t_psum, u0 + step - 2)
                        dve.tensor_tensor_reduce(prob[0:m, step % 3, 0:n], bank[0:m, step % 2, 0:n],
                                                 mask[0:m, t % NT, 0:n], -1.0, neg_sink[0:m, head:head + 1],
                                                 ALU.add, ALU.min,
                                                 neg_max[0:m, step:step + 1]).then_inc(masked_ready, 1)
                    u = step - 2
                    if 0 <= u < len(us) and u % 2:
                        dve.wait_ge(prob_t_psum, u0 + u + 1)
                        if u >= 2:
                            dve.wait_ge(head_out_ready, u0 + u - 1)
                        copy_turned(u, us[u][0], dve.tensor_copy).then_inc(prob_t_ready[1], 1)
                    u = step - 4
                    if u >= 0 and u % 2 and u < len(us):
                        t, j, b = us[u]
                        m = P if t < NT else META
                        pair = u // 2
                        both = slice(u - 1, u + 1)
                        dve.wait_ge(exp_ready, u0 + u + 1)
                        dve.wait_ge(exp_sink_ready, u0 + u + 1)
                        dve.tensor_tensor(den[0:m, both], exp_sum[0:m, both], exp_sink[0:m, both],
                                          ALU.add).then_inc(den_ready, 1)
                        dve.wait_ge(den_ready, p0 + pair + 1)
                        dve.reciprocal(inv_den[0:m, both], den[0:m, both]).then_inc(inv_den_ready, 1)
                        dve.wait_ge(inv_den_ready, p0 + pair + 1)
                        dve.wait_ge(head_out_ready, u0 + u + 1)
                        if pair >= 2:
                            dve.wait_ge(pair_turned, p0 + pair - 1)
                        dve.tensor_tensor(o_tok[0:m, pair % 2, :].rearrange("p (b d) -> p b d", b=2),
                                          bank[0:m, 5 + pair % 2, 0:P].rearrange("p (b d) -> p b d", b=2),
                                          inv_den[0:m, both].unsqueeze(2).to_broadcast([m, 2, HD]),
                                          ALU.mult).then_inc(head_norm_ready, 1)
                    if step == len(us) + 3:
                        split(MIX1 * l + 5 + AHEAD)
                    u = step - 7
                    if u >= 0 and u % 2:
                        t, j, b = us[u]
                        dve.wait_ge(mix_hi_ready, p0 + u // 2 + 1)
                        w = P if t < NT else META
                        dve.tensor_tensor(mix_lo[:, POOL_GROUPS + j, tile_cols(t)], bank[:, 7, 0:w],
                                          mix_hi[:, POOL_GROUPS + j, tile_cols(t)].bitcast(F32),
                                          ALU.subtract).then_inc(mix_lo_ready, 1)
                    g = (step - 8) // 3
                    if step >= 8 and step % 3 == 2 and g < POOL_GROUPS:
                        dve.wait_ge(pool_hi_ready, POOL_GROUPS * l + g + 1)
                        dve.scalar_tensor_tensor(mix_lo[:, g, :], bank[:, 2, 0:L],
                                                 pscale[:, POOL_GROUPS * l + g:POOL_GROUPS * l + g + 1],
                                                 mix_hi[:, g, :].bitcast(F32), ALU.mult,
                                                 ALU.subtract).then_inc(pool_lo_ready, 1)

            dve.wait_ge(consts_built, CONSTS)
            dve.reciprocal(inv_count[:], head_count[:]).then_inc(inv_count_ready, 1)
            dve.wait_ge(gain_loaded, 16)
            for b in range(2):
                for k in range(4 * b, 4 * b + 4):
                    gained_rest(0, k)
                if b == 0:
                    split(0)
            split(1)
            project(0)
            dve.wait_ge(consts_loaded, 16 * LOADS)
            dve.tensor_scalar(neg_sink[:], sink[:], -1.0, None, ALU.mult).then_inc(neg_sink_ready, 1)
            dve.wait_ge(neg_sink_ready, 1)
            attention(0)
            for gg in range(4):
                if gg:
                    split(5 + gg + AHEAD)
                dve.wait_ge(weights_done, 5 + gg + 1)
                for c in range(2):
                    dt = 2 * gg + c
                    dve.tensor_tensor(h_t[:, dt, :], h_t[:, dt, :], bank[:, dt, 0:L],
                                      ALU.add).then_inc(out_added, 1)
                if gg:
                    gained_rest(1, 2 * gg - 2)
                    gained_rest(1, 2 * gg - 1)
            gained_rest(1, 6)
            gained_rest(1, 7)
            add_squares(1)

            def add_down(q, g):
                for d in range(4):
                    if d < 3:
                        dve.wait_ge(down_part, 3 * q + d + 1)
                    else:
                        dve.wait_ge(weights_done, g + 1)
                    if q >= 2:
                        dve.wait_ge(down_added, 4 * (q - 2) + d + 1)
                    dt = 4 * (q % 2) + d
                    dve.tensor_tensor(h_t[:, dt, :], h_t[:, dt, :], bank[:, 4 + d, 0:L],
                                      ALU.add).then_inc(down_added, 1)

            def hidden_rest(pair):
                dve.wait_ge(ff_hi_ready, pair + 1)
                dve.tensor_tensor(ff_lo[:, pair % 4], ff_h[:], ff_hi[:, pair % 4].bitcast(F32),
                                  ALU.subtract).then_inc(ff_lo_ready, 1)

            for n in range(STEPS):
                for s in range(2):
                    pair = 2 * n + s
                    g = ffn_gate(n, s)
                    split(g + AHEAD)
                    if not pair:
                        rstd_of(1)
                    both = rstd[:].unsqueeze(1).to_broadcast([P, 2, L])
                    dve.wait_ge(weights_done, g + 1)
                    if pair:
                        dve.wait_ge(ff_h_ready, pair)
                    dve.tensor_tensor(ff_silu[:], bank[:, 0:2, 0:L], both, ALU.mult).then_inc(gate_scaled, 1)
                    split(g + 1 + AHEAD)
                    dve.wait_ge(weights_done, g + 2)
                    if pair:
                        dve.wait_ge(ff_lo_ready, pair)
                    dve.tensor_tensor(ff_h[:], bank[:, 2:4, 0:L], both, ALU.mult).then_inc(up_scaled, 1)
                    dve.wait_ge(up_scaled, pair + 1)
                    dve.wait_ge(silu_ready, pair + 1)
                    dve.tensor_tensor(ff_h[:], ff_silu[:], ff_h[:], ALU.mult).then_inc(ff_h_ready, 1)
                    if n:
                        split(g + 2 + AHEAD)
                    hidden_rest(pair)
                    if n:
                        add_down(pair - 2, g + 2)
            split(MIX1)
            add_down(2 * STEPS - 2, MIX1 - 2)
            for k in range(4):
                gained_rest(2, k)
            split(MIX1 + 1)
            add_down(2 * STEPS - 1, MIX1 - 1)
            for k in range(4, KT):
                gained_rest(2, k)

            project(1)
            attention(1)
            def residual(n, t):
                dve.wait_ge(out_tok_psum, 2 * n + t + 1)
                dve.tensor_copy(h_tok[:, t, 512 * n:512 * n + 512], bank[:, 2 * n + t, :]
                                ).then_inc(h_tok_ready, 1)

            for gg in range(4):
                if gg:
                    split(MIX1 + 5 + gg + AHEAD)
                if gg == 2:
                    residual(0, 0)
                    residual(0, 1)
            residual(1, 0)
            residual(1, 1)

            def token_rstd(first):
                dve.wait_ge(tok_sum_ready, 4 * first + 4)
                dve.tensor_tensor(total[:], sums[:, 0, :], sums[:, 1, :], ALU.add).then_inc(total_ready, 1)
                dve.wait_ge(tok_rms_ready, first + 1)
                dve.reciprocal(rstd2[:], rms[:]).then_inc(tok_rstd_ready, 1)
                dve.wait_ge(tok_rstd_ready, first + 1)

            dve.wait_ge(xr_psum, 3)
            dve.tensor_tensor(xr[:, 4:6, :], bank[:, 6, :].rearrange("p (k m) -> p k m", k=2),
                              gain[:, 3, 4:6].unsqueeze(2).to_broadcast([P, 2, SEQ]),
                              ALU.mult).then_inc(xr_late_ready, 1)
            token_rstd(0)

            def wide(a):
                return a.to_broadcast([P, NT, EXPERTS])

            def by_token(a, first):
                return a[:, first:first + EXPERTS, :].rearrange("p e t -> p t e")

            dve.wait_ge(logits_psum, 1)
            for t in range(NT):
                dve.tensor_scalar(lg[:, t, :], bank[:, t, 0:EXPERTS], rstd2[:, t:t + 1],
                                  None, ALU.mult).then_inc(route_step, 1)
            for t in range(NT):
                dve.wait_ge(route_step, t + 1)
                dve.max(top[:, t, :], lg[:, t, :]).then_inc(route_step, 1)
            dve.wait_ge(route_step, 4)
            dve.tensor_tensor(gap[:], top[:, :, 1], top[:, :, 0], ALU.subtract).then_inc(route_step, 1)
            for t in range(NT):
                dve.max_index(top_at[:, t, :], top[:, t, :], lg[:, t, :]).then_inc(route_step, 1)
            dve.wait_ge(route_step, 7)
            dve.tensor_copy(top_no[:], top_at[:, :, 0:2]).then_inc(route_step, 1)
            dve.wait_ge(route_step, 8)
            dve.tensor_tensor(oh1[:], expert_no[:], wide(top_no[:, :, 0:1]), ALU.is_equal).then_inc(route_step, 1)
            dve.tensor_tensor(oh2[:], expert_no[:], wide(top_no[:, :, 1:2]), ALU.is_equal).then_inc(route_step, 1)
            dve.wait_ge(route_step, 10)
            dve.tensor_tensor(chosen[:], oh1[:], oh2[:], ALU.add).then_inc(route_step, 1)
            dve.wait_ge(places_psum, 1)
            dve.wait_ge(route_step, CHOSEN)
            dve.scalar_tensor_tensor(posa[:], bank[:, 1, 0:16].rearrange("p (t e) -> p t e", t=NT), 1000.0,
                                     chosen[:], ALU.add, ALU.mult).then_inc(route_step, 1)
            dve.tensor_reduce(most[:], bank[:, 1, 16:24], AXX, ALU.max).then_inc(route_step, 1)
            dve.wait_ge(route_step, 12)
            for q in range(2):
                dve.tensor_scalar(by_token(place, EXPERTS * q), posa[:], -1000.0 - P * q, None,
                                  ALU.add).then_inc(route_step, 1)
            dve.wait_ge(route_step, 13)
            dve.tensor_scalar(rounds_f[:], most[:], float(P), float(EXPERTS), ALU.is_gt,
                              ALU.mult).then_inc(route_step, 1)
            dve.wait_ge(route_step, 16)
            dve.tensor_scalar(rounds[:], rounds_f[:], float(EXPERTS), None, ALU.add).then_inc(route_step, 1)

            def choose(r):
                for t in range(NT):
                    dve.tensor_scalar(pick[:, t, :], slot_no[:], place[:, bass.ds(r, 1), t], None,
                                      ALU.is_equal).then_inc(pick_ready, 1)

            def gates_of(r):
                dve.tensor_copy(gate_col[:], gates[:, bass.ds(r, 1), :].rearrange("p a t -> p (a t)")
                                ).then_inc(gate_col_ready, 1)

            def gained(r, k0):
                for b in range(2):
                    dve.wait_ge(gathered_psum, k0 + b)
                    dve.tensor_tensor(xg[:, 4 * b:4 * b + 4, :],
                                      bank[:, 5 + b, :].rearrange("p (k m) -> p k m", k=4),
                                      gain[:, 3, 4 * b:4 * b + 4].unsqueeze(2).to_broadcast([P, 4, P]),
                                      ALU.mult).then_inc(xg_ready, 1)

            def gathered_rest(r, b):
                dve.wait_ge(xg_hi_ready, 2 * r + b + 1)
                dve.tensor_tensor(xg_lo[:, 4 * b:4 * b + 4, :], xg[:, 4 * b:4 * b + 4, :],
                                  xg_hi[:, 4 * b:4 * b + 4, :].bitcast(F32),
                                  ALU.subtract).then_inc(xg_lo_ready, 1)

            dve.wait_ge(route_step, 15)
            choose(0)
            dve.wait_ge(gap_exp_ready, 1)
            dve.tensor_scalar(den2[:], e2[:], 1.0, None, ALU.add).then_inc(route_step, 1)
            dve.wait_ge(route_step, ROUTED + 1)
            dve.reciprocal(g1[:], den2[:]).then_inc(route_step, 1)
            dve.wait_ge(route_step, ROUTED + 2)
            dve.tensor_tensor(g2[:], e2[:], g1[:], ALU.mult).then_inc(route_step, 1)
            dve.tensor_tensor(ga[:], oh1[:], wide(g1[:].unsqueeze(2)), ALU.mult).then_inc(route_step, 1)
            dve.wait_ge(route_step, ROUTED + 3)
            dve.tensor_tensor(gb[:], oh2[:], wide(g2[:].unsqueeze(2)), ALU.mult).then_inc(route_step, 1)
            dve.wait_ge(route_step, ROUTED + 5)
            for q in range(2):
                dve.tensor_tensor(by_token(gates, EXPERTS * q), ga[:], gb[:], ALU.add).then_inc(route_step, 1)
            gained(0, 1)
            dve.wait_ge(route_step, GATED)
            gates_of(0)
            end = dve.value_load(rounds[0:1, 0:1], min_val=EXPERTS, max_val=2 * EXPERTS)
            gathered_rest(0, 0)
            gathered_rest(0, 1)
            split(MOE + 2)
            dve.nop().then_inc(e_h_ready, 1)
            dve.nop().then_inc(scatter_added, 5)
            dve.nop().then_inc(y_lo_ready, 2)
            def add_round(r):
                dve.wait_ge(scatter_added, 4 * r + 5)
                for c in range(2):
                    for t in range(NT):
                        dve.wait_ge(scattered_psum, 4 * r + 2 * c + t + 5)
                        dve.tensor_tensor(h_tok[:, t, 512 * c:512 * c + 512], h_tok[:, t, 512 * c:512 * c + 512],
                                          bank[:, (5, 6, 7, 2)[2 * c + t], :], ALU.add).then_inc(scatter_added, 1)

            with dve.Fori(0, end) as i:
                def step_of(j):
                    if j == 1:
                        with dve.If(i > 0):
                            add_round(i - 1)
                        with dve.Else():
                            dve.nop()
                        dve.nop()
                    for n in range(STEPS):
                        if j == e_gate(n) + 3:
                            dve.wait_ge(weights_done, MOE + j + 1 + FFN_G * i)
                            dve.wait_ge(e_silu_ready, 1 + STEPS * i + n + 1)
                            dve.wait_ge(ht_psum, 1 + STEPS * i + n)
                            dve.scalar_tensor_tensor(e_h[:], bank[:, 1, :], slot_rstd[:], e_silu[:],
                                                     ALU.mult, ALU.mult).then_inc(e_h_ready, 1)
                        if j == e_turned(n):
                            dve.wait_ge(ht_hi_ready, STEPS * i + n + 1)
                            dve.tensor_tensor(ht_lo[:, n % 2], bank[:, 2, :].rearrange("p (f m) -> p f m", f=4),
                                              ht_hi[:, n % 2].bitcast(F32), ALU.subtract).then_inc(ht_lo_ready, 1)
                    if j == 12:
                        with dve.If(i < end - 1):
                            dve.wait_ge(slots_psum, i + 1)
                            choose(i + 1)
                            gates_of(i + 1)
                        with dve.Else():
                            dve.nop()
                        dve.nop()
                    if j == e_down(3) - 4:
                        with dve.If(i < end - 1):
                            gained(i + 1, 2 * i + 3)
                        with dve.Else():
                            dve.nop()
                        dve.nop()
                    if j == FFN_G - 3:
                        with dve.If(i < end - 1):
                            gathered_rest(i + 1, 0)
                            gathered_rest(i + 1, 1)
                        with dve.Else():
                            dve.nop()
                        dve.nop()

                for j in range(FFN_G):
                    step_of(j)
                    if j + SPLIT < FFN_G:
                        split(MOE + j + SPLIT, i)
                    elif j < FFN_G - 1:
                        with dve.If(i < end - 1):
                            split(MOE + j + SPLIT, i)
                        with dve.Else():
                            dve.nop()
                        dve.nop()
                for c in range(2):
                    dve.wait_ge(y_hi_ready, 2 * i + c + 1)
                    dve.tensor_tensor(y_lo[:, c, :], y[:, c, :], y_hi[:, c, :].bitcast(F32),
                                      ALU.subtract).then_inc(y_lo_ready, 1)
                with dve.If(i < end - 1):
                    split(MOE + FFN_G + SPLIT - 1, i)
                with dve.Else():
                    dve.nop()
                dve.nop()
            add_round(end - 1)

            token_rstd(1)
            for t in range(NT):
                dve.scalar_tensor_tensor(n_tok[:, t, :], h_tok[:, t, :], rstd2[:, t:t + 1], g_final[:],
                                         ALU.mult, ALU.mult).then_inc(out_ready, 1)


def kernel(x, meta_tokens, norm_mix_g, w_in, attn_sinks, pool_w, pool_scale, w_out, norm_ffn_g,
           dense_w_gate, dense_w_up, dense_w_down, moe_w_router, moe_w_gate, moe_w_up, moe_w_down,
           final_norm_g):
    import numpy as np
    import concourse.bacc as bacc
    from concourse.bass_utils import run_bass_kernel_spmd

    (x, meta_tokens, norm_mix_g, w_in, attn_sinks, pool_w, pool_scale, w_out, norm_ffn_g, dense_w_gate,
     dense_w_up, dense_w_down, moe_w_router, moe_w_gate, moe_w_up, moe_w_down, final_norm_g) = (
        np.asarray(a) for a in (
            x, meta_tokens, norm_mix_g, w_in, attn_sinks, pool_w, pool_scale, w_out, norm_ffn_g,
            dense_w_gate, dense_w_up, dense_w_down, moe_w_router, moe_w_gate, moe_w_up, moe_w_down,
            final_norm_g))

    h0 = np.concatenate([meta_tokens, x[0]], axis=0)
    x_t = np.ascontiguousarray(h0.T.reshape(KT, P, L).transpose(1, 0, 2))
    gains = np.ascontiguousarray(
        np.concatenate([norm_mix_g, norm_ffn_g], axis=0).reshape(4, KT, P).transpose(2, 0, 1))
    sinks = np.ascontiguousarray(attn_sinks.reshape(-1))
    pw = np.ascontiguousarray(pool_w.reshape(2 * POOL_GROUPS, P, P).transpose(1, 0, 2))
    pscale = np.ascontiguousarray(pool_scale.reshape(2 * POOL_GROUPS, P).T)
    router = np.ascontiguousarray(moe_w_router[0].reshape(KT, P, EXPERTS).transpose(1, 0, 2))

    heads = [h for j in range(HEADS // 2) for h in (j, j + HEADS // 2)]
    qcols = np.concatenate([np.arange(HD * h, HD * h + HD) for h in heads])
    d_attn = HEADS * HD

    def col_tiles(w):
        n = w.shape[1] // (2 * P)
        return w.reshape(KT, P, n, 2, P).transpose(2, 1, 3, 0, 4).reshape(n, P, GW)

    w_mix = np.empty((2, MIX_G, P, GW), w_in.dtype)
    for l in range(2):
        w_mix[l, 0:2] = col_tiles(w_in[l][:, d_attn + 2 * P:])
        w_mix[l, 2] = w_in[l][:, d_attn:d_attn + 2 * P].reshape(KT, P, 2 * P).transpose(1, 0, 2).reshape(P, GW)
        w_mix[l, 3:5] = col_tiles(w_in[l][:, qcols])
        wo = np.concatenate([w_out[l][d_attn:], w_out[l][qcols]], axis=0)
        if l == 0:
            w_mix[l, 5:9] = col_tiles(wo)
        else:
            w_mix[l, 5:9] = wo.reshape(2, 4, P, 2, 512).transpose(3, 0, 2, 1, 4).reshape(4, P, GW)

    w_ffn = np.empty((FFN_G, P, GW), dense_w_gate.dtype)
    gate, up = col_tiles(dense_w_gate[0]), col_tiles(dense_w_up[0])
    down = dense_w_down[0].reshape(STEPS, 4, P, 2, 4, P).transpose(0, 3, 2, 4, 1, 5).reshape(STEPS, 2, P, GW)
    for n in range(STEPS):
        for s in range(2):
            g = 2 * s if n == 0 else 4 + 6 * (n - 1) + 3 * s
            w_ffn[g] = gate[2 * n + s]
            w_ffn[g + 1] = up[2 * n + s]
            w_ffn[6 * (n + 1) + 3 * s if n < STEPS - 1 else FFN_G - 2 + s] = down[n, s]

    w_moe = np.empty((EXPERTS, FFN_G, P, GW), moe_w_gate.dtype)
    gate, up = (w[0].reshape(EXPERTS, 2, 4, P, STEPS, 512).transpose(0, 4, 1, 3, 2, 5).reshape(
        EXPERTS, STEPS, 2, P, GW) for w in (moe_w_gate, moe_w_up))
    down = moe_w_down[0].reshape(EXPERTS, STEPS, 2, 2, P, D).transpose(0, 1, 2, 4, 3, 5).reshape(
        EXPERTS, STEPS, 2, P, GW)
    for n in range(STEPS):
        g = 0 if n == 0 else 4 + 6 * (n - 1)
        w_moe[:, g:g + 2] = gate[:, n]
        w_moe[:, g + 2:g + 4] = up[:, n]
        d = 8 + 6 * n if n < STEPS - 1 else FFN_G - 2
        w_moe[:, d:d + 2] = down[:, n]

    arrays = {
        "x_t": x_t, "gains": gains, "sinks": sinks, "pool_w": pw, "pool_scale": pscale,
        "final_g": np.ascontiguousarray(final_norm_g), "w_router": router, "w_mix": w_mix,
        "w_ffn": w_ffn, "w_moe": w_moe,
    }
    nc = bacc.Bacc("TRN2", target_bir_lowering=False, num_devices=1)
    args = [nc.dram_tensor(n, a.shape, mybir.dt.from_np(a.dtype), kind="ExternalInput").ap()
            for n, a in arrays.items()]
    out = nc.dram_tensor("out", (SEQ, D), F32, kind="ExternalOutput").ap()
    build(nc, *args, out)
    r = run_bass_kernel_spmd(nc, [arrays], core_ids=[0])
    return r.results[0]["out"].reshape(1, SEQ, D)
```
